# Optimizing a Trainium2 kernel written in Bass

```python
import math
import jax, jax.numpy as jnp
from jax import lax
import numpy as np

D_MODEL = 1024
BATCH = 1
SEQ = 512
DEPTH = 1

HEAD_DIM = 64
SWA_Q_HEADS = 8
SWA_KV_HEADS = 2
SWA_GROUP = SWA_Q_HEADS // SWA_KV_HEADS
WINDOW = 128
DIFF_HEADS = 4
DIFF_V_DIM = 2 * HEAD_DIM
SWA_WIDTH = SWA_Q_HEADS * HEAD_DIM
DIFF_WIDTH = DIFF_HEADS * DIFF_V_DIM
MIX_WIDTH = SWA_WIDTH + DIFF_WIDTH
QA_COLS = SWA_Q_HEADS * HEAD_DIM
KA_COLS = SWA_KV_HEADS * HEAD_DIM
VA_COLS = SWA_KV_HEADS * HEAD_DIM
QB_COLS = DIFF_HEADS * 2 * HEAD_DIM
KB_COLS = DIFF_HEADS * 2 * HEAD_DIM
VB_COLS = DIFF_HEADS * DIFF_V_DIM
IN_COLS = QA_COLS + KA_COLS + VA_COLS + QB_COLS + KB_COLS + VB_COLS
IN_SPLITS = (QA_COLS, QA_COLS + KA_COLS, QA_COLS + KA_COLS + VA_COLS,
             QA_COLS + KA_COLS + VA_COLS + QB_COLS,
             QA_COLS + KA_COLS + VA_COLS + QB_COLS + KB_COLS)
Q_BLOCK = 128
D_FF = 4 * D_MODEL
CONV_WIDTH = 3
EPS = 1e-6


def rms_norm(x, g):
    xf = x.astype(jnp.float32)
    xf = xf * lax.rsqrt(jnp.mean(xf * xf, axis=-1, keepdims=True) + EPS)
    return (xf * g.astype(jnp.float32)).astype(x.dtype)

def alibi_slopes(n):
    def pow2(m):
        start = 2.0 ** (-8.0 / m)
        return [start ** (i + 1) for i in range(m)]
    if math.log2(n).is_integer():
        s = pow2(n)
    else:
        c = 2 ** int(math.floor(math.log2(n)))
        s = pow2(c) + pow2(2 * c)[0::2][: n - c]
    return np.array(sorted(s, reverse=True), dtype=np.float32)

def swa_sink_attention(q, k, v, sinks, slopes):
    B, S = q.shape[0], q.shape[1]
    nb = S // WINDOW
    qb = q.reshape(B, nb, WINDOW, SWA_KV_HEADS, SWA_GROUP, HEAD_DIM)
    kb = k.reshape(B, nb, WINDOW, SWA_KV_HEADS, HEAD_DIM)
    vb = v.reshape(B, nb, WINDOW, SWA_KV_HEADS, HEAD_DIM)
    pad = ((0, 0), (1, 0), (0, 0), (0, 0), (0, 0))
    kk = jnp.concatenate([jnp.pad(kb, pad)[:, :-1], kb], axis=2)
    vv = jnp.concatenate([jnp.pad(vb, pad)[:, :-1], vb], axis=2)
    scores = jnp.einsum("bnqhgd,bnkhd->bnhgqk", qb, kk).astype(jnp.float32)
    scores = scores * (HEAD_DIM ** -0.5)
    qpos = jnp.arange(WINDOW)[:, None] + WINDOW
    kpos = jnp.arange(2 * WINDOW)[None, :]
    dist = qpos - kpos
    valid = (dist >= 0) & (dist < WINDOW)
    abs_k = jnp.arange(nb)[:, None, None] * WINDOW + kpos[None] - WINDOW
    valid = valid[None] & (abs_k >= 0)
    sl = slopes.reshape(SWA_KV_HEADS, SWA_GROUP)[:, :, None, None]
    scores = scores - sl * dist.astype(jnp.float32)[None, None]
    scores = jnp.where(valid[None, :, None, None], scores, -jnp.inf)
    sink = jnp.broadcast_to(
        sinks.astype(jnp.float32).reshape(1, 1, SWA_KV_HEADS, SWA_GROUP, 1, 1),
        scores.shape[:-1] + (1,))
    p = jax.nn.softmax(jnp.concatenate([scores, sink], axis=-1), axis=-1)[..., :-1]
    out = jnp.einsum("bnhgqk,bnkhd->bnqhgd", p.astype(v.dtype), vv)
    return out.reshape(B, S, SWA_Q_HEADS * HEAD_DIM)

def diff_attention(q, k, v, lam, slopes, subln_g, lambda_init):
    B, S = q.shape[0], q.shape[1]
    nb = S // Q_BLOCK
    qb = q.reshape(B, nb, Q_BLOCK, DIFF_HEADS, 2, HEAD_DIM).transpose(1, 0, 2, 3, 4, 5)
    kpos = jnp.arange(S)

    def block(args):
        q_blk, i = args
        s = jnp.einsum("bqhmd,bkhmd->bhmqk", q_blk, k).astype(jnp.float32)
        s = s * (HEAD_DIM ** -0.5)
        dist = (i * Q_BLOCK + jnp.arange(Q_BLOCK))[:, None] - kpos[None, :]
        s = s - slopes[None, :, None, None, None] * dist.astype(jnp.float32)
        s = jnp.where(dist >= 0, s, -jnp.inf)
        p = jax.nn.softmax(s, axis=-1)
        p_diff = p[:, :, 0] - lam * p[:, :, 1]
        return jnp.einsum("bhqk,bkhe->bqhe", p_diff.astype(v.dtype), v)

    out = lax.map(block, (qb, jnp.arange(nb)))
    out = out.transpose(1, 0, 2, 3, 4).reshape(B, S, DIFF_HEADS, DIFF_V_DIM)
    out = rms_norm(out, subln_g) * (1.0 - lambda_init)
    return out.reshape(B, S, DIFF_HEADS * DIFF_V_DIM)

def conv_ffn(h, w_up, conv_w, conv_b, w_down):
    u = jnp.einsum("bsd,df->bsf", h, w_up)
    up = jnp.pad(u, ((0, 0), (CONV_WIDTH - 1, 0), (0, 0)))
    S = u.shape[1]
    c = (conv_w[0] * up[:, 0:S] + conv_w[1] * up[:, 1:S + 1]
         + conv_w[2] * up[:, 2:S + 2] + conv_b)
    g, val = jnp.split(c, 2, axis=-1)
    return jnp.einsum("bsf,fd->bsd", jax.nn.gelu(g, approximate=True) * val, w_down)

def first_inputs(seed: int = 0) -> dict:
    key = jax.random.key(seed)
    ks = jax.random.split(key, 18)
    f32 = jnp.float32

    def nrm(k, shape, scale):
        return jax.random.normal(k, shape, f32) * scale

    def gain(k, shape):
        return 1.0 + 0.05 * jax.random.normal(k, shape, f32)

    return {
        "x": nrm(ks[0], (BATCH, SEQ, D_MODEL), 1.0),
        "attn_pre_g": gain(ks[1], (DEPTH, D_MODEL)),
        "w_in": nrm(ks[2], (DEPTH, D_MODEL, IN_COLS), D_MODEL ** -0.5),
        "swa_sinks": nrm(ks[3], (DEPTH, SWA_Q_HEADS), 0.5),
        "swa_out_g": gain(ks[4], (DEPTH, SWA_WIDTH)),
        "diff_lq1": nrm(ks[5], (DEPTH, HEAD_DIM), 0.1),
        "diff_lk1": nrm(ks[6], (DEPTH, HEAD_DIM), 0.1),
        "diff_lq2": nrm(ks[7], (DEPTH, HEAD_DIM), 0.1),
        "diff_lk2": nrm(ks[8], (DEPTH, HEAD_DIM), 0.1),
        "diff_subln_g": gain(ks[9], (DEPTH, DIFF_V_DIM)),
        "w_out": nrm(ks[10], (DEPTH, MIX_WIDTH, D_MODEL), MIX_WIDTH ** -0.5),
        "attn_post_g": gain(ks[11], (DEPTH, D_MODEL)),
        "ffn_pre_g": gain(ks[12], (DEPTH, D_MODEL)),
        "w_up": nrm(ks[13], (DEPTH, D_MODEL, 2 * D_FF), D_MODEL ** -0.5),
        "conv_w": nrm(ks[14], (DEPTH, CONV_WIDTH, 2 * D_FF), CONV_WIDTH ** -0.5),
        "conv_b": nrm(ks[15], (DEPTH, 2 * D_FF), 0.02),
        "w_down": nrm(ks[16], (DEPTH, D_FF, D_MODEL), D_FF ** -0.5),
        "ffn_post_g": gain(ks[17], (DEPTH, D_MODEL)),
    }

def first_block(x, attn_pre_g, w_in, swa_sinks, swa_out_g, diff_lq1, diff_lk1, diff_lq2,
              diff_lk2, diff_subln_g, w_out, attn_post_g, ffn_pre_g, w_up, conv_w, conv_b,
              w_down, ffn_post_g):
    B, S = x.shape[0], x.shape[1]
    slopes = jnp.asarray(alibi_slopes(SWA_Q_HEADS + DIFF_HEADS))
    swa_slopes = slopes[:SWA_Q_HEADS]
    diff_slopes = slopes[SWA_Q_HEADS:]
    for layer in range(DEPTH):
        lambda_init = 0.8 - 0.6 * math.exp(-0.3 * layer)
        h = rms_norm(x, attn_pre_g[layer])
        proj = jnp.einsum("bsd,de->bse", h, w_in[layer])
        q_a, k_a, v_a, q_b, k_b, v_b = jnp.split(proj, IN_SPLITS, axis=-1)
        y_a = swa_sink_attention(
            q_a.reshape(B, S, SWA_Q_HEADS, HEAD_DIM),
            k_a.reshape(B, S, SWA_KV_HEADS, HEAD_DIM),
            v_a.reshape(B, S, SWA_KV_HEADS, HEAD_DIM),
            swa_sinks[layer], swa_slopes)
        y_a = rms_norm(y_a, swa_out_g[layer])
        lam = (jnp.exp(jnp.sum(diff_lq1[layer].astype(jnp.float32) * diff_lk1[layer].astype(jnp.float32)))
               - jnp.exp(jnp.sum(diff_lq2[layer].astype(jnp.float32) * diff_lk2[layer].astype(jnp.float32)))
               + lambda_init)
        y_b = diff_attention(
            q_b.reshape(B, S, DIFF_HEADS, 2, HEAD_DIM),
            k_b.reshape(B, S, DIFF_HEADS, 2, HEAD_DIM),
            v_b.reshape(B, S, DIFF_HEADS, DIFF_V_DIM),
            lam, diff_slopes, diff_subln_g[layer], lambda_init)
        mix = jnp.concatenate([y_a, y_b], axis=-1)
        x = x + rms_norm(jnp.einsum("bse,ed->bsd", mix, w_out[layer]), attn_post_g[layer])
        h2 = rms_norm(x, ffn_pre_g[layer])
        f = conv_ffn(h2, w_up[layer], conv_w[layer], conv_b[layer], w_down[layer])
        x = x + rms_norm(f, ffn_post_g[layer])
    return x


N_HEADS = 16
ATTN_WIDTH = N_HEADS * HEAD_DIM
KV_LATENT = 128
IDX_HEADS = 8
IDX_DIM = 64
TOPK_MAX = 256
RNN_WIDTH = 1024
RNN_BLOCKS = 16
RNN_BLOCK_DIM = RNN_WIDTH // RNN_BLOCKS
CONV_WIDTH_2 = 4
LRU_C = 8.0
NORM_EPS = 1e-6
SPLITS = (ATTN_WIDTH, KV_LATENT, IDX_HEADS * IDX_DIM, IDX_DIM, IDX_HEADS, ATTN_WIDTH, RNN_WIDTH, RNN_WIDTH, 2 * D_MODEL)
IN_WIDTH = sum(SPLITS)


def rms_norm_2(x, g):
    xf = x.astype(jnp.float32)
    y = xf * lax.rsqrt(jnp.mean(xf * xf, axis=-1, keepdims=True) + NORM_EPS)
    return (y * g.astype(jnp.float32)).astype(x.dtype)

def layer_norm(x, g, b):
    xf = x.astype(jnp.float32)
    mu = jnp.mean(xf, axis=-1, keepdims=True)
    xc = xf - mu
    y = xc * lax.rsqrt(jnp.mean(xc * xc, axis=-1, keepdims=True) + NORM_EPS)
    return (y * g.astype(jnp.float32) + b.astype(jnp.float32)).astype(x.dtype)

def alibi_slopes_2(n):
    return jnp.exp2(-8.0 * jnp.arange(1, n + 1, dtype=jnp.float32) / n)

def split_cols(z):
    offsets = np.cumsum(np.array(SPLITS))[:-1].tolist()
    return jnp.split(z, offsets, axis=-1)

def sparse_mla_attention(q, c_kv, q_idx, k_idx, w_idx, w_uk, w_uv):
    B, S = q.shape[0], q.shape[1]
    topk = min(TOPK_MAX, S // 4)
    tb = min(Q_BLOCK, S)
    nblk = S // tb
    f32 = jnp.float32
    q_lat = jnp.einsum('bshd,hcd->bshc', q, w_uk) * (HEAD_DIM ** -0.5)
    slopes = alibi_slopes_2(N_HEADS)
    key_pos = jnp.arange(S, dtype=jnp.int32)
    k_idx_f = k_idx.astype(f32)

    def to_blocks(a):
        return a.reshape((B, nblk, tb) + a.shape[2:]).swapaxes(0, 1)

    def block_fn(args):
        ql, qi, wi, t0 = args
        t = t0 + jnp.arange(tb, dtype=jnp.int32)
        s_idx = jax.nn.relu(jnp.einsum('btjd,bsd->btjs', qi.astype(f32), k_idx_f))
        s_idx = jnp.einsum('btjs,btj->bts', s_idx, wi.astype(f32))
        causal = key_pos[None, :] <= t[:, None]
        s_idx = jnp.where(causal[None], s_idx, -jnp.inf)
        _, idx = lax.top_k(s_idx, topk)
        c_sel = jax.vmap(lambda c, i: c[i])(c_kv, idx).astype(f32)
        logits = jnp.einsum('bthc,btkc->bthk', ql.astype(f32), c_sel)
        dist = (t[None, :, None] - idx).astype(f32)
        logits = logits - slopes[None, None, :, None] * dist[:, :, None, :]
        valid = idx <= t[None, :, None]
        logits = jnp.where(valid[:, :, None, :], logits, -jnp.inf)
        p = jax.nn.softmax(logits, axis=-1)
        o = jnp.einsum('bthk,btkc->bthc', p, c_sel)
        return o.astype(ql.dtype)

    t0s = jnp.arange(nblk, dtype=jnp.int32) * tb
    o_lat = lax.map(block_fn, (to_blocks(q_lat), to_blocks(q_idx), to_blocks(w_idx), t0s))
    o_lat = o_lat.swapaxes(0, 1).reshape(B, S, N_HEADS, KV_LATENT)
    return jnp.einsum('bshc,hcd->bshd', o_lat, w_uv)

def causal_depthwise_conv(x, w, b):
    S = x.shape[1]
    xp = jnp.pad(x, ((0, 0), (CONV_WIDTH_2 - 1, 0), (0, 0)))
    out = b
    for k in range(CONV_WIDTH_2):
        out = out + xp[:, k:k + S] * w[k]
    return out

def rg_lru(x, w_a, b_a, w_x, b_x, lam):
    B, S, C = x.shape
    f32 = jnp.float32
    xb = x.reshape(B, S, RNN_BLOCKS, RNN_BLOCK_DIM)
    r = jax.nn.sigmoid(jnp.einsum('bsgi,gij->bsgj', xb, w_a).reshape(B, S, C) + b_a).astype(f32)
    i = jax.nn.sigmoid(jnp.einsum('bsgi,gij->bsgj', xb, w_x).reshape(B, S, C) + b_x).astype(f32)
    log_a = -LRU_C * r * jax.nn.softplus(-lam.astype(f32))
    a = jnp.exp(log_a)
    b_in = jnp.sqrt(-jnp.expm1(2.0 * log_a)) * (i * x.astype(f32))

    def combine(left, right):
        a1, b1 = left
        a2, b2 = right
        return a1 * a2, a2 * b1 + b2

    _, h = lax.associative_scan(combine, (a, b_in), axis=1)
    return h.astype(x.dtype)

def hybrid_layer(x, norm_g, w_in, b_merge, kv_norm_g, w_uk, w_uv, idx_ln_g, idx_ln_b,
                 w_attn_proj, conv_w, conv_b, w_rg_a, b_rg_a, w_rg_x, b_rg_x, lru_lambda,
                 w_rnn_proj, w_out):
    B, S, _ = x.shape
    xn = rms_norm_2(x, norm_g)
    z = xn @ w_in
    q, c_kv, q_idx, k_idx, w_idx, g_attn, x_rnn, g_rnn, merge = split_cols(z)
    q = q.reshape(B, S, N_HEADS, HEAD_DIM)
    c_kv = rms_norm_2(c_kv, kv_norm_g)
    q_idx = q_idx.reshape(B, S, IDX_HEADS, IDX_DIM) * (IDX_DIM ** -0.5)
    k_idx = layer_norm(k_idx, idx_ln_g, idx_ln_b)
    w_idx = w_idx * (IDX_HEADS ** -0.5)
    o = sparse_mla_attention(q, c_kv, q_idx, k_idx, w_idx, w_uk, w_uv).reshape(B, S, ATTN_WIDTH)
    y_attn = (o * jax.nn.silu(g_attn)) @ w_attn_proj
    h = rg_lru(causal_depthwise_conv(x_rnn, conv_w, conv_b), w_rg_a, b_rg_a, w_rg_x, b_rg_x, lru_lambda)
    y_rnn = (h * jax.nn.silu(g_rnn)) @ w_rnn_proj
    gates = jax.nn.sigmoid(merge + b_merge)
    g_a, g_r = gates[..., :D_MODEL], gates[..., D_MODEL:]
    mixed = g_a * y_attn + g_r * y_rnn
    return x + mixed @ w_out

def second_inputs(seed: int = 0) -> dict:
    key = jax.random.key(seed)
    ks = jax.random.split(key, 24)
    f32 = jnp.float32

    def nrm(k, shape, scale):
        return jax.random.normal(k, shape, f32) * scale

    u = jax.random.uniform(ks[20], (DEPTH, RNN_WIDTH), f32, minval=0.9, maxval=0.999)
    return {
        'x': jax.random.normal(ks[0], (BATCH, SEQ, D_MODEL), f32),
        'norm_gain': 1.0 + nrm(ks[1], (DEPTH, D_MODEL), 0.01),
        'w_in': nrm(ks[2], (DEPTH, D_MODEL, IN_WIDTH), D_MODEL ** -0.5),
        'b_merge': nrm(ks[3], (DEPTH, 2 * D_MODEL), 0.01),
        'kv_norm_gain': 1.0 + nrm(ks[4], (DEPTH, KV_LATENT), 0.01),
        'w_uk': nrm(ks[5], (DEPTH, N_HEADS, KV_LATENT, HEAD_DIM), KV_LATENT ** -0.5),
        'w_uv': nrm(ks[6], (DEPTH, N_HEADS, KV_LATENT, HEAD_DIM), KV_LATENT ** -0.5),
        'idx_ln_gain': 1.0 + nrm(ks[7], (DEPTH, IDX_DIM), 0.01),
        'idx_ln_bias': nrm(ks[8], (DEPTH, IDX_DIM), 0.01),
        'w_attn_proj': nrm(ks[9], (DEPTH, ATTN_WIDTH, D_MODEL), ATTN_WIDTH ** -0.5),
        'conv_w': nrm(ks[10], (DEPTH, CONV_WIDTH_2, RNN_WIDTH), CONV_WIDTH_2 ** -0.5),
        'conv_b': nrm(ks[11], (DEPTH, RNN_WIDTH), 0.01),
        'w_rg_a': nrm(ks[12], (DEPTH, RNN_BLOCKS, RNN_BLOCK_DIM, RNN_BLOCK_DIM), RNN_BLOCK_DIM ** -0.5),
        'b_rg_a': nrm(ks[13], (DEPTH, RNN_WIDTH), 0.01),
        'w_rg_x': nrm(ks[14], (DEPTH, RNN_BLOCKS, RNN_BLOCK_DIM, RNN_BLOCK_DIM), RNN_BLOCK_DIM ** -0.5),
        'b_rg_x': nrm(ks[15], (DEPTH, RNN_WIDTH), 0.01),
        'lru_lambda': jnp.log(u) - jnp.log1p(-u),
        'w_rnn_proj': nrm(ks[16], (DEPTH, RNN_WIDTH, D_MODEL), RNN_WIDTH ** -0.5),
        'w_out': nrm(ks[17], (DEPTH, D_MODEL, D_MODEL), D_MODEL ** -0.5),
        'final_norm_gain': 1.0 + nrm(ks[18], (D_MODEL,), 0.01),
    }

def second_block(x, norm_gain, w_in, b_merge, kv_norm_gain, w_uk, w_uv, idx_ln_gain, idx_ln_bias,
              w_attn_proj, conv_w, conv_b, w_rg_a, b_rg_a, w_rg_x, b_rg_x, lru_lambda,
              w_rnn_proj, w_out, final_norm_gain):
    for l in range(DEPTH):
        x = hybrid_layer(x, norm_gain[l], w_in[l], b_merge[l], kv_norm_gain[l], w_uk[l], w_uv[l],
                         idx_ln_gain[l], idx_ln_bias[l], w_attn_proj[l], conv_w[l], conv_b[l],
                         w_rg_a[l], b_rg_a[l], w_rg_x[l], b_rg_x[l], lru_lambda[l],
                         w_rnn_proj[l], w_out[l])
    return rms_norm_2(x, final_norm_gain)


def setup_inputs(seed=0):
    out = dict(first_inputs(seed))
    for name, value in second_inputs(seed + 1).items():
        if name != "x":
            out[name + "_2"] = value
    return out


def reference(
    x, attn_pre_g, w_in, swa_sinks, swa_out_g, diff_lq1, diff_lk1, diff_lq2, diff_lk2,
    diff_subln_g, w_out, attn_post_g, ffn_pre_g, w_up, conv_w, conv_b, w_down, ffn_post_g,
    norm_gain_2, w_in_2, b_merge_2, kv_norm_gain_2, w_uk_2, w_uv_2, idx_ln_gain_2,
    idx_ln_bias_2, w_attn_proj_2, conv_w_2, conv_b_2, w_rg_a_2, b_rg_a_2, w_rg_x_2, b_rg_x_2,
    lru_lambda_2, w_rnn_proj_2, w_out_2, final_norm_gain_2,
):
    x = first_block(
        x, attn_pre_g, w_in, swa_sinks, swa_out_g, diff_lq1, diff_lk1, diff_lq2, diff_lk2,
        diff_subln_g, w_out, attn_post_g, ffn_pre_g, w_up, conv_w, conv_b, w_down, ffn_post_g,
    )
    return second_block(
        x, norm_gain_2, w_in_2, b_merge_2, kv_norm_gain_2, w_uk_2, w_uv_2, idx_ln_gain_2,
        idx_ln_bias_2, w_attn_proj_2, conv_w_2, conv_b_2, w_rg_a_2, b_rg_a_2, w_rg_x_2,
        b_rg_x_2, lru_lambda_2, w_rnn_proj_2, w_out_2, final_norm_gain_2,
    )


_drawn_inputs = setup_inputs


def setup_inputs(seed=0):
    import zlib

    import numpy as np

    out = dict(_drawn_inputs(seed))
    spreads = {}
    factors = {'diff_lq1': 8.0,
     'conv_b': 2.714,
     'norm_gain_2': 6.655,
     'b_merge_2': 37.799,
     'kv_norm_gain_2': 8.0,
     'idx_ln_gain_2': 8.0,
     'idx_ln_bias_2': 8.0,
     'conv_b_2': 24.26,
     'b_rg_a_2': 64.0,
     'b_rg_x_2': 64.0,
     'final_norm_gain_2': 31.111}
    for name, (base, spread) in spreads.items():
        noise = np.random.default_rng([zlib.crc32(name.encode()), seed]).standard_normal(out[name].shape)
        drawn = base * np.exp(spread * noise) if base else spread * noise
        out[name] = __import__('jax').numpy.asarray(drawn.astype(out[name].dtype))
    for name, factor in factors.items():
        out[name] = (out[name] * factor).astype(out[name].dtype)
    return out
```

```python
from contextlib import ExitStack

import concourse.bass as bass
from concourse import mybir

F32 = mybir.dt.float32
F32R = mybir.dt.float32r
I32 = mybir.dt.int32
ALU = mybir.AluOpType
ACT = mybir.ActivationFunctionType
AX_X = mybir.AxisListType.X

P = 128
S = 512
D = 1024
DC = D // P
NB = S // P
HD = 64
SWA_PAIRS = 4
DIFF_HEADS = 4
MLA_HEADS = 16
IDX_HEADS = 8
TOPK = 128
EPS = 1e-6
SCALE = HD ** -0.5
FAR = 1e30
LAMBDA_INIT = 0.2
SLOPES_1 = sorted([2.0 ** -(i + 1) for i in range(8)] + [2.0 ** -(0.5 * (2 * i + 1)) for i in range(4)], reverse=True)
SLOPES_2 = [2.0 ** (-8.0 * (i + 1) / MLA_HEADS) for i in range(MLA_HEADS)]

STAGES = [("in1", 9), ("out1", 4), ("up0", 8), ("up1", 8), ("dn0", 4), ("up2", 8), ("dn1", 4),
          ("up3", 8), ("dn2", 4), ("dn3", 4), ("in2a", 7), ("in2b", 8), ("gattn", 4), ("mr", 8),
          ("ma", 8), ("out2", 4)]
FIRST, NPANELS = {}, 0
for _name, _n in STAGES:
    FIRST[_name] = (NPANELS, _n)
    NPANELS += _n

COLS, NCOLS = {}, 0
for _name, _n in [("attn_pre", 8), ("swa_out", 4), ("subln", 1), ("attn_post", 8), ("ffn_pre", 8),
                  ("cw0", 64), ("cw1", 64), ("cw2", 64), ("cb", 64), ("ffn_post", 8), ("norm2", 8),
                  ("b_merge", 16), ("kv_norm", 1), ("ln_g", 1), ("ln_b", 1), ("rw", 32), ("rb", 8),
                  ("b_rg_a", 8), ("b_rg_x", 8), ("lru", 8), ("final", 8), ("sinks", 8)]:
    COLS[_name] = NCOLS
    NCOLS += _n


class Count:

    def __init__(self, sem):
        self.sem, self.n = sem, 0

    def __call__(self, ins):
        ins.then_inc(self.sem, 1)
        self.n = self.n + 1


def build(nc, panels, xT, cols_in, lamv_in, wi_in, rgw_in, uk_in, uv_in, outT):
    spill = nc.dram_tensor("x2_spill", (P, DC, S), F32, kind="Internal").ap()
    with ExitStack() as ctx:
        KB = 1024
        ARENA0 = 16512 + 32
        arena_used = []

        def at(name, shape, kb, dt=F32):
            size = 4
            for n in shape[1:]:
                size *= n
            assert kb * KB + size <= 207.5 * KB, (name, kb, size)
            arena_used.append((name, kb, size))
            return nc.alloc_sbuf_tensor_at(name, shape, dt, offset=ARENA0 + int(kb * KB))

        def sem(name):
            return ctx.enter_context(nc.semaphore(name))

        XT = at("XT", [P, DC, S], 0)
        XH = at("XH", [P, DC, S], 16, F32R)
        XL = at("XL", [P, DC, S], 32, F32R)
        WH = at("WH", [P, 2, DC, 256], 48, F32R)
        WL = at("WL", [P, 2, DC, 256], 64, F32R)
        RAW = at("RAW", [P, 2, DC * 256], 80)
        PROJ = at("PROJ", [P, 18, S], 96)
        VA = at("VA", [P, NB, P], 132)
        VB = at("VB", [P, DIFF_HEADS, NB, P], 134)
        MIX = at("MIX", [P, DC, S], 142)
        SQ1 = at("SQ1", [P, DC, S], 142)
        DS4 = at("DS4", [P, NB, 256], 158)
        PSW = at("PSW", [P, 2, NB, 256], 162)
        PD = at("PD", [P, 2, 2, S], 162)
        PTW = at("PTW", [P, 2, NB, 256], 170)
        PTD = at("PTD", [P, 2, NB, S], 170)
        MSQ = at("MSQ", [P, DC, S], 96)
        DG1 = at("DG1", [P, 20, P], 112)
        RM = at("RM", [P, 5, S], 122)
        Y1 = at("Y1", [P, DC, S], 142)
        SQY = at("SQY", [P, DC, S], 96)
        AH = at("AH", [P, 2, DC, S], 96, F32R)
        AL = at("AL", [P, 2, DC, S], 128, F32R)
        FA = at("FA", [P, DC, S], 160)
        U = at("U", [P, 2, 2, S], 176)
        C = at("C", [P, 2, 2, S], 184)
        Z = at("Z", [P, 2, S], 192)
        SQF = at("SQF", [P, DC, S], 96)
        QT = at("QT", [P, 8, S], 96)
        CKV = at("CKV", [P, 2, S], 112)
        CKT = at("CKT", [P, NB, P], 116)
        XR = at("XR", [P, 8, S], 118)
        GR = at("GR", [P, 8, S], 134)
        RH = at("RH", [P, 8, S], 118, F32R)
        RL = at("RL", [P, 8, S], 134, F32R)
        GA = at("GA", [P, 8, S], 150)
        QI = at("QI", [P, 4, S], 150)
        CSQ = at("CSQ", [P, 2, S], 158)
        KC = at("KC", [P, S], 162)
        WIH = at("WIH", [P, DC, 8], 164, F32R)
        WIL = at("WIL", [P, DC, 8], 164.25, F32R)
        WIR = at("WIR", [P, DC, 8], 164.5)
        MD = at("MD", [P, 1152], 166)
        IA = at("IA", [P, 1152], 171)
        IW = at("IW", [P, 1152], 175.5)
        RLU = at("RLU", [P, 2, S], 181)
        RGT = at("RGT", [P, 5, 2, S], 171)
        M2 = at("M2", [P, 8, S], 171)
        SG = at("SG", [P, 2, S], 191)
        RGW = at("RGW", [P, 2, 8, P], 0)
        UK = at("UK", [P, 8, P], 8)
        UV = at("UV", [P, MLA_HEADS, HD], 12)
        PM = at("PM", [P, 2, 2, S], 118)
        PTM = at("PTM", [P, 2, NB, S], 126)
        OL = at("OL", [P, 2, S], 142)
        SGA = at("SGA", [P, 2, S], 146)
        QL = at("QL", [P, 2, 2, S], 187)
        SQ2 = at("SQ2", [P, DC, S], 118)
        COL = at("COL", [P, NCOLS], 196)
        EC = at("EC", [P, S], 198)
        IDN = at("IDN", [P, P], 200)
        ONE = at("ONE", [P, P], 200.5)
        R = at("R", [P, S], 201)
        DG = at("DG", [P, NB, P], 203)
        LV = at("LV", [P, 4, HD], 205)
        SM = at("SM", [P, 192], 206)

        PG = ctx.enter_context(nc.psum_tensor("PG", [P, 4, S], F32))
        PX = ctx.enter_context(nc.psum_tensor("PX", [P, 4, S], F32))

        def col(name, k, n=1):
            return COL[:, COLS[name] + k:COLS[name] + k + n] if isinstance(k, int) else \
                COL[:, bass.ds(k + COLS[name], n)]

        SMN = [0]

        def small(n):
            SMN[0] += n
            assert SMN[0] <= 192
            return SM[:, SMN[0] - n:SMN[0]]

        EPST = small(1)
        LAM = small(1)
        LDOT = small(2)
        NEG_SP8 = small(8)
        POS_SP8 = small(8)
        SP = small(24)
        SINK8 = small(8)
        STD = small(20)
        RT = small(20)
        MX = small(4)
        NM = small(8)
        DEN = small(8)
        ES = small(4)
        M8 = small(24)
        WX = small(32)
        RTL = small(1)
        WORD = small(1)

        loaded_x = sem("loaded_x")
        loaded_c = sem("loaded_c")
        loaded_b2 = sem("loaded_b2")
        loaded_wi = sem("loaded_wi")
        spilled = sem("spilled")
        reloaded = sem("reloaded")
        stored = sem("stored")
        raw_in = [sem("raw_in0"), sem("raw_in1")]
        w_hi = sem("w_hi")
        w_lo = sem("w_lo")
        panel_done = sem("panel_done")
        evac = sem("evac")
        consts = sem("consts")
        act_step = sem("act_step")
        dve_step = sem("dve_step")
        pe_sig = {}

        def once(name):
            if name not in pe_sig:
                pe_sig[name] = sem(name)
            return pe_sig[name]

        block = ctx.enter_context(nc.Block())

        def pairs(eng, name, step, upto=None):
            p0, n = FIRST[name]
            if n >= 4:
                with eng.Fori(0, n // 2) as i:
                    step(i * 2 + p0, i * 2, 0, i)
                    step(i * 2 + (p0 + 1), i * 2 + 1, 1, i)
            if n % 2:
                step(p0 + n - 1, n - 1, 0, n // 2)

        @block.sync
        def _(sp):
            sp.dma_start(XT[:], xT.rearrange("(c p) n -> p c n", p=P)).then_inc(loaded_x, 16)
            sp.dma_start(COL[:], cols_in).then_inc(loaded_c, 16)
            sp.dma_start(LV[:], lamv_in).then_inc(loaded_c, 16)
            for s in range(2):
                sp.dma_start(RAW[:, s, :], panels[s]).then_inc(raw_in[s], 16)
            with sp.Fori(1, NPANELS // 2) as i:
                for s in range(2):
                    sp.wait_ge(w_lo, i * 2 + (s - 1))
                    sp.dma_start(RAW[:, s, :], panels[bass.ds(i * 2 + s, 1), :, :].rearrange("a p n -> p (a n)"))\
                        .then_inc(raw_in[s], 16)
            sp.wait_ge(once("out_ready"), 8)
            sp.dma_start(outT.rearrange("(c p) n -> p c n", p=P), SQ2[:]).then_inc(stored, 16)
            sp.wait_ge(stored, 16)

        @block.gpsimd
        def _(pool):
            pool.memset(ONE[:], 1.0).then_inc(consts, 1)
            pool.memset(IDN[:], 0.0).then_inc(consts, 1)
            pool.wait_ge(consts, 2)
            pool.affine_select(out=IDN[:], in_=IDN[:], compare_op=ALU.not_equal, fill=1.0, base=0,
                               pattern=[[-1, P]], channel_multiplier=1).then_inc(consts, 1)
            pool.iota(EC[:].bitcast(I32), pattern=[[-1, S]], base=(NB - 1) * P, channel_multiplier=1).then_inc(consts, 1)
            pool.wait_ge(consts, 4)
            pool.tensor_copy(DG[:].rearrange("p a b -> p (a b)"), EC[:].bitcast(I32)).then_inc(consts, 1)
            pool.wait_ge(consts, 5)
            pool.affine_select(out=EC[:], in_=DG[:].rearrange("p a b -> p (a b)"), compare_op=ALU.is_ge, fill=FAR,
                               base=(NB - 1) * P, pattern=[[-1, S]], channel_multiplier=1).then_inc(consts, 1)
            pool.wait_ge(consts, 6)
            for b in range(NB):
                pool.affine_select(out=DS4[:, b, :], in_=EC[:, 2 * P:], compare_op=ALU.is_ge, fill=FAR,
                                   base=-1, pattern=[[1, 256]], channel_multiplier=-1).then_inc(consts, 1)
            pool.wait_ge(consts, 10)
            pool.memset(DS4[:, 0, 0:P], FAR).then_inc(consts, 1)

            def lo(s, value):
                pool.wait_ge(w_hi, value)
                pool.tensor_tensor(WL[:, s].rearrange("p a b -> p (a b)"), RAW[:, s, :],
                                   WH[:, s].rearrange("p a b -> p (a b)").bitcast(F32), ALU.subtract)\
                    .then_inc(w_lo, 1)

            with pool.Fori(0, NPANELS // 2) as i:
                for s in range(2):
                    lo(s, i * 2 + (s + 1))

        @block.tensor
        def _(pe):
            def gemm(name, first_wait, xh=None, xl=None):
                xh = XH if xh is None else xh
                xl = XL if xl is None else xl
                p0, _ = FIRST[name]

                def step(p, k, b, i):
                    s = (p0 + b) % 2
                    pe.wait_ge(w_lo, p + 1)
                    if not (isinstance(p, int) and p < 2) and not (name == "in1" and b < 2 and not isinstance(p, int)):
                        pe.wait_ge(evac, p - 1)
                    for m in range(2):
                        ms = slice(m * P, (m + 1) * P)
                        for c in range(DC):
                            o = PG[:, 2 * s + m, :]
                            pe.matmul(o, WH[:, s, c, ms], xh[:, c, :], start=(c == 0), stop=False)
                            pe.matmul(o, WH[:, s, c, ms], xl[:, c, :], start=False, stop=False)
                            mm = pe.matmul(o, WL[:, s, c, ms], xh[:, c, :], start=False, stop=(c == DC - 1))
                    mm.then_inc(panel_done, 1)

                if name == "in1":
                    step(0, 0, 0, 0)
                    step(1, 1, 1, 0)
                    with pe.Fori(1, 4) as i:
                        for b in range(2):
                            pi = i * 2 + b
                            s = b
                            pe.wait_ge(w_lo, pi + 1)
                            pe.wait_ge(evac, pi - 1)
                            for m in range(2):
                                ms = slice(m * P, (m + 1) * P)
                                for c in range(DC):
                                    o = PG[:, 2 * s + m, :]
                                    pe.matmul(o, WH[:, s, c, ms], xh[:, c, :], start=(c == 0), stop=False)
                                    pe.matmul(o, WH[:, s, c, ms], xl[:, c, :], start=False, stop=False)
                                    mm = pe.matmul(o, WL[:, s, c, ms], xh[:, c, :], start=False, stop=(c == DC - 1))
                            mm.then_inc(panel_done, 1)
                    step(8, 8, 0, 4)
                else:
                    pairs(pe, name, step)

            def sums(name, src, nchunks):
                for c in range(nchunks):
                    pe.wait_ge(once(name + "_sq"), c + 1)
                    for b in range(NB):
                        mm = pe.matmul(PX[:, 0, b:b + 1], src[:, c, b * P:(b + 1) * P], ONE[:, 0:1],
                                       start=(c == 0 and b == 0), stop=(c == nchunks - 1), skip_group_check=True)
                mm.then_inc(once(name + "_sum"), 1)

            def spread(name, dg, k, bank, done):
                for b in range(NB):
                    mm = pe.matmul(PX[:, bank, b * P:(b + 1) * P], ONE[:], dg[:, k * NB + b, :], start=True, stop=True)
                mm.then_inc(once(done), 1)

            def norm(name, src, nchunks=DC):
                sums(name, src, nchunks)
                pe.wait_ge(once(name + "_diag"), NB)
                spread(name, DG, 0, 1, name + "_bc")

            pe.wait_ge(consts, 11)
            norm("n1", SQ1)
            pe.wait_ge(once("x1_split"), 8)
            gemm("in1", None)

            pe.wait_ge(evac, FIRST["out1"][0])
            for t, tile in enumerate([5, 14, 15, 16, 17]):
                if t >= 2:
                    pe.wait_ge(once("v_copied"), t - 1)
                for b in range(NB):
                    mm = pe.transpose(PX[:, t % 2, b * P:(b + 1) * P], PROJ[:, tile, b * P:(b + 1) * P], IDN[:])
                mm.then_inc(once("v_turned"), 1)

            def swa_scores(h):
                g, j = divmod(h, SWA_PAIRS)
                rows = slice(g * HD, (g + 1) * HD)
                if h >= 2:
                    pe.wait_ge(once("swa_logits"), h - 1)
                s = h % 2
                for qb in range(NB):
                    q = PROJ[rows, j, qb * P:(qb + 1) * P]
                    o = PG[:, 2 * s + qb // 2, (qb % 2) * 256:(qb % 2) * 256 + 256]
                    if qb == 0:
                        pe.matmul(o[:, 0:P], q, PROJ[rows, 4, 0:P], start=True, stop=True)
                        mm = pe.matmul(o[:, P:], q, PROJ[rows, 4, 0:P], start=True, stop=True)
                    else:
                        mm = pe.matmul(o, q, PROJ[rows, 4, (qb - 1) * P:(qb + 1) * P], start=True, stop=True)
                mm.then_inc(once("swa_s"), 1)

            def swa_turn(h):
                pe.wait_ge(once("swa_probs"), h + 1)
                if h >= 1:
                    pe.wait_ge(once("swa_copied"), h)
                else:
                    pe.wait_ge(once("v_copied"), 5)
                for kb in range(NB):
                    o = PX[:, kb // 2, (kb % 2) * 256:(kb % 2) * 256 + 256]
                    mm = pe.transpose(o[:, 0:P], PSW[:, h % 2, kb, P:256], IDN[:])
                    if kb < NB - 1:
                        mm = pe.transpose(o[:, P:256], PSW[:, h % 2, kb + 1, 0:P], IDN[:])
                mm.then_inc(once("swa_turned"), 1)

            def swa_pv(h):
                g, j = divmod(h, SWA_PAIRS)
                rows = slice(g * HD, (g + 1) * HD)
                pe.wait_ge(once("swa_copied"), h + 1)
                if h >= 2:
                    pe.wait_ge(once("swa_out"), h - 1)
                for kb in range(NB):
                    n = 256 if kb < NB - 1 else P
                    mm = pe.matmul(PX[rows, 2 + h % 2, kb * P:kb * P + n], VA[:, kb, rows], PTW[:, h % 2, kb, 0:n],
                                   start=(kb == 0), stop=(kb == NB - 1), skip_group_check=True)
                mm.then_inc(once("swa_pv"), 1)

            swa_scores(0)
            swa_scores(1)
            for h in range(8):
                swa_turn(h)
                if h + 2 < 8:
                    swa_scores(h + 2)
                swa_pv(h)

            def unit_turn(pre, src, u, qb, maps):
                pe.wait_ge(once(pre + "_probs"), u + 1)
                if u >= 1:
                    pe.wait_ge(once(pre + "_copied"), u)
                for m in range(maps):
                    for kb in range(qb + 1):
                        mm = pe.transpose(PX[:, m, kb * P:(kb + 1) * P], src[:, u % 2, m, kb * P:(kb + 1) * P], IDN[:])
                mm.then_inc(once(pre + "_turned"), 1)

            def diff_scores(u):
                h, qb = divmod(u, NB)
                if u >= 2:
                    pe.wait_ge(once("diff_logits"), u - 1)
                n = (qb + 1) * P
                for m in range(2):
                    rows = slice(m * HD, (m + 1) * HD)
                    mm = pe.matmul(PG[:, 2 * (u % 2) + m, 0:n], PROJ[rows, 6 + h, qb * P:(qb + 1) * P],
                                   PROJ[rows, 10 + h, 0:n], start=True, stop=True)
                mm.then_inc(once("diff_s"), 1)

            pe.wait_ge(once("swa_logits"), 8)
            diff_scores(0)
            diff_scores(1)
            for u in range(16):
                h, qb = divmod(u, NB)
                if u == 0:
                    pe.wait_ge(once("swa_out"), 8)
                if u + 2 < 16:
                    diff_scores(u + 2)
                unit_turn("diff", PD, u, qb, 1)
                if qb == NB - 1:
                    pe.wait_ge(once("diff_copied"), u + 1)
                    if h >= 1:
                        pe.wait_ge(once("diff_out"), h)
                    for kb in range(NB):
                        mm = pe.matmul(PX[:, 2, kb * P:], VB[:, h, kb, :], PTD[:, h % 2, kb, kb * P:],
                                       start=(kb == 0), stop=(kb == NB - 1), skip_group_check=True)
                    mm.then_inc(once("diff_pv"), 1)

            pe.wait_ge(once("diff_out"), 4)
            for c in range(DC):
                pe.wait_ge(once("mix_sq"), c + 1)
                for b in range(NB):
                    k = b if c < 4 else (c - 3) * NB + b
                    mm = pe.matmul(PX[:, 3, k:k + 1], MSQ[:, c, b * P:(b + 1) * P], ONE[:, 0:1],
                                   start=(c == 0 and b == 0), stop=(c >= 3), skip_group_check=True)
            mm.then_inc(once("mix_sum"), 1)
            for k in range(5):
                pe.wait_ge(once("mix_diag"), 20 if k == 0 else 20)
                if k >= 2:
                    pe.wait_ge(once("mix_r"), k - 1)
                spread("mix", DG1, k, k % 2, "mix_bc")
            pe.wait_ge(once("mix_split"), 8)
            gemm("out1", None)
            norm("n2", SQY)
            norm("n3", SQY)
            pe.wait_ge(once("x2_split"), 8)
            gemm("up0", None)
            gemm("up1", None)
            for q, nxt in enumerate(["up2", "up3", None, None]):
                pe.wait_ge(once("a_lo"), 8 * (q + 1))
                gemm(f"dn{q}", None, AH[:, q % 2], AL[:, q % 2])
                if nxt:
                    gemm(nxt, None)
            norm("n4", SQF)
            norm("n5", SQF)
            pe.wait_ge(once("x3_split"), 8)

            pe.wait_ge(once("wi_split"), 2)
            for b in range(NB):
                for c in range(DC):
                    o = PX[:, 2, b * 8:(b + 1) * 8]
                    tb = slice(b * P, (b + 1) * P)
                    pe.matmul(o, XH[:, c, tb], WIH[:, c, :], start=(c == 0 and b == 0), stop=False, skip_group_check=True)
                    pe.matmul(o, XH[:, c, tb], WIL[:, c, :], start=False, stop=False, skip_group_check=True)
                    mm = pe.matmul(o, XL[:, c, tb], WIH[:, c, :], start=False, stop=(c == DC - 1), skip_group_check=True)
            mm.then_inc(once("wx_ready"), 1)
            gemm("in2a", None)

            pe.wait_ge(once("kv_sq"), 1)
            for b in range(NB):
                mm = pe.matmul(PX[:, 0, b:b + 1], CSQ[:, 0, b * P:(b + 1) * P], ONE[:, 0:1],
                               start=(b == 0), stop=True, skip_group_check=True)
            mm.then_inc(once("kv_sum"), 1)
            pe.matmul(PX[:, 3, :], ONE[:], CKV[:, 1, :], start=True, stop=True).then_inc(once("ln_mean"), 1)
            pe.wait_ge(once("kv_diag"), NB)
            spread("kv", DG, 0, 1, "kv_bc")
            pe.wait_ge(once("ln_sq"), 1)
            for b in range(NB):
                mm = pe.matmul(PX[:, 0, b:b + 1], CSQ[:, 1, b * P:(b + 1) * P], ONE[:, 0:1],
                               start=(b == 0), stop=True, skip_group_check=True)
            mm.then_inc(once("ln_sum"), 1)
            pe.wait_ge(once("ln_diag"), NB)
            spread("ln", DG, 0, 2, "ln_bc")
            pe.wait_ge(once("kv_done"), 1)
            for b in range(NB):
                mm = pe.transpose(PX[:, 3, b * P:(b + 1) * P], CKV[:, 0, b * P:(b + 1) * P], IDN[:])
            mm.then_inc(once("kv_turned"), 1)
            pe.wait_ge(once("ki_done"), 1)
            pe.wait_ge(evac, FIRST["in2b"][0])

            for u in range(3 * IDX_HEADS):
                qb, j = u // IDX_HEADS + 1, u % IDX_HEADS
                n = (qb + 1) * P
                rows = slice((j % 2) * HD, (j % 2) * HD + HD)
                if u >= 4:
                    pe.wait_ge(once("idx_relu"), u - 3)
                elif u == 3:
                    pe.wait_ge(once("kv_copied"), 1)
                pe.matmul(PG[:, u % 4, 0:n], QI[rows, j // 2, qb * P:(qb + 1) * P], CKV[rows, 1, 0:n],
                          start=True, stop=True).then_inc(once("idx_s"), 1)
            pe.wait_ge(once("idx_relu"), 24)
            gemm("in2b", None)

            p0 = FIRST["gattn"][0]

            def one_panel(p, xh, xl):
                s = p % 2
                pe.wait_ge(w_lo, p + 1)
                pe.wait_ge(evac, p - 1)
                for m in range(2):
                    ms = slice(m * P, (m + 1) * P)
                    for c in range(DC):
                        o = PG[:, 2 * s + m, :]
                        pe.matmul(o, WH[:, s, c, ms], xh[:, c, :], start=(c == 0), stop=False)
                        pe.matmul(o, WH[:, s, c, ms], xl[:, c, :], start=False, stop=False)
                        mm = pe.matmul(o, WL[:, s, c, ms], xh[:, c, :], start=False, stop=(c == DC - 1))
                mm.then_inc(panel_done, 1)

            pe.wait_ge(loaded_b2, 48)
            for t in range(4):
                one_panel(p0 + t, XH, XL)
                pe.wait_ge(once("rg_conv"), t + 1)
                if t >= 1:
                    pe.wait_ge(once("rg_gates"), t)
                for m in range(2):
                    pe.matmul(PX[:, m, :], RGW[:, 0, 2 * t + m, :], RGT[:, 0, m, :], start=True, stop=True)
                    mm = pe.matmul(PX[:, 2 + m, :], RGW[:, 1, 2 * t + m, :], RGT[:, 0, m, :], start=True, stop=True)
                mm.then_inc(once("rg_proj"), 1)
            p0 = FIRST["mr"][0]
            for t in range(4):
                one_panel(p0 + 2 * t, XH, XL)
                if t == 0:
                    pe.wait_ge(once("rg_lo"), 4)
                one_panel(p0 + 2 * t + 1, RH, RL)

            def qlat(g):
                if g >= 1:
                    pe.wait_ge(once("mla_y"), g - 1) if g >= 2 else None
                if g == 0:
                    pe.wait_ge(once("rg_gates"), 4)
                for m in range(2):
                    rows = slice(m * HD, (m + 1) * HD)
                    mm = pe.matmul(PX[:, 2 + m, :], UK[rows, g, :], QT[rows, g, :], start=True, stop=True)
                mm.then_inc(once("mla_ql"), 1)

            def mla_scores(u):
                g, qb = divmod(u, NB)
                pe.wait_ge(once("mla_qlc"), g + 1)
                if u >= 2:
                    pe.wait_ge(once("mla_logits"), u - 1)
                n = (qb + 1) * P
                for m in range(2):
                    mm = pe.matmul(PG[:, 2 * (u % 2) + m, 0:n], QL[:, g % 2, m, qb * P:(qb + 1) * P],
                                   CKV[:, 0, 0:n], start=True, stop=True)
                mm.then_inc(once("mla_s"), 1)

            def mla_y(g):
                pe.wait_ge(once("mla_ol"), g + 1)
                for m in range(2):
                    mm = pe.matmul(PX[m * HD:(m + 1) * HD, 2, :], UV[:, 2 * g + m, :], OL[:, m, :],
                                   start=True, stop=True)
                mm.then_inc(once("mla_yp"), 1)

            pe.wait_ge(evac, FIRST["ma"][0])
            qlat(0)
            mla_scores(0)
            mla_scores(1)
            for u in range(32):
                g, qb = divmod(u, NB)
                if u + 2 < 32:
                    mla_scores(u + 2)
                unit_turn("mla", PM, u, qb, 2)
                if qb == 0:
                    if g >= 1:
                        mla_y(g - 1)
                    if g < 7:
                        if g >= 1:
                            pe.wait_ge(once("mla_y"), g)
                        for m in range(2):
                            rows = slice(m * HD, (m + 1) * HD)
                            mm = pe.matmul(PX[:, 2 + m, :], UK[rows, g + 1, :], QT[rows, g + 1, :], start=True, stop=True)
                        mm.then_inc(once("mla_ql"), 1)
                if qb == NB - 1:
                    pe.wait_ge(once("mla_copied"), u + 1)
                    pe.wait_ge(once("mla_qlc"), min(g + 2, 8))
                    if g == 7:
                        pe.wait_ge(once("mla_y"), 7)
                    for m in range(2):
                        for kb in range(NB):
                            mm = pe.matmul(PX[:, 2 + m, kb * P:], CKT[:, kb, :], PTM[:, m, kb, kb * P:],
                                           start=(kb == 0), stop=(kb == NB - 1), skip_group_check=True)
                    mm.then_inc(once("mla_pv"), 1)
            mla_y(7)
            p0 = FIRST["ma"][0]
            for t in range(4):
                one_panel(p0 + 2 * t, XH, XL)
                if t == 0:
                    pe.wait_ge(once("o_split"), 8)
                one_panel(p0 + 2 * t + 1, RH, RL)
            pe.wait_ge(once("m_split"), 8)
            gemm("out2", None)
            norm("n6", GA)

        @block.scalar
        def _(act):
            step_ = Count(act_step)

            def hi(p, s, turn):
                act.wait_ge(raw_in[s], turn * 16 + 16)
                act.activation(WH[:, s].rearrange("p a b -> p (a b)"), RAW[:, s, :], ACT.Copy).then_inc(w_hi, 1)

            def hi_ahead(p, p0b):
                s = p0b % 2
                act.wait_ge(panel_done, p + 1)
                if isinstance(p, int):
                    if p + 2 < NPANELS:
                        hi(p + 2, s, (p + 2) // 2)
                else:
                    raise AssertionError

            def hi_stage(name):
                p0, n = FIRST[name]
                with act.Fori(0, n // 2) as i:
                    for b in range(2):
                        s = (p0 + b) % 2
                        act.wait_ge(panel_done, i * 2 + (p0 + b + 1))
                        hi(None, s, i + (p0 + b + 2) // 2)
                if n % 2:
                    hi_ahead(p0 + n - 1, p0 + n - 1)

            def squares(name, dst, src, n=DC, wait=None):
                for c in range(n):
                    if wait is not None:
                        act.wait_ge(once(wait), c + 1)
                    act.activation(dst[:, c, :], src[:, c, :], ACT.Square).then_inc(once(name + "_sq"), 1)

            def std(name, width, scale, k=0, n=NB, bank=0):
                act.wait_ge(once(name + "_sum"), 1)
                act.activation(STD[:, k:k + n], PX[:, bank, k:k + n], ACT.Sqrt, bias=EPST, scale=1.0 / width)\
                    .then_inc(once(name + "_std"), 1)

            def split(name, ready, src, cname=None, dst=XH):
                for c in range(DC):
                    if ready is not None:
                        act.wait_ge(once(ready), c + 1)
                    if cname is None:
                        act.activation(dst[:, c, :], src[:, c, :], ACT.Copy).then_inc(once(name), 1)
                    else:
                        act.activation(dst[:, c, :], src[:, c, :], ACT.Copy, scale=col(cname, c)).then_inc(once(name), 1)

            act.wait_ge(loaded_c, 32)
            act.wait_ge(loaded_x, 16)
            split("x1_hi", None, XT, "attn_pre")
            hi(0, 0, 0)
            hi(1, 1, 0)
            squares("n1", SQ1, XT)
            act.wait_ge(once("lam_dot"), 2)
            act.activation(LDOT, LDOT, ACT.Exp).then_inc(once("lam_exp"), 1)
            act.wait_ge(once("lru_abs"), 1)
            act.activation(SP[:, 8:16], SP[:, 0:8], ACT.Exp, scale=-1.0).then_inc(once("lru_exp"), 1)
            act.wait_ge(once("eps_set"), 1)
            std("n1", D, D)
            hi_stage("in1")

            for t in range(5):
                act.wait_ge(once("v_turned"), t + 1)
                dst = VA[:].rearrange("p a b -> p (a b)") if t == 0 else VB[:, t - 1].rearrange("p a b -> p (a b)")
                act.activation(dst, PX[:, t % 2, :], ACT.Copy).then_inc(once("v_copied"), 1)

            def swa_exp(h):
                act.wait_ge(once("swa_negmax"), h + 1)
                s = h % 2
                for qb in range(NB):
                    act.activation(PSW[:, s, qb, :], PSW[:, s, qb, :], ACT.Exp, bias=NM[:, 4 * s + qb:4 * s + qb + 1],
                                   scale=SCALE, accum_out=DEN[:, 4 * s + qb:4 * s + qb + 1])
                if h >= 1:
                    act.wait_ge(once("swa_den"), h)
                act.activation(ES, NM[:, 4 * s:4 * s + 4], ACT.Exp, bias=col("sinks", h)).then_inc(once("swa_exp"), 1)

            def swa_copy(h):
                act.wait_ge(once("swa_turned"), h + 1)
                if h >= 2:
                    act.wait_ge(once("swa_pv"), h - 1)
                s = h % 2
                act.activation(PTW[:, s, 0:2, :], PX[:, 0, :].rearrange("p (a b) -> p a b", b=256), ACT.Copy)
                act.activation(PTW[:, s, 2:4, :].rearrange("p a b -> p (a b)")[:, 0:384], PX[:, 1, 0:384], ACT.Copy)\
                    .then_inc(once("swa_copied"), 1)

            for h in range(8):
                swa_exp(h)
                if h >= 1:
                    swa_copy(h - 1)
            swa_copy(7)

            def unit_exp(pre, buf, u, qb):
                n = (qb + 1) * P
                act.wait_ge(once(pre + "_negmax"), u + 1)
                s = u % 2
                for m in range(2):
                    ins = act.activation(buf[:, s, m, 0:n], buf[:, s, m, 0:n], ACT.Exp,
                                         bias=NM[:, 2 * s + m:2 * s + m + 1], scale=SCALE,
                                         accum_out=DEN[:, 2 * s + m:2 * s + m + 1])
                ins.then_inc(once(pre + "_exp"), 1)

            def unit_copy(pre, dst, u, qb, maps):
                act.wait_ge(once(pre + "_turned"), u + 1)
                for m in range(maps):
                    ins = act.activation(dst(m, qb), PX[:, m, 0:(qb + 1) * P].rearrange("p (a b) -> p a b", b=P), ACT.Copy)
                ins.then_inc(once(pre + "_copied"), 1)

            def diff_dst(h):
                return lambda m, qb: PTD[:, h % 2, 0:qb + 1, qb * P:(qb + 1) * P]

            for u in range(16):
                unit_exp("diff", PD, u, u % NB)
                if u >= 1:
                    h, qb = divmod(u - 1, NB)
                    if h >= 2 and qb == 0:
                        act.wait_ge(once("diff_pv"), h - 1)
                    if u - 1 == 0:
                        act.wait_ge(once("swa_pv"), 8)
                    unit_copy("diff", diff_dst(h), u - 1, qb, 1)
            unit_copy("diff", diff_dst(3), 15, 3, 1)

            act.wait_ge(once("diff_out"), 4)
            for c in range(DC):
                act.activation(MSQ[:, c, :], MIX[:, c, :], ACT.Square).then_inc(once("mix_sq"), 1)
            act.wait_ge(once("mix_sum"), 1)
            act.activation(STD[:, 0:4], PX[:, 3, 0:4], ACT.Sqrt, bias=EPST, scale=1.0 / 512).then_inc(once("mix_std"), 1)
            act.activation(STD[:, 4:20], PX[:, 3, 4:20], ACT.Sqrt, bias=EPST, scale=1.0 / 128).then_inc(once("mix_std"), 1)
            split("mix_hi", "mix_y", MIX)
            hi_stage("out1")
            act.wait_ge(evac, FIRST["up0"][0])
            squares("n2", SQY, Y1)
            std("n2", D, D)
            squares("n3", SQY, XT, wait="x2_new")
            split("x2_hi", None, XT, "ffn_pre")
            std("n3", D, D)

            def up(q):
                p0 = FIRST[f"up{q}"][0]

                def conv0(c, k, b, p):
                    act.wait_ge(evac, p + 1)
                    for m in range(2):
                        ins = act.activation(C[:, b, m, :], U[:, b, m, :], ACT.Identity,
                                             bias=col("cb", k + 32 * m), scale=col("cw2", k + 32 * m))
                    ins.then_inc(once("conv0"), 1)

                def a_hi(c, n, b):
                    act.wait_ge(once("a_ready"), n)
                    act.activation(AH[:, q % 2, c, :] if isinstance(c, int) else
                                   AH[:, q % 2, bass.ds(c, 1), :].rearrange("p a n -> p (a n)"),
                                   Z[:, b, :], ACT.Copy).then_inc(once("a_hi"), 1)

                def tanh(n, b):
                    act.wait_ge(once("inner"), n)
                    act.activation(Z[:, b, :], Z[:, b, :], ACT.Tanh, scale=0.7978845608028654).then_inc(once("tanh"), 1)

                def panel(i, b, first):
                    p = i * 2 + (p0 + b)
                    c = i * 2 + b
                    n = c + 8 * q
                    act.wait_ge(panel_done, p + 1)
                    hi(None, (p0 + b) % 2, i + (p0 + b + 2) // 2)
                    conv0(c, n, b, p)
                    if not first:
                        a_hi(c - 1, n, 1 - b)
                    tanh(n + 1, b)

                panel(0, 0, True)
                panel(0, 1, False)
                with act.Fori(1, 4) as i:
                    panel(i, 0, False)
                    panel(i, 1, False)
                a_hi(7, 8 * q + 8, 1)

            up(0)
            up(1)
            hi_stage("dn0")
            up(2)
            hi_stage("dn1")
            up(3)
            hi_stage("dn2")
            hi_stage("dn3")
            act.wait_ge(evac, FIRST["in2a"][0])
            squares("n4", SQF, FA)
            std("n4", D, D)
            squares("n5", SQF, XT, wait="x3_new")
            split("x3_hi", None, XT, "norm2")
            act.dma_start(spill, XT[:]).then_inc(spilled, 16)
            act.dma_start(WIR[:], wi_in).then_inc(loaded_wi, 16)
            std("n5", D, D)
            act.wait_ge(loaded_wi, 16)
            act.activation(WIH[:], WIR[:], ACT.Copy).then_inc(once("wi_hi"), 1)
            hi_stage("in2a")
            act.wait_ge(once("x3_split"), 8)
            act.wait_ge(spilled, 16)
            act.dma_start(RGW[:], rgw_in).then_inc(loaded_b2, 16)
            act.dma_start(UK[:], uk_in).then_inc(loaded_b2, 16)
            act.dma_start(UV[:], uv_in).then_inc(loaded_b2, 16)
            act.wait_ge(evac, FIRST["in2b"][0])
            act.activation(CSQ[:, 0, :], CKV[:, 0, :], ACT.Square).then_inc(once("kv_sq"), 1)
            std("kv", 128, 128)
            act.wait_ge(once("ln_x"), 1)
            act.activation(CSQ[:, 1, :], KC[:], ACT.Square).then_inc(once("ln_sq"), 1)
            std("ln", 128, 128)
            act.wait_ge(once("kv_turned"), 1)
            act.activation(CKT[:].rearrange("p a b -> p (a b)"), PX[:, 3, :], ACT.Copy).then_inc(once("kv_copied"), 1)
            for u in range(24):
                n = (u // 8 + 2) * P
                act.wait_ge(once("idx_s"), u + 1)
                if u >= 2:
                    act.wait_ge(once("idx_acc"), u - 1)
                act.activation(RLU[:, u % 2, 0:n], PG[:, u % 4, 0:n], ACT.Relu).then_inc(once("idx_relu"), 1)
            hi_stage("in2b")

            p0 = FIRST["gattn"][0]
            for t in range(4):
                for m in range(2):
                    if t >= 1:
                        act.wait_ge(once("rg_h"), t)
                    act.activation(RGT[:, 0, m, :], XR[:, 2 * t + m, :], ACT.Identity, bias=col("rb", 2 * t + m),
                                   scale=col("rw", 24 + 2 * t + m)).then_inc(once("rg_conv0"), 1)
                act.activation(RGT[:, 4], GR[:, 2 * t:2 * t + 2, :], ACT.Sigmoid).then_inc(once("rg_sg"), 1)
                hi_ahead(p0 + t, p0 + t)
                act.wait_ge(once("rg_proj"), t + 1)
                for m in range(2):
                    act.activation(RGT[:, 1, m, :], PX[:, m, :], ACT.Sigmoid, bias=col("b_rg_a", 2 * t + m)).then_inc(act_step, 1)
                    step_.n += 1
                for m in range(2):
                    act.activation(RGT[:, 2, m, :], PX[:, 2 + m, :], ACT.Sigmoid, bias=col("b_rg_x", 2 * t + m))\
                        .then_inc(act_step, 1)
                    step_.n += 1
                act.wait_ge(act_step, step_.n)
                for m in range(2):
                    ins = act.activation(RGT[:, 3, m, :], RGT[:, 1, m, :], ACT.Exp, scale=NEG_SP8[:, 2 * t + m:2 * t + m + 1])
                ins.then_inc(once("rg_gates"), 1)
                act.wait_ge(once("rg_gates"), t + 1)
                for m in range(2):
                    ins = act.activation(RGT[:, 1, m, :], RGT[:, 1, m, :], ACT.Tanh, scale=POS_SP8[:, 2 * t + m:2 * t + m + 1])
                ins.then_inc(once("rg_tanh"), 1)
                act.wait_ge(once("rg_m"), t + 1)
                act.activation(RGT[:, 4], RGT[:, 4], ACT.Sqrt).then_inc(once("rg_sqrt"), 1)
                act.wait_ge(once("rg_y"), t + 1)
                act.activation(RH[:, 2 * t:2 * t + 2, :], RGT[:, 2], ACT.Copy).then_inc(once("rg_hi"), 1)

            def gate_stage(name, bcol):
                p0 = FIRST[name][0]
                for t in range(4):
                    hi_ahead(p0 + 2 * t, p0 + 2 * t)
                    act.wait_ge(evac, p0 + 2 * t + 1)
                    for m in range(2):
                        act.activation(SG[:, m, :], SG[:, m, :], ACT.Sigmoid, bias=col("b_merge", bcol + 2 * t + m))\
                            .then_inc(once(name + "_sg"), 1)
                    hi_ahead(p0 + 2 * t + 1, p0 + 2 * t + 1)

            gate_stage("mr", 8)

            act.wait_ge(panel_done, FIRST["ma"][0])
            for t in range(4):
                if t >= 1:
                    act.wait_ge(once("silu_ga"), t)
                act.activation(SGA[:], GA[:, 2 * t:2 * t + 2, :], ACT.Sigmoid).then_inc(once("sig_ga"), 1)

            def ql_copy(g):
                act.wait_ge(once("mla_ql"), g + 1)
                for m in range(2):
                    ins = act.activation(QL[:, g % 2, m, :], PX[:, 2 + m, :], ACT.Copy)
                ins.then_inc(once("mla_qlc"), 1)

            ql_copy(0)
            for u in range(32):
                g, qb = divmod(u, NB)
                unit_exp("mla", PM, u, qb)
                if u >= 1:
                    gp, qp = divmod(u - 1, NB)
                    if qp == 0 and gp >= 1:
                        act.wait_ge(once("mla_pv"), gp)
                    unit_copy("mla", lambda m, q: PTM[:, m, 0:q + 1, q * P:(q + 1) * P], u - 1, qp, 2)
                if qb == 1 and g < 7:
                    ql_copy(g + 1)
            unit_copy("mla", lambda m, q: PTM[:, m, 0:q + 1, q * P:(q + 1) * P], 31, 3, 2)
            act.wait_ge(once("mla_y"), 8)
            split("o_hi", None, GA, None, RH)
            gate_stage("ma", 0)
            act.wait_ge(evac, FIRST["out2"][0])
            act.dma_start(XT[:], spill).then_inc(reloaded, 16)
            split("m_hi", None, M2)
            p0 = FIRST["out2"][0]
            for t in range(4):
                hi_ahead(p0 + t, p0 + t)
            for c in range(DC):
                act.wait_ge(evac, p0 + c // 2 + 1)
                act.activation(GA[:, c, :], M2[:, c, :], ACT.Square).then_inc(once("n6_sq"), 1)
            std("n6", D, D)

        @block.vector
        def _(dve):
            step_ = Count(dve_step)

            def link(ins):
                step_(ins)
                dve.wait_ge(dve_step, step_.n)

            def diags(name, dg, k0, n, scale=None):
                for k in range(k0, k0 + n):
                    dve.tensor_scalar(dg[:, k, :], IDN[:], RT[:, k:k + 1], scale, ALU.mult,
                                      *([ALU.mult] if scale is not None else [])).then_inc(once(name + "_diag"), 1)

            def recip_r(name, k=0, n=NB, count=1):
                dve.wait_ge(once(name + "_std"), count)
                link(dve.reciprocal(RT[:, k:k + n], STD[:, k:k + n]))

            def norm(name, dst=R):
                recip_r(name)
                diags(name, DG, 0, NB)
                dve.wait_ge(once(name + "_bc"), 1)
                link(dve.tensor_copy(dst[:], PX[:, 1, :]))

            def split(name, hi_name, src, cname=None, dh=XH, dl=XL):
                for c in range(DC):
                    dve.wait_ge(once(hi_name), c + 1)
                    if cname is None:
                        ins = dve.tensor_tensor(dl[:, c, :], src[:, c, :], dh[:, c, :].bitcast(F32), ALU.subtract)
                    else:
                        ins = dve.scalar_tensor_tensor(out=dl[:, c, :], in0=src[:, c, :], scalar=col(cname, c),
                                                       in1=dh[:, c, :].bitcast(F32), op0=ALU.mult, op1=ALU.subtract)
                    ins.then_inc(once(name), 1)

            def psum_of(p0b):
                s = p0b % 2
                return PG[:, 2 * s:2 * s + 2, :]

            def evac_stage(name, out, p0=None):
                p0, n = FIRST[name]

                def step(p, k, b, i):
                    dve.wait_ge(panel_done, p + 1)
                    out(k, psum_of(p0 + b), b).then_inc(evac, 1)

                pairs(dve, name, step)

            def two(buf, k, off=0):
                if isinstance(k, int):
                    return buf[:, 2 * k + off:2 * k + off + 2, :]
                return buf[:, bass.ds(k * 2 + off, 2), :]

            def rr():
                return R[:].rearrange("p (a n) -> p a n", a=1).broadcast_to([P, 2, S])

            dve.memset(EPST, EPS).then_inc(once("eps_set"), 1)
            dve.wait_ge(loaded_c, 32)
            for k in range(2):
                dve.tensor_tensor_reduce(out=R[:, k * HD:(k + 1) * HD], in0=LV[:, 2 * k, :], in1=LV[:, 2 * k + 1, :], scale=1.0,
                                         scalar=0.0, op0=ALU.mult, op1=ALU.add, accum_out=LDOT[:, k:k + 1])\
                    .then_inc(once("lam_dot"), 1)
            lru = col("lru", 0, 8)
            link(dve.tensor_scalar(SP[:, 0:8], lru, -1.0, None, ALU.mult))
            dve.tensor_tensor(SP[:, 0:8], SP[:, 0:8], lru, ALU.max).then_inc(once("lru_abs"), 1)
            dve.tensor_scalar(SINK8, col("sinks", 0, 8), 1.0 / SCALE, None, ALU.mult).then_inc(dve_step, 1)
            step_.n += 1
            dve.wait_ge(loaded_x, 16)
            split("x1_split", "x1_hi", XT, "attn_pre")
            dve.wait_ge(once("lam_exp"), 1)
            link(dve.tensor_scalar(LDOT[:, 0:1], LDOT[:, 0:1], LAMBDA_INIT, None, ALU.add))
            link(dve.tensor_tensor(LAM, LDOT[:, 0:1], LDOT[:, 1:2], ALU.subtract))
            dve.wait_ge(once("lru_exp"), 1)
            link(dve.tensor_scalar(SP[:, 0:8], SP[:, 8:16], 2.0, None, ALU.add))
            link(dve.reciprocal(SP[:, 0:8], SP[:, 0:8]))
            link(dve.tensor_tensor(SP[:, 0:8], SP[:, 0:8], SP[:, 8:16], ALU.mult))
            link(dve.tensor_tensor(SP[:, 8:16], SP[:, 0:8], SP[:, 0:8], ALU.mult))
            link(dve.tensor_scalar(SP[:, 16:24], SP[:, 8:16], 1.0 / 17, 1.0 / 15, ALU.mult, ALU.add))
            for d in (13, 11, 9, 7, 5, 3, 1):
                link(dve.tensor_tensor(SP[:, 16:24], SP[:, 16:24], SP[:, 8:16], ALU.mult))
                link(dve.tensor_scalar(SP[:, 16:24], SP[:, 16:24], 1.0 / d, None, ALU.add))
            link(dve.tensor_tensor(SP[:, 16:24], SP[:, 16:24], SP[:, 0:8], ALU.mult))
            link(dve.tensor_scalar(SP[:, 8:16], lru, -1.0, 0.0, ALU.mult, ALU.max))
            link(dve.scalar_tensor_tensor(out=SP[:, 0:8], in0=SP[:, 16:24], scalar=2.0, in1=SP[:, 8:16],
                                          op0=ALU.mult, op1=ALU.add))
            dve.tensor_scalar(NEG_SP8, SP[:, 0:8], -8.0, None, ALU.mult).then_inc(dve_step, 1)
            link(dve.tensor_scalar(POS_SP8, SP[:, 0:8], 8.0, None, ALU.mult))
            step_.n += 1
            dve.wait_ge(consts, 11)
            norm("n1")

            evac_stage("in1", lambda k, ps, b: dve.tensor_tensor(two(PROJ, k), ps, rr(), ALU.mult))

            def swa_logits(h):
                s = h % 2
                dve.wait_ge(once("swa_s"), h + 1)
                if h >= 2:
                    dve.wait_ge(once("swa_turned"), h - 1)
                dve.scalar_tensor_tensor(out=PSW[:, s].rearrange("p a b -> p (a b)"), in0=DS4[:].rearrange("p a b -> p (a b)"),
                                         scalar=-SLOPES_1[h] / SCALE,
                                         in1=PG[:, 2 * s:2 * s + 2, :].rearrange("p a b -> p (a b)"),
                                         op0=ALU.mult, op1=ALU.add).then_inc(once("swa_logits"), 1)
                dve.wait_ge(once("swa_logits"), h + 1)
                link(dve.tensor_reduce(MX, PSW[:, s], AX_X, ALU.max))
                dve.tensor_scalar(NM[:, 4 * s:4 * s + 4], MX, SINK8[:, h:h + 1], -SCALE, ALU.max, ALU.mult)\
                    .then_inc(once("swa_negmax"), 1)

            def swa_probs(h):
                s = h % 2
                den = DEN[:, 4 * s:4 * s + 4]
                dve.wait_ge(once("swa_exp"), h + 1)
                dve.tensor_tensor(den, den, ES, ALU.add).then_inc(once("swa_den"), 1)
                dve.wait_ge(once("swa_den"), h + 1)
                link(dve.reciprocal(den, den))
                for qb in range(NB):
                    ins = dve.tensor_scalar(PSW[:, s, qb, :], PSW[:, s, qb, :], den[:, qb:qb + 1], None, ALU.mult)
                ins.then_inc(once("swa_probs"), 1)

            def swa_out(h):
                g, j = divmod(h, SWA_PAIRS)
                rows = slice(g * HD, (g + 1) * HD)
                dve.wait_ge(once("swa_pv"), h + 1)
                dve.tensor_copy(MIX[rows, j, :], PX[rows, 2 + h % 2, :]).then_inc(once("swa_out"), 1)

            swa_logits(0)
            for h in range(8):
                if h + 1 < 8:
                    swa_logits(h + 1)
                swa_probs(h)
                if h >= 1:
                    swa_out(h - 1)
            swa_out(7)

            def unit_logits(pre, buf, u, qb, dist, slopes):
                s, n = u % 2, (qb + 1) * P
                dve.wait_ge(once(pre + "_s"), u + 1)
                if u >= 2:
                    dve.wait_ge(once(pre + "_turned"), u - 1)
                for m in range(2):
                    ins = dve.scalar_tensor_tensor(out=buf[:, s, m, 0:n], in0=dist, scalar=-slopes[m] / SCALE,
                                                   in1=PG[:, 2 * s + m, 0:n], op0=ALU.mult, op1=ALU.add)
                ins.then_inc(once(pre + "_logits"), 1)
                dve.wait_ge(once(pre + "_logits"), u + 1)
                link(dve.tensor_reduce(MX[:, 0:2], buf[:, s, :, 0:n], AX_X, ALU.max))
                dve.tensor_scalar(NM[:, 2 * s:2 * s + 2], MX[:, 0:2], -SCALE, None, ALU.mult).then_inc(once(pre + "_negmax"), 1)

            def diff_probs(u, qb):
                s, n = u % 2, (qb + 1) * P
                den = DEN[:, 2 * s:2 * s + 2]
                dve.wait_ge(once("diff_exp"), u + 1)
                link(dve.reciprocal(den, den))
                link(dve.tensor_scalar(RTL, den[:, 1:2], LAM, None, ALU.mult))
                link(dve.tensor_scalar(PD[:, s, 1, 0:n], PD[:, s, 1, 0:n], RTL, None, ALU.mult))
                dve.scalar_tensor_tensor(out=PD[:, s, 0, 0:n], in0=PD[:, s, 0, 0:n], scalar=den[:, 0:1],
                                         in1=PD[:, s, 1, 0:n], op0=ALU.mult, op1=ALU.subtract).then_inc(once("diff_probs"), 1)

            def diff_logits(u):
                h, qb = divmod(u, NB)
                sl = SLOPES_1[8 + h]
                unit_logits("diff", PD, u, qb, EC[:, (3 - qb) * P:], [sl, sl])

            diff_logits(0)
            for u in range(16):
                h, qb = divmod(u, NB)
                if u + 1 < 16:
                    diff_logits(u + 1)
                diff_probs(u, qb)
                if qb == NB - 1:
                    dve.wait_ge(once("diff_pv"), h + 1)
                    dve.tensor_copy(MIX[:, 4 + h, :], PX[:, 2, :]).then_inc(once("diff_out"), 1)

            recip_r("mix", 0, 20, 2)
            diags("mix", DG1, 0, 4)
            diags("mix", DG1, 4, 16, 1.0 - LAMBDA_INIT)
            for k in range(5):
                dve.wait_ge(once("mix_bc"), k + 1)
                dve.tensor_copy(RM[:, k, :], PX[:, k % 2, :]).then_inc(once("mix_r"), 1)
            dve.wait_ge(once("mix_r"), 5)
            for c in range(DC):
                dve.scalar_tensor_tensor(out=MIX[:, c, :], in0=MIX[:, c, :],
                                         scalar=col("swa_out", c) if c < 4 else col("subln", 0),
                                         in1=RM[:, 0 if c < 4 else c - 3, :], op0=ALU.mult, op1=ALU.mult)\
                    .then_inc(once("mix_y"), 1)
            dve.wait_ge(once("mix_y"), 8)
            split("mix_split", "mix_hi", MIX)
            evac_stage("out1", lambda k, ps, b: dve.tensor_scalar(two(Y1, k), ps, 1.0, None, ALU.mult))

            def post(name, y, cname, new):
                norm(name)
                for c in range(DC):
                    link(dve.scalar_tensor_tensor(out=y[:, c, :], in0=y[:, c, :], scalar=col(cname, c), in1=R[:],
                                                  op0=ALU.mult, op1=ALU.mult))
                    dve.tensor_tensor(XT[:, c, :], XT[:, c, :], y[:, c, :], ALU.add).then_inc(once(new), 1)

            post("n2", Y1, "attn_post", "x2_new")
            dve.wait_ge(once("x2_new"), 8)
            split("x2_split", "x2_hi", XT, "ffn_pre")
            norm("n3")

            def up(q):
                p0 = FIRST[f"up{q}"][0]

                def one(buf, c):
                    return buf[:, q % 2, c, :] if isinstance(c, int) else \
                        buf[:, q % 2, bass.ds(c, 1), :].rearrange("p a n -> p (a n)")

                def a_mult(n, b):
                    dve.wait_ge(once("tanh"), n)
                    link(dve.scalar_tensor_tensor(out=Z[:, b, :], in0=Z[:, b, :], scalar=1.0, in1=C[:, b, 0, :],
                                                  op0=ALU.add, op1=ALU.mult))
                    dve.scalar_tensor_tensor(out=Z[:, b, :], in0=Z[:, b, :], scalar=0.5, in1=C[:, b, 1, :],
                                             op0=ALU.mult, op1=ALU.mult).then_inc(once("a_ready"), 1)

                def a_lo(c, n, b):
                    dve.wait_ge(once("a_hi"), n)
                    dve.tensor_tensor(one(AL, c), Z[:, b, :], one(AH, c).bitcast(F32), ALU.subtract)\
                        .then_inc(once("a_lo"), 1)

                def panel(i, b, first):
                    p = i * 2 + (p0 + b)
                    c = i * 2 + b
                    n = c + 8 * q
                    dve.wait_ge(panel_done, p + 1)
                    dve.tensor_tensor(U[:, b], psum_of(p0 + b), rr(), ALU.mult).then_inc(evac, 1)
                    if not first:
                        a_mult(n, 1 - b)
                    dve.wait_ge(evac, p + 1)
                    dve.wait_ge(once("conv0"), n + 1)
                    for m in range(2):
                        step_(dve.scalar_tensor_tensor(out=C[:, b, m, 1:], in0=U[:, b, m, 0:S - 1], scalar=col("cw1", n + 32 * m),
                                                       in1=C[:, b, m, 1:], op0=ALU.mult, op1=ALU.add))
                    dve.wait_ge(dve_step, step_.n)
                    for m in range(2):
                        step_(dve.scalar_tensor_tensor(out=C[:, b, m, 2:], in0=U[:, b, m, 0:S - 2], scalar=col("cw0", n + 32 * m),
                                                       in1=C[:, b, m, 2:], op0=ALU.mult, op1=ALU.add))
                    dve.wait_ge(dve_step, step_.n)
                    link(dve.scalar_tensor_tensor(out=Z[:, b, :], in0=C[:, b, 0, :], scalar=0.044715, in1=C[:, b, 0, :],
                                                  op0=ALU.mult, op1=ALU.mult))
                    dve.scalar_tensor_tensor(out=Z[:, b, :], in0=Z[:, b, :], scalar=1.0, in1=C[:, b, 0, :],
                                             op0=ALU.add, op1=ALU.mult).then_inc(once("inner"), 1)
                    if not first:
                        a_lo(c - 1, n, 1 - b)

                panel(0, 0, True)
                panel(0, 1, False)
                base, per = step_.n, 12
                with dve.Fori(1, 4) as i:
                    step_.n = i * per + (base - per)
                    panel(i, 0, False)
                    panel(i, 1, False)
                step_.n = base + 3 * per
                a_mult(8 * q + 8, 1)
                a_lo(7, 8 * q + 8, 1)

            up(0)
            up(1)
            evac_stage("dn0", lambda k, ps, b: dve.tensor_scalar(two(FA, k), ps, 1.0, None, ALU.mult))
            add_f = lambda k, ps, b: dve.tensor_tensor(two(FA, k), ps, two(FA, k), ALU.add)
            up(2)
            evac_stage("dn1", add_f)
            up(3)
            evac_stage("dn2", add_f)
            evac_stage("dn3", add_f)
            post("n4", FA, "ffn_post", "x3_new")
            dve.wait_ge(once("x3_new"), 8)
            split("x3_split", "x3_hi", XT, "norm2")
            dve.wait_ge(once("wi_hi"), 1)
            dve.tensor_tensor(WIL[:], WIR[:], WIH[:].bitcast(F32), ALU.subtract).then_inc(once("wi_split"), 2)
            norm("n5")

            dve.wait_ge(once("wx_ready"), 1)
            for b in range(NB):
                dve.tensor_scalar(WX[:, 8 * b:8 * b + 8], PX[:, 2, 8 * b:8 * b + 8], RT[:, b:b + 1],
                                  IDX_HEADS ** -0.5 * HD ** -0.5, ALU.mult, ALU.mult).then_inc(dve_step, 1)
                step_.n += 1
            p0 = FIRST["in2a"][0]
            for t in range(7):
                dve.wait_ge(panel_done, p0 + t + 1)
                dst = CKV[:] if t == 0 else two(QI, t - 1) if t < 3 else two(QT, t - 3)
                dve.tensor_tensor(dst, psum_of(p0 + t), rr(), ALU.mult).then_inc(evac, 1)
            dve.wait_ge(evac, p0 + 7)
            dve.wait_ge(once("ln_mean"), 1)
            dve.scalar_tensor_tensor(out=KC[:], in0=PX[:, 3, :], scalar=-1.0 / P, in1=CKV[:, 1, :],
                                     op0=ALU.mult, op1=ALU.add).then_inc(once("ln_x"), 1)
            recip_r("kv")
            diags("kv", DG, 0, NB)
            dve.wait_ge(once("kv_bc"), 1)
            dve.scalar_tensor_tensor(out=CKV[:, 0, :], in0=CKV[:, 0, :], scalar=col("kv_norm", 0), in1=PX[:, 1, :],
                                     op0=ALU.mult, op1=ALU.mult).then_inc(once("kv_done"), 1)
            recip_r("ln")
            diags("ln", DG, 0, NB)
            dve.wait_ge(once("ln_bc"), 1)
            link(dve.scalar_tensor_tensor(out=KC[:], in0=KC[:], scalar=col("ln_g", 0), in1=PX[:, 2, :],
                                          op0=ALU.mult, op1=ALU.mult))
            dve.tensor_scalar(CKV[:, 1, :], KC[:], col("ln_b", 0), None, ALU.add).then_inc(once("ki_done"), 1)
            OFF = {1: 0, 2: 256, 3: 640}
            for u in range(24):
                qb, j = u // 8 + 1, u % 8
                n = (qb + 1) * P
                acc = IA[:, OFF[qb]:OFF[qb] + n]
                if j == 0:
                    link(dve.tensor_scalar(acc, EC[:, (3 - qb) * P:], 1e29, -3e38, ALU.is_ge, ALU.mult))
                dve.wait_ge(once("idx_relu"), u + 1)
                dve.scalar_tensor_tensor(out=acc, in0=RLU[:, u % 2, 0:n], scalar=WX[:, 8 * qb + j:8 * qb + j + 1],
                                         in1=acc, op0=ALU.mult, op1=ALU.add).then_inc(once("idx_acc"), 1)
                dve.wait_ge(once("idx_acc"), u + 1)
            link(dve.tensor_copy(IW[:], IA[:]))

            def settled():
                dve.wait_ge(dve_step, step_.n)
                dve.memset(WORD, 0.0)

            def topk_round():
                blocks = [(M8[:, 8 * qb - 8:8 * qb], IW[:, OFF[qb]:OFF[qb] + (qb + 1) * P]) for qb in (1, 2, 3)]
                for m8, w in blocks:
                    step_(dve.max(m8, w))
                settled()
                for m8, w in blocks:
                    step_(dve.match_replace(out=w, in_to_replace=m8, in_values=w, imm_value=-3.3e38))
                settled()

            p0 = FIRST["in2b"][0]
            for half, buf in enumerate((XR, GR)):
                base = step_.n
                with dve.Fori(0, 2) as i:
                    step_.n = i * 24 + base
                    for b in range(2):
                        p = i * 2 + (p0 + 4 * half + b)
                        dve.wait_ge(panel_done, p + 1)
                        dve.tensor_tensor(two(buf, i * 2 + b), psum_of(p0 + b), rr(), ALU.mult).then_inc(evac, 1)
                        topk_round()
                        topk_round()
                step_.n = base + 48
            link(dve.tensor_scalar(IW[:], IW[:], -3.2e38, FAR, ALU.is_ge, ALU.mult))
            for qb in (1, 2, 3):
                w = IW[:, OFF[qb]:OFF[qb] + (qb + 1) * P]
                dve.tensor_tensor(MD[:, OFF[qb]:OFF[qb] + (qb + 1) * P], w, EC[:, (3 - qb) * P:], ALU.add)\
                    .then_inc(once("md_done"), 1)
            dve.wait_ge(once("md_done"), 3)

            p0 = FIRST["gattn"][0]
            for t in range(4):
                tt = slice(2 * t, 2 * t + 2)
                xc, r_, i_, a_, m_ = (RGT[:, k] for k in range(5))
                dve.wait_ge(once("rg_conv0"), 2 * t + 2)
                for d in (1, 2, 3):
                    for m in range(2):
                        step_(dve.scalar_tensor_tensor(out=xc[:, m, d:], in0=XR[:, 2 * t + m, 0:S - d],
                                                       scalar=col("rw", (3 - d) * 8 + 2 * t + m), in1=xc[:, m, d:],
                                                       op0=ALU.mult, op1=ALU.add)) if d < 3 else \
                            dve.scalar_tensor_tensor(out=xc[:, m, d:], in0=XR[:, 2 * t + m, 0:S - d],
                                                     scalar=col("rw", (3 - d) * 8 + 2 * t + m), in1=xc[:, m, d:],
                                                     op0=ALU.mult, op1=ALU.add).then_inc(once("rg_conv_m"), 1)
                    if d < 3:
                        dve.wait_ge(dve_step, step_.n)
                dve.wait_ge(once("rg_conv_m"), 2 * t + 2)
                dve.wait_ge(once("rg_sg"), t + 1)
                dve.tensor_tensor(GR[:, tt, :], GR[:, tt, :], m_, ALU.mult).then_inc(once("rg_conv"), 1)
                dve.wait_ge(panel_done, p0 + t + 1)
                dve.tensor_tensor(two(GA, t), psum_of(p0 + t), rr(), ALU.mult).then_inc(evac, 1)
                dve.wait_ge(once("rg_gates"), t + 1)
                step_(dve.tensor_tensor(i_, i_, xc, ALU.mult))
                link(dve.tensor_tensor(m_, a_, a_, ALU.mult))
                dve.wait_ge(once("rg_tanh"), t + 1)
                dve.scalar_tensor_tensor(out=m_, in0=m_, scalar=1.0, in1=r_, op0=ALU.add, op1=ALU.mult)\
                    .then_inc(once("rg_m"), 1)
                dve.wait_ge(once("rg_sqrt"), t + 1)
                link(dve.tensor_tensor(i_, i_, m_, ALU.mult))
                for m in range(2):
                    ins = dve.tensor_tensor_scan(out=xc[:, m, :], data0=a_[:, m, :], data1=i_[:, m, :], initial=0.0,
                                                 op0=ALU.mult, op1=ALU.add)
                    step_(ins) if m == 0 else ins.then_inc(once("rg_hs"), 1)
                dve.wait_ge(dve_step, step_.n)
                dve.wait_ge(once("rg_hs"), t + 1)
                dve.tensor_tensor(i_, xc, GR[:, tt, :], ALU.mult).then_inc(once("rg_y"), 1)
                dve.wait_ge(once("rg_y"), t + 1)
                dve.wait_ge(once("rg_hi"), t + 1)
                dve.tensor_tensor(RL[:, tt, :], i_, RH[:, tt, :].bitcast(F32), ALU.subtract).then_inc(once("rg_lo"), 1)
                dve.wait_ge(once("rg_lo"), t + 1)
                dve.tensor_copy(RTL, RTL).then_inc(once("rg_h"), 1)

            p0 = FIRST["mr"][0]
            for t in range(4):
                dve.wait_ge(panel_done, p0 + 2 * t + 1)
                dve.tensor_tensor(SG[:], psum_of(p0), rr(), ALU.mult).then_inc(evac, 1)
                dve.wait_ge(panel_done, p0 + 2 * t + 2)
                dve.wait_ge(once("mr_sg"), 2 * t + 2)
                dve.tensor_tensor(two(M2, t), psum_of(p0 + 1), SG[:], ALU.mult).then_inc(evac, 1)
                dve.wait_ge(evac, p0 + 2 * t + 2)
            for t in range(4):
                dve.wait_ge(once("sig_ga"), t + 1)
                dve.tensor_tensor(two(GA, t), two(GA, t), SGA[:], ALU.mult).then_inc(once("silu_ga"), 1)
            dve.wait_ge(once("silu_ga"), 4)

            def mla_logits(u):
                g, qb = divmod(u, NB)
                dist = EC[:, 3 * P:] if qb == 0 else MD[:, OFF[qb]:OFF[qb] + (qb + 1) * P]
                unit_logits("mla", PM, u, qb, dist, SLOPES_2[2 * g:2 * g + 2])

            def mla_probs(u, qb):
                s, n = u % 2, (qb + 1) * P
                den = DEN[:, 2 * s:2 * s + 2]
                dve.wait_ge(once("mla_exp"), u + 1)
                link(dve.reciprocal(den, den))
                for m in range(2):
                    ins = dve.tensor_scalar(PM[:, s, m, 0:n], PM[:, s, m, 0:n], den[:, m:m + 1], None, ALU.mult)
                ins.then_inc(once("mla_probs"), 1)

            def mla_gate(g):
                dve.wait_ge(once("mla_yp"), g + 1)
                dve.tensor_tensor(GA[:, g, :], PX[:, 2, :], GA[:, g, :], ALU.mult).then_inc(once("mla_y"), 1)

            mla_logits(0)
            for u in range(32):
                g, qb = divmod(u, NB)
                if u + 1 < 32:
                    mla_logits(u + 1)
                mla_probs(u, qb)
                if qb == 0 and g >= 1:
                    mla_gate(g - 1)
                if qb == NB - 1:
                    dve.wait_ge(once("mla_pv"), g + 1)
                    dve.tensor_copy(OL[:], PX[:, 2:4, :]).then_inc(once("mla_ol"), 1)
            mla_gate(7)
            split("o_split", "o_hi", GA, None, RH, RL)
            p0 = FIRST["ma"][0]
            for t in range(4):
                dve.wait_ge(panel_done, p0 + 2 * t + 1)
                dve.tensor_tensor(SG[:], psum_of(p0), rr(), ALU.mult).then_inc(evac, 1)
                dve.wait_ge(panel_done, p0 + 2 * t + 2)
                dve.wait_ge(once("ma_sg"), 2 * t + 2)
                link(dve.tensor_tensor(SG[:], psum_of(p0 + 1), SG[:], ALU.mult))
                dve.tensor_tensor(two(M2, t), two(M2, t), SG[:], ALU.add).then_inc(evac, 1)
                dve.wait_ge(evac, p0 + 2 * t + 2)
            split("m_split", "m_hi", M2)
            p0 = FIRST["out2"][0]
            dve.wait_ge(once("m_split"), 8)
            dve.wait_ge(reloaded, 16)
            evac_stage("out2", lambda k, ps, b: dve.tensor_tensor(two(M2, k), ps, two(XT, k), ALU.add))
            norm("n6")
            for c in range(DC):
                dve.scalar_tensor_tensor(out=SQ2[:, c, :], in0=M2[:, c, :], scalar=col("final", c), in1=R[:],
                                         op0=ALU.mult, op1=ALU.mult).then_inc(once("out_ready"), 1)


def kernel(**inputs):
    import numpy as np
    import concourse.bacc as bacc
    from concourse.bass_utils import run_bass_kernel_spmd

    a = {k: np.asarray(v) for k, v in inputs.items()}
    a = {k: (v[0] if v.ndim > 1 and v.shape[0] == 1 and k != "x" else v) for k, v in a.items()}

    def panel(w):
        n = w.shape[1] // 256
        return w.reshape(8, 128, n, 256).transpose(2, 1, 0, 3).reshape(n, 128, 2048)

    perm = np.concatenate([np.arange(64) + 64 * h for j in range(4) for h in (j, 4 + j)])
    w_in = a["w_in"]
    w_in = np.concatenate([w_in[:, :512][:, perm], w_in[:, 512:]], 1)
    w_out = np.concatenate([a["w_out"][:512][perm], a["w_out"][512:]], 0)
    up = a["w_up"].reshape(1024, 2, 32, 128).transpose(0, 2, 1, 3).reshape(1024, 8192)
    w2 = a["w_in_2"]
    off = np.cumsum([0, 1024, 128, 512, 64, 8, 1024, 1024, 1024, 2048])
    q2, ckv, qi, ki, wi, ga, xr, gr, mg = (w2[:, off[i]:off[i + 1]] for i in range(9))

    def inter(x, y):
        x, y = panel(x), panel(y)
        return np.stack([x, y], 1).reshape(2 * x.shape[0], 128, 2048)

    ups, downs = panel(up), [panel(a["w_down"][1024 * q:1024 * (q + 1)]) for q in range(4)]
    panels = np.concatenate([
        panel(w_in), panel(w_out), ups[0:8], ups[8:16], downs[0], ups[16:24], downs[1], ups[24:32],
        downs[2], downs[3],
        panel(np.concatenate([ckv, ki, ki], 1)), panel(qi), panel(q2), panel(xr), panel(gr), panel(ga),
        inter(mg[:, 1024:], a["w_rnn_proj_2"]), inter(mg[:, :1024], a["w_attn_proj_2"]), panel(a["w_out_2"]),
    ], 0)

    def cols(v):
        return v.reshape(-1, 128).T

    sink = np.broadcast_to(a["swa_sinks"][None, :], (128, 8))
    twice = lambda v: np.concatenate([v, v])
    col = np.concatenate([
        cols(a["attn_pre_g"]), cols(a["swa_out_g"][perm]), cols(a["diff_subln_g"]), cols(a["attn_post_g"]),
        cols(a["ffn_pre_g"]), cols(a["conv_w"][0]), cols(a["conv_w"][1]), cols(a["conv_w"][2]), cols(a["conv_b"]),
        cols(a["ffn_post_g"]), cols(a["norm_gain_2"]), cols(a["b_merge_2"]), cols(a["kv_norm_gain_2"]),
        cols(twice(a["idx_ln_gain_2"])), cols(twice(a["idx_ln_bias_2"])),
        *[cols(a["conv_w_2"][k]) for k in range(4)], cols(a["conv_b_2"]), cols(a["b_rg_a_2"]), cols(a["b_rg_x_2"]),
        cols(a["lru_lambda_2"]), cols(a["final_norm_gain_2"]), sink], 1)
    lamv = np.stack([a[k] for k in ("diff_lq1", "diff_lk1", "diff_lq2", "diff_lk2")])
    lamv = np.broadcast_to(lamv[None], (128, 4, 64))
    rgw = np.zeros((128, 2, 8, 128), np.float32)
    for k, name in enumerate(("w_rg_a_2", "w_rg_x_2")):
        w = a[name].reshape(8, 2, 64, 64)
        for m in range(2):
            rgw[64 * m:64 * m + 64, k, :, 64 * m:64 * m + 64] = w[:, m].transpose(1, 0, 2)
    uk = a["w_uk_2"].reshape(8, 2, 128, 64).transpose(1, 3, 0, 2).reshape(128, 8, 128)
    uv = a["w_uv_2"].transpose(1, 0, 2)
    wis = wi.reshape(8, 128, 8).transpose(1, 0, 2)
    arrays = {"panels": panels, "xT": a["x"].reshape(512, 1024).T, "cols": col, "lamv": lamv, "wi": wis,
              "rgw": rgw, "uk": uk, "uv": uv}
    arrays = {k: np.ascontiguousarray(v) for k, v in arrays.items()}
    nc = bacc.Bacc("TRN2", target_bir_lowering=False, num_devices=1)
    args = [nc.dram_tensor(k, v.shape, mybir.dt.from_np(v.dtype), kind="ExternalInput").ap() for k, v in arrays.items()]
    args.append(nc.dram_tensor("outT", (1024, 512), F32, kind="ExternalOutput").ap())
    build(nc, *args)
    r = run_bass_kernel_spmd(nc, [arrays], core_ids=[0])
    return np.ascontiguousarray(r.results[0]["outT"].T).reshape(1, 512, 1024)
```

```python
from contextlib import ExitStack

import concourse.bass as bass
from concourse import mybir

F32 = mybir.dt.float32
F32R = mybir.dt.float32r
I32 = mybir.dt.int32
ALU = mybir.AluOpType
ACT = mybir.ActivationFunctionType
AX_X = mybir.AxisListType.X

P = 128
S = 512
D = 1024
DC = D // P
NB = S // P
HD = 64
SWA_PAIRS = 4
DIFF_HEADS = 4
MLA_HEADS = 16
IDX_HEADS = 8
TOPK = 128
EPS = 1e-6
SCALE = HD ** -0.5
FAR = 1e30
LAMBDA_INIT = 0.2
SLOPES_1 = sorted([2.0 ** -(i + 1) for i in range(8)] + [2.0 ** -(0.5 * (2 * i + 1)) for i in range(4)], reverse=True)
SLOPES_2 = [2.0 ** (-8.0 * (i + 1) / MLA_HEADS) for i in range(MLA_HEADS)]

STAGES = [("in1", 9), ("out1", 4), ("up0", 8), ("up1", 8), ("dn0", 4), ("up2", 8), ("dn1", 4),
          ("up3", 8), ("dn2", 4), ("dn3", 4), ("in2a", 7), ("xr", 4), ("rg", 8), ("wr", 4),
          ("ga", 4), ("mga", 4), ("ap", 4), ("out2", 4)]
FIRST, NPANELS = {}, 0
for _name, _n in STAGES:
    FIRST[_name] = (NPANELS, _n)
    NPANELS += _n

COLS, NCOLS = {}, 0
for _name, _n in [("attn_pre", 8), ("swa_out", 4), ("subln", 1), ("attn_post", 8), ("ffn_pre", 8),
                  ("cw0", 64), ("cw1", 64), ("cw2", 64), ("cb", 64), ("ffn_post", 8), ("norm2", 8),
                  ("b_merge", 16), ("kv_norm", 1), ("ln_g", 1), ("ln_b", 1), ("rw", 32), ("rb", 8),
                  ("b_rg_a", 8), ("b_rg_x", 8), ("lru", 8), ("final", 8), ("sinks", 8)]:
    COLS[_name] = NCOLS
    NCOLS += _n


class Count:

    def __init__(self, sem):
        self.sem, self.n = sem, 0

    def __call__(self, ins):
        ins.then_inc(self.sem, 1)
        self.n = self.n + 1


def build(nc, panels, xT, cols_in, lamv_in, wi_in, rgw_in, uk_in, uv_in, outT):
    spill = nc.dram_tensor("x2_spill", (P, DC, S), F32, kind="Internal").ap()
    with ExitStack() as ctx:
        KB = 1024
        ARENA0 = 16512 + 32
        arena_used = []

        def at(name, shape, kb, dt=F32):
            size = 4
            for n in shape[1:]:
                size *= n
            assert kb * KB + size <= 207.5 * KB, (name, kb, size)
            arena_used.append((name, kb, size))
            return nc.alloc_sbuf_tensor_at(name, shape, dt, offset=ARENA0 + int(kb * KB))

        def sem(name):
            return ctx.enter_context(nc.semaphore(name))

        XT = at("XT", [P, DC, S], 0)
        XH = at("XH", [P, DC, S], 16, F32R)
        XL = at("XL", [P, DC, S], 32, F32R)
        WH = at("WH", [P, 2, DC, 256], 48, F32R)
        WL = at("WL", [P, 2, DC, 256], 64, F32R)
        RAW = at("RAW", [P, 2, DC * 256], 80)
        PROJ = at("PROJ", [P, 18, S], 96)
        VA = at("VA", [P, NB, P], 132)
        VB = at("VB", [P, DIFF_HEADS, NB, P], 134)
        MIX = at("MIX", [P, DC, S], 142)
        SQ1 = at("SQ1", [P, DC, S], 142)
        DS4 = at("DS4", [P, NB, 256], 158)
        PSW = at("PSW", [P, 2, NB, 256], 162)
        PD = [at(f"PD{k}", [P, 2, S], 162 + 4 * k) for k in range(3)]
        PTW = at("PTW", [P, 2, NB, 256], 170)
        PTD = at("PTD", [P, 2, NB, S], 174)
        MSQ = at("MSQ", [P, DC, S], 96)
        Y1 = at("Y1", [P, DC, S], 142)
        SQY = at("SQY", [P, DC, S], 96)
        AH = at("AH", [P, 2, DC, S], 96, F32R)
        AL = at("AL", [P, 2, DC, S], 128, F32R)
        FA = at("FA", [P, DC, S], 160)
        U = at("U", [P, 2, 2, S], 176)
        C = at("C", [P, 2, 2, S], 184)
        Z = at("Z", [P, 2, S], 192)
        SQF = at("SQF", [P, DC, S], 96)
        QT = at("QT", [P, 8, S], 96)
        CKV = at("CKV", [P, 2, S], 112)
        CKT = at("CKT", [P, NB, P], 116)
        XR = at("XR", [P, 8, S], 118)
        GR = at("GR", [P, 8, S], 134)
        RH = at("RH", [P, 8, S], 118, F32R)
        RL = at("RL", [P, 8, S], 134, F32R)
        GA = at("GA", [P, 8, S], 150)
        MGA = [at(f"MGA{k}", [P, 2, S], kb) for k, kb in enumerate((4, 134, 138, 146))]
        OLO = at("OLO", [P, 8, S], 96, F32R)
        QI = at("QI", [P, 4, S], 150)
        CSQ = at("CSQ", [P, 2, S], 158)
        KC = at("KC", [P, S], 162)
        WIH = at("WIH", [P, DC, 8], 164, F32R)
        WIL = at("WIL", [P, DC, 8], 164.25, F32R)
        WIR = at("WIR", [P, DC, 8], 164.5)
        MD = at("MD", [P, 1152], 166)
        RLU = at("RLU", [P, 2, S], 191)
        XC = at("XC", [P, 2, 2, S], 171)
        RGT = at("RGT", [P, 4, 2, S], 179)
        M2 = at("M2", [P, 8, S], 171)
        SG = at("SG", [P, 2, S], 191)
        RGW = at("RGW", [P, 2, 8, P], 0)
        UK = at("UK", [P, 8, P], 8)
        UV = at("UV", [P, MLA_HEADS, HD], 12)
        PM = [at(f"PM{k}", [P, 2, S], kb) for k, kb in enumerate((118, 122, 0))]
        PTM = at("PTM", [P, 2, NB, S], 126)
        OL = at("OL", [P, 2, S], 142)
        SGA = at("SGA", [P, 2, S], 146)
        QL = at("QL", [P, 2, 2, S], 187)
        SQ2 = at("SQ2", [P, DC, S], 118)
        COL = at("COL", [P, NCOLS], 196)
        EC = at("EC", [P, S], 198)
        IDN = at("IDN", [P, P], 200)
        ONE = at("ONE", [P, P], 200.5)
        R = at("R", [P, S], 201)
        DG = at("DG", [P, NB, P], 203)
        LV = at("LV", [P, 4, HD], 205)
        SM = at("SM", [P, 224], 206)

        PG = ctx.enter_context(nc.psum_tensor("PG", [P, 4, S], F32))
        PX = ctx.enter_context(nc.psum_tensor("PX", [P, 4, S], F32))

        def col(name, k, n=1):
            return COL[:, COLS[name] + k:COLS[name] + k + n] if isinstance(k, int) else \
                COL[:, bass.ds(k + COLS[name], n)]

        SMN = [0]

        def small(n):
            SMN[0] += n
            assert SMN[0] <= 224
            return SM[:, SMN[0] - n:SMN[0]]

        EPST = small(1)
        LAM = small(1)
        LDOT = small(2)
        NEG_SP4 = small(8)
        POS_SP4 = small(8)
        HALF_B = small(16)
        SP = small(24)
        SINK8 = small(8)
        STD = small(20)
        RT = small(20)
        MX = small(4)
        NM = small(8)
        DEN = small(8)
        ES = small(4)
        M8 = small(24)
        WX = small(32)
        NM3 = small(6)
        DEN3 = small(6)
        RTL = small(1)
        WORD = small(1)

        loaded_x = [sem(f"loaded_x{k}") for k in range(4)]
        loaded_lam = sem("loaded_lam")
        loaded_c = sem("loaded_c")
        loaded_b2 = sem("loaded_b2")
        loaded_wi = sem("loaded_wi")
        spilled = sem("spilled")
        reloaded = sem("reloaded")
        stored = sem("stored")
        raw_in = [sem("raw_in0"), sem("raw_in1")]
        w_hi = sem("w_hi")
        w_lo = sem("w_lo")
        panel_done = sem("panel_done")
        evac = sem("evac")
        consts = sem("consts")
        act_step = sem("act_step")
        dve_step = sem("dve_step")
        pe_sig = {}

        def once(name):
            if name not in pe_sig:
                pe_sig[name] = sem(name)
            return pe_sig[name]

        block = ctx.enter_context(nc.Block())

        def pairs(eng, name, step, skip=0):
            p0, n = FIRST[name]
            if n - skip >= 4:
                with eng.Fori(0, (n - skip) // 2) as i:
                    for b in range(2):
                        step(i * 2 + (p0 + skip + b), i * 2 + (skip + b), b, i)
            else:
                for k in range(skip, n - (n - skip) % 2):
                    step(p0 + k, k, (k - skip) % 2, None)
            if (n - skip) % 2:
                step(p0 + n - 1, n - 1, 0, None)

        def xT_chunks(k):
            return xT.rearrange("(c p) n -> p c n", p=P)[:, 2 * k:2 * k + 2, :]

        @block.sync
        def _(sp):
            sp.dma_start(COL[:], cols_in).then_inc(loaded_c, 16)
            sp.dma_start(RAW[:, 0, :], panels[0]).then_inc(raw_in[0], 16)
            for k in range(0, 4, 2):
                sp.dma_start(XT[:, 2 * k:2 * k + 2, :], xT_chunks(k)).then_inc(loaded_x[k], 16)
            sp.dma_start(RAW[:, 1, :], panels[1]).then_inc(raw_in[1], 16)
            sp.dma_start(LV[:], lamv_in).then_inc(loaded_lam, 16)
            with sp.Fori(1, NPANELS // 2) as i:
                for s in range(2):
                    sp.wait_ge(w_lo, i * 2 + (s - 1))
                    sp.dma_start(RAW[:, s, :], panels[bass.ds(i * 2 + s, 1), :, :].rearrange("a p n -> p (a n)"))\
                        .then_inc(raw_in[s], 16)
            for k in range(4):
                sp.wait_ge(once("out_ready"), 2 * k + 2)
                sp.dma_start(outT.rearrange("(c p) n -> p c n", p=P)[:, 2 * k:2 * k + 2, :], SQ2[:, 2 * k:2 * k + 2, :])\
                    .then_inc(stored, 16)
            sp.wait_ge(stored, 64)

        @block.gpsimd
        def _(pool):
            pool.memset(ONE[:], 1.0).then_inc(consts, 1)
            pool.memset(IDN[:], 0.0).then_inc(consts, 1)
            pool.wait_ge(consts, 2)
            pool.affine_select(out=IDN[:], in_=IDN[:], compare_op=ALU.not_equal, fill=1.0, base=0,
                               pattern=[[-1, P]], channel_multiplier=1).then_inc(consts, 1)

            def lo(s, value):
                pool.wait_ge(w_hi, value)
                pool.tensor_tensor(WL[:, s].rearrange("p a b -> p (a b)"), RAW[:, s, :],
                                   WH[:, s].rearrange("p a b -> p (a b)").bitcast(F32), ALU.subtract)\
                    .then_inc(w_lo, 1)

            lo(0, 1)
            lo(1, 2)
            dist_i = PSW[:, 0, 0:2].rearrange("p a b -> p (a b)")
            pool.iota(EC[:].bitcast(I32), pattern=[[-1, S]], base=(NB - 1) * P, channel_multiplier=1).then_inc(consts, 1)
            pool.wait_ge(consts, 4)
            pool.tensor_copy(dist_i, EC[:].bitcast(I32)).then_inc(consts, 1)
            pool.wait_ge(consts, 5)
            pool.affine_select(out=EC[:], in_=dist_i, compare_op=ALU.is_ge, fill=FAR,
                               base=(NB - 1) * P, pattern=[[-1, S]], channel_multiplier=1).then_inc(consts, 1)
            pool.wait_ge(consts, 6)
            for b in range(NB):
                pool.affine_select(out=DS4[:, b, :], in_=EC[:, 2 * P:], compare_op=ALU.is_ge, fill=FAR,
                                   base=-1, pattern=[[1, 256]], channel_multiplier=-1).then_inc(consts, 1)
            pool.wait_ge(consts, 10)
            pool.memset(DS4[:, 0, 0:P], FAR).then_inc(consts, 1)

            with pool.Fori(1, NPANELS // 2) as i:
                for s in range(2):
                    lo(s, i * 2 + (s + 1))

        @block.tensor
        def _(pe):
            def one_panel(p, s, xh=XH, xl=XL, ready=None, mid=None):
                pe.wait_ge(w_lo, p + 1)
                if not (isinstance(p, int) and p < 2):
                    pe.wait_ge(evac, p - 1)
                for m in range(2):
                    ms = slice(m * P, (m + 1) * P)
                    for c in range(DC):
                        if ready is not None and m == 0:
                            pe.wait_ge(ready[0], ready[1] + c + 1)
                        o = PG[:, 2 * s + m, :]
                        pe.matmul(o, WH[:, s, c, ms], xh[:, c, :], start=(c == 0), stop=False)
                        pe.matmul(o, WH[:, s, c, ms], xl[:, c, :], start=False, stop=False)
                        mm = pe.matmul(o, WL[:, s, c, ms], xh[:, c, :], start=False, stop=(c == DC - 1))
                    if m == 0 and mid is not None:
                        mid()
                mm.then_inc(panel_done, 1)

            def gemm(name, xh=XH, xl=XL, ready=None, after={}, mids={}):
                p0, _ = FIRST[name]
                peeled = 1 + max([-1, *after, *mids, 0 if ready else -1, 1 if p0 == 0 else -1])
                for k in range(peeled):
                    one_panel(p0 + k, (p0 + k) % 2, xh, xl, ready if k == 0 else None, mids.get(k))
                    if k in after:
                        after[k]()
                pairs(pe, name, lambda p, k, b, i: one_panel(p, (p0 + peeled + b) % 2, xh, xl), peeled)

            def sums(name, src, c0=0, n=DC):
                for c in range(c0, c0 + n):
                    pe.wait_ge(once(name + "_sq"), c + 1)
                    for b in range(NB):
                        mm = pe.matmul(PX[:, 0, b:b + 1], src[:, c, b * P:(b + 1) * P], ONE[:, 0:1],
                                       start=(c == 0 and b == 0), stop=(c == DC - 1), skip_group_check=True)
                if c0 + n == DC:
                    mm.then_inc(once(name + "_sum"), 1)

            def spread(name, dg, k, bank, done):
                for b in range(NB):
                    mm = pe.matmul(PX[:, bank, b * P:(b + 1) * P], ONE[:], dg[:, k * NB + b, :], start=True, stop=True)
                mm.then_inc(once(done), 1)

            def spread_norm(name):
                pe.wait_ge(once(name + "_diag"), NB)
                spread(name, DG, 0, 1, name + "_bc")

            def gemm_sums(name, norm, src, xh=XH, xl=XL, ready=None):
                gemm(name, xh, xl, ready, after={k: (lambda k=k: sums(norm, src, 2 * k - 2, 2)) for k in (1, 2, 3)})
                sums(norm, src, 6, 2)
                spread_norm(norm)

            def gemm_norm(name, norm, src, ready, more={}):
                gemm(name, ready=(once(ready), 0), after={0: lambda: sums(norm, src), **more},
                     mids={1: lambda: spread_norm(norm)})

            pe.wait_ge(consts, 3)
            gemm_norm("in1", "n1", SQ1, "x1_split")

            pe.wait_ge(evac, FIRST["out1"][0])
            for t, tile in enumerate([5, 14, 15, 16, 17]):
                if t >= 2:
                    pe.wait_ge(once("v_copied"), t - 1)
                for b in range(NB):
                    mm = pe.transpose(PX[:, t % 2, b * P:(b + 1) * P], PROJ[:, tile, b * P:(b + 1) * P], IDN[:])
                mm.then_inc(once("v_turned"), 1)

            def swa_scores(h):
                g, j = divmod(h, SWA_PAIRS)
                rows = slice(g * HD, (g + 1) * HD)
                if h >= 2:
                    pe.wait_ge(once("swa_logits"), h - 1)
                s = h % 2
                for qb in range(NB):
                    q = PROJ[rows, j, qb * P:(qb + 1) * P]
                    o = PG[:, 2 * s + qb // 2, (qb % 2) * 256:(qb % 2) * 256 + 256]
                    if qb == 0:
                        pe.matmul(o[:, 0:P], q, PROJ[rows, 4, 0:P], start=True, stop=True)
                        mm = pe.matmul(o[:, P:], q, PROJ[rows, 4, 0:P], start=True, stop=True)
                    else:
                        mm = pe.matmul(o, q, PROJ[rows, 4, (qb - 1) * P:(qb + 1) * P], start=True, stop=True)
                mm.then_inc(once("swa_s"), 1)

            def swa_turn(h):
                pe.wait_ge(once("swa_probs"), h + 1)
                if h >= 1:
                    pe.wait_ge(once("swa_copied"), h)
                else:
                    pe.wait_ge(once("v_copied"), 5)
                for kb in range(NB):
                    o = PX[:, kb // 2, (kb % 2) * 256:(kb % 2) * 256 + 256]
                    mm = pe.transpose(o[:, 0:P], PSW[:, h % 2, kb, P:256], IDN[:])
                    if kb < NB - 1:
                        mm = pe.transpose(o[:, P:256], PSW[:, h % 2, kb + 1, 0:P], IDN[:])
                mm.then_inc(once("swa_turned"), 1)

            def swa_pv(h):
                g, j = divmod(h, SWA_PAIRS)
                rows = slice(g * HD, (g + 1) * HD)
                pe.wait_ge(once("swa_copied"), h + 1)
                if h >= 2:
                    pe.wait_ge(once("swa_out"), h - 1)
                for kb in range(NB):
                    n = 256 if kb < NB - 1 else P
                    mm = pe.matmul(PX[rows, 2 + h % 2, kb * P:kb * P + n], VA[:, kb, rows], PTW[:, h % 2, kb, 0:n],
                                   start=(kb == 0), stop=(kb == NB - 1), skip_group_check=True)
                mm.then_inc(once("swa_pv"), 1)

            swa_scores(0)
            swa_scores(1)
            for h in range(8):
                swa_turn(h)
                if h + 2 < 8:
                    swa_scores(h + 2)
                swa_pv(h)

            def unit_turn(pre, src, u, qb, maps):
                pe.wait_ge(once(pre + "_probs"), u + 1)
                if u >= 1:
                    pe.wait_ge(once(pre + "_copied"), u)
                for m in range(maps):
                    for kb in range(qb + 1):
                        mm = pe.transpose(PX[:, m, kb * P:(kb + 1) * P], src[u % 3][:, m, kb * P:(kb + 1) * P], IDN[:])
                mm.then_inc(once(pre + "_turned"), 1)

            def diff_scores(u):
                h, qb = divmod(u, NB)
                if u >= 2:
                    pe.wait_ge(once("diff_logits"), u - 1)
                n = (qb + 1) * P
                for m in range(2):
                    rows = slice(m * HD, (m + 1) * HD)
                    mm = pe.matmul(PG[:, 2 * (u % 2) + m, 0:n], PROJ[rows, 6 + h, qb * P:(qb + 1) * P],
                                   PROJ[rows, 10 + h, 0:n], start=True, stop=True)
                mm.then_inc(once("diff_s"), 1)

            def mix_sums(k):
                tiles = range(4) if k == 0 else [3 + k]
                for c in tiles:
                    pe.wait_ge(once("mix_sq"), c + 1)
                    for b in range(NB):
                        mm = pe.matmul(PX[:, 3, k * NB + b:k * NB + b + 1], MSQ[:, c, b * P:(b + 1) * P], ONE[:, 0:1],
                                       start=(c == tiles[0] and b == 0), stop=(c == tiles[-1]), skip_group_check=True)
                mm.then_inc(once("mix_sum"), 1)

            def mix_spread(k):
                pe.wait_ge(once("mix_diag"), NB * (k + 1))
                if k >= 1:
                    pe.wait_ge(once("mix_y"), 3 + k)
                spread("mix", DG, 0, 1, "mix_bc")

            pe.wait_ge(once("swa_logits"), 8)
            diff_scores(0)
            diff_scores(1)
            for u in range(16):
                h, qb = divmod(u, NB)
                if u == 0:
                    pe.wait_ge(once("swa_out"), 8)
                if u + 2 < 16:
                    diff_scores(u + 2)
                unit_turn("diff", PD, u, qb, 1)
                if qb == 2:
                    mix_sums(h)
                if qb == NB - 1:
                    pe.wait_ge(once("diff_copied"), u + 1)
                    if h >= 1:
                        pe.wait_ge(once("diff_out"), h)
                    for kb in range(NB):
                        mm = pe.matmul(PX[:, 2, kb * P:], VB[:, h, kb, :], PTD[:, h % 2, kb, kb * P:],
                                       start=(kb == 0), stop=(kb == NB - 1), skip_group_check=True)
                    mm.then_inc(once("diff_pv"), 1)
                    mix_spread(h)
            mix_sums(4)
            mix_spread(4)
            gemm_sums("out1", "n2", SQY, ready=(once("mix_split"), 0))
            gemm_norm("up0", "n3", SQY, "x2_split")
            gemm("up1")
            for q, nxt in enumerate(["up2", "up3", None, None]):
                pe.wait_ge(once("a_lo"), 8 * (q + 1))
                if q < 3:
                    gemm(f"dn{q}", AH[:, q % 2], AL[:, q % 2])
                if nxt:
                    gemm(nxt)
            gemm_sums("dn3", "n4", SQF, AH[:, 1], AL[:, 1])

            def w_idx():
                pe.wait_ge(once("wi_split"), 2)
                for b in range(NB):
                    for c in range(DC):
                        o = PX[:, 2, b * 8:(b + 1) * 8]
                        tb = slice(b * P, (b + 1) * P)
                        pe.matmul(o, XH[:, c, tb], WIH[:, c, :], start=(c == 0 and b == 0), stop=False, skip_group_check=True)
                        pe.matmul(o, XH[:, c, tb], WIL[:, c, :], start=False, stop=False, skip_group_check=True)
                        mm = pe.matmul(o, XL[:, c, tb], WIH[:, c, :], start=False, stop=(c == DC - 1), skip_group_check=True)
                mm.then_inc(once("wx_ready"), 1)

            gemm_norm("in2a", "n5", SQF, "x3_split", {2: w_idx})

            pe.wait_ge(once("kv_sq"), 1)
            for b in range(NB):
                mm = pe.matmul(PX[:, 0, b:b + 1], CSQ[:, 0, b * P:(b + 1) * P], ONE[:, 0:1],
                               start=(b == 0), stop=True, skip_group_check=True)
            mm.then_inc(once("kv_sum"), 1)
            pe.matmul(PX[:, 3, :], ONE[:], CKV[:, 1, :], start=True, stop=True).then_inc(once("ln_mean"), 1)
            pe.wait_ge(once("kv_diag"), NB)
            spread("kv", DG, 0, 1, "kv_bc")
            pe.wait_ge(once("ln_sq"), 1)
            for b in range(NB):
                mm = pe.matmul(PX[:, 0, b:b + 1], CSQ[:, 1, b * P:(b + 1) * P], ONE[:, 0:1],
                               start=(b == 0), stop=True, skip_group_check=True)
            mm.then_inc(once("ln_sum"), 1)
            pe.wait_ge(once("ln_diag"), NB)
            spread("ln", DG, 0, 2, "ln_bc")
            pe.wait_ge(once("kv_done"), 1)
            for b in range(NB):
                mm = pe.transpose(PX[:, 3, b * P:(b + 1) * P], CKV[:, 0, b * P:(b + 1) * P], IDN[:])
            mm.then_inc(once("kv_turned"), 1)
            pe.wait_ge(once("ki_done"), 1)
            pe.wait_ge(evac, FIRST["xr"][0])

            for u in range(3 * IDX_HEADS):
                qb, j = u // IDX_HEADS + 1, u % IDX_HEADS
                n = (qb + 1) * P
                rows = slice((j % 2) * HD, (j % 2) * HD + HD)
                if u >= 4:
                    pe.wait_ge(once("idx_relu"), u - 3)
                elif u == 3:
                    pe.wait_ge(once("kv_copied"), 1)
                pe.matmul(PG[:, u % 4, 0:n], QI[rows, j // 2, qb * P:(qb + 1) * P], CKV[rows, 1, 0:n],
                          start=True, stop=True).then_inc(once("idx_s"), 1)
            pe.wait_ge(once("idx_relu"), 24)
            gemm("xr")

            p0 = FIRST["rg"][0]
            pe.wait_ge(loaded_b2, 48)
            for t in range(4):
                pe.wait_ge(once("rg_conv"), 2 * t + 2)
                if t >= 1:
                    pe.wait_ge(once("rg_ti"), t)
                for m in range(2):
                    pe.matmul(PX[:, m, :], RGW[:, 0, 2 * t + m, :], XC[:, t % 2, m, :], start=True, stop=True)
                    mm = pe.matmul(PX[:, 2 + m, :], RGW[:, 1, 2 * t + m, :], XC[:, t % 2, m, :], start=True, stop=True)
                mm.then_inc(once("rg_proj"), 1)
                one_panel(p0 + 2 * t, p0 % 2)
                one_panel(p0 + 2 * t + 1, (p0 + 1) % 2)
            gemm("wr", RH, RL, ready=(once("rg_lo"), 0))
            gemm("ga")

            def qlat(g):
                if g >= 1:
                    pe.wait_ge(once("mla_y"), g - 1) if g >= 2 else None
                if g == 0:
                    pe.wait_ge(once("rg_ti"), 4)
                for m in range(2):
                    rows = slice(m * HD, (m + 1) * HD)
                    mm = pe.matmul(PX[:, 2 + m, :], UK[rows, g, :], QT[rows, g, :], start=True, stop=True)
                mm.then_inc(once("mla_ql"), 1)

            def mla_scores(u):
                g, qb = divmod(u, NB)
                pe.wait_ge(once("mla_qlc"), g + 1)
                if u >= 2:
                    pe.wait_ge(once("mla_logits"), u - 1)
                n = (qb + 1) * P
                for m in range(2):
                    mm = pe.matmul(PG[:, 2 * (u % 2) + m, 0:n], QL[:, g % 2, m, qb * P:(qb + 1) * P],
                                   CKV[:, 0, 0:n], start=True, stop=True)
                mm.then_inc(once("mla_s"), 1)

            def mla_y(g):
                pe.wait_ge(once("mla_ol"), g + 1)
                for m in range(2):
                    mm = pe.matmul(PX[m * HD:(m + 1) * HD, 2, :], UV[:, 2 * g + m, :], OL[:, m, :],
                                   start=True, stop=True)
                mm.then_inc(once("mla_yp"), 1)

            pe.wait_ge(evac, FIRST["mga"][0])
            qlat(0)
            mla_scores(0)
            mla_scores(1)
            for u in range(32):
                g, qb = divmod(u, NB)
                if u + 2 < 32:
                    mla_scores(u + 2)
                unit_turn("mla", PM, u, qb, 2)
                if qb == 0:
                    if g >= 1:
                        mla_y(g - 1)
                    if g < 7:
                        if g >= 1:
                            pe.wait_ge(once("mla_y"), g)
                        for m in range(2):
                            rows = slice(m * HD, (m + 1) * HD)
                            mm = pe.matmul(PX[:, 2 + m, :], UK[rows, g + 1, :], QT[rows, g + 1, :], start=True, stop=True)
                        mm.then_inc(once("mla_ql"), 1)
                if qb == NB - 1:
                    pe.wait_ge(once("mla_copied"), u + 1)
                    pe.wait_ge(once("mla_qlc"), min(g + 2, 8))
                    if g == 7:
                        pe.wait_ge(once("mla_y"), 7)
                    for m in range(2):
                        for kb in range(NB):
                            mm = pe.matmul(PX[:, 2 + m, kb * P:], CKT[:, kb, :], PTM[:, m, kb, kb * P:],
                                           start=(kb == 0), stop=(kb == NB - 1), skip_group_check=True)
                    mm.then_inc(once("mla_pv"), 1)
            mla_y(7)
            gemm("mga")
            gemm("ap", RH, OLO, ready=(once("o_split"), 0))
            gemm_sums("out2", "n6", GA, ready=(once("m_split"), 0))

        @block.scalar
        def _(act):
            step_ = Count(act_step)

            def hi(p, s, turn):
                act.wait_ge(raw_in[s], turn * 16 + 16)
                act.activation(WH[:, s].rearrange("p a b -> p (a b)"), RAW[:, s, :], ACT.Copy).then_inc(w_hi, 1)

            def hi_ahead(p, p0b):
                s = p0b % 2
                act.wait_ge(panel_done, p + 1)
                if isinstance(p, int):
                    if p + 2 < NPANELS:
                        hi(p + 2, s, (p + 2) // 2)
                else:
                    raise AssertionError

            def hi_stage(name, skip=0):
                p0, n = FIRST[name]
                q0 = p0 + skip
                with act.Fori(0, (n - skip) // 2) as i:
                    for b in range(2):
                        act.wait_ge(panel_done, i * 2 + (q0 + b + 1))
                        hi(None, (q0 + b) % 2, i + (q0 + b + 2) // 2)
                if (n - skip) % 2:
                    hi_ahead(p0 + n - 1, p0 + n - 1)

            def hi_squares(name, norm, dst, src):
                p0 = FIRST[name][0]
                for k in range(4):
                    hi_ahead(p0 + k, p0 + k)
                    act.wait_ge(evac, p0 + k + 1)
                    for c in (2 * k, 2 * k + 1):
                        act.activation(dst[:, c, :], src[:, c, :], ACT.Square).then_inc(once(norm + "_sq"), 1)

            def squares(name, dst, src, n=DC, wait=None):
                for c in range(n):
                    if wait is not None:
                        act.wait_ge(once(wait), c + 1)
                    act.activation(dst[:, c, :], src[:, c, :], ACT.Square).then_inc(once(name + "_sq"), 1)

            def std(name, width, scale, k=0, n=NB, bank=0):
                act.wait_ge(once(name + "_sum"), 1)
                act.activation(STD[:, k:k + n], PX[:, bank, k:k + n], ACT.Sqrt, bias=EPST, scale=1.0 / width)\
                    .then_inc(once(name + "_std"), 1)

            def split(name, ready, src, cname=None, dst=XH):
                for c in range(DC):
                    if ready is not None:
                        act.wait_ge(once(ready), c + 1)
                    if cname is None:
                        act.activation(dst[:, c, :], src[:, c, :], ACT.Copy).then_inc(once(name), 1)
                    else:
                        act.activation(dst[:, c, :], src[:, c, :], ACT.Copy, scale=col(cname, c)).then_inc(once(name), 1)

            for k in (1, 3):
                act.dma_start(XT[:, 2 * k:2 * k + 2, :], xT_chunks(k)).then_inc(loaded_x[k], 16)
            hi(0, 0, 0)
            act.wait_ge(loaded_c, 16)
            for k in range(4):
                act.wait_ge(loaded_x[k], 16)
                for c in (2 * k, 2 * k + 1):
                    act.activation(XH[:, c, :], XT[:, c, :], ACT.Copy, scale=col("attn_pre", c)).then_inc(once("x1_hi"), 1)
            hi(1, 1, 0)
            squares("n1", SQ1, XT)
            act.wait_ge(once("lam_dot"), 2)
            act.activation(LDOT, LDOT, ACT.Exp).then_inc(once("lam_exp"), 1)
            act.wait_ge(once("lru_abs"), 1)
            act.activation(SP[:, 8:16], SP[:, 0:8], ACT.Exp, scale=-1.0).then_inc(once("lru_exp"), 1)
            act.wait_ge(once("eps_set"), 1)
            std("n1", D, D)
            hi_stage("in1")

            for t in range(5):
                act.wait_ge(once("v_turned"), t + 1)
                dst = VA[:].rearrange("p a b -> p (a b)") if t == 0 else VB[:, t - 1].rearrange("p a b -> p (a b)")
                act.activation(dst, PX[:, t % 2, :], ACT.Copy).then_inc(once("v_copied"), 1)

            def swa_exp(h):
                act.wait_ge(once("swa_negmax"), h + 1)
                s = h % 2
                for qb in range(NB):
                    act.activation(PSW[:, s, qb, :], PSW[:, s, qb, :], ACT.Exp, bias=NM[:, 4 * s + qb:4 * s + qb + 1],
                                   scale=SCALE, accum_out=DEN[:, 4 * s + qb:4 * s + qb + 1])
                if h >= 1:
                    act.wait_ge(once("swa_den"), h)
                act.activation(ES, NM[:, 4 * s:4 * s + 4], ACT.Exp, bias=col("sinks", h)).then_inc(once("swa_exp"), 1)

            def swa_copy(h):
                act.wait_ge(once("swa_turned"), h + 1)
                if h >= 2:
                    act.wait_ge(once("swa_pv"), h - 1)
                s = h % 2
                act.activation(PTW[:, s, 0:2, :], PX[:, 0, :].rearrange("p (a b) -> p a b", b=256), ACT.Copy)
                act.activation(PTW[:, s, 2:4, :].rearrange("p a b -> p (a b)")[:, 0:384], PX[:, 1, 0:384], ACT.Copy)\
                    .then_inc(once("swa_copied"), 1)

            for h in range(8):
                swa_exp(h)
                if h >= 1:
                    swa_copy(h - 1)
            swa_copy(7)

            def unit_exp(pre, buf, u, qb):
                n = (qb + 1) * P
                act.wait_ge(once(pre + "_negmax"), u + 1)
                s = u % 3
                for m in range(2):
                    ins = act.activation(buf[s][:, m, 0:n], buf[s][:, m, 0:n], ACT.Exp,
                                         bias=NM3[:, 2 * s + m:2 * s + m + 1], scale=SCALE,
                                         accum_out=DEN3[:, 2 * s + m:2 * s + m + 1])
                ins.then_inc(once(pre + "_exp"), 1)

            def unit_copy(pre, dst, u, qb, maps):
                act.wait_ge(once(pre + "_turned"), u + 1)
                for m in range(maps):
                    ins = act.activation(dst(m, qb), PX[:, m, 0:(qb + 1) * P].rearrange("p (a b) -> p a b", b=P), ACT.Copy)
                ins.then_inc(once(pre + "_copied"), 1)

            def diff_dst(h):
                return lambda m, qb: PTD[:, h % 2, 0:qb + 1, qb * P:(qb + 1) * P]

            def mix_square(k):
                if k >= 1:
                    act.wait_ge(once("diff_out"), k)
                for c in range(4) if k == 0 else [3 + k]:
                    act.activation(MSQ[:, c, :], MIX[:, c, :], ACT.Square).then_inc(once("mix_sq"), 1)

            def mix_std(k):
                act.wait_ge(once("mix_sum"), k + 1)
                act.activation(STD[:, 4 * k:4 * k + 4], PX[:, 3, 4 * k:4 * k + 4], ACT.Sqrt, bias=EPST,
                               scale=1.0 / (512 if k == 0 else 128)).then_inc(once("mix_std"), 1)

            def mix_hi(k):
                for c in range(4) if k == 0 else [3 + k]:
                    act.wait_ge(once("mix_y"), c + 1)
                    act.activation(XH[:, c, :], MIX[:, c, :], ACT.Copy).then_inc(once("mix_hi"), 1)

            for u in range(16):
                h, qb = divmod(u, NB)
                unit_exp("diff", PD, u, qb)
                if u >= 1:
                    hp, qp = divmod(u - 1, NB)
                    if hp >= 2 and qp == 0:
                        act.wait_ge(once("diff_pv"), hp - 1)
                    if u - 1 == 0:
                        act.wait_ge(once("swa_pv"), 8)
                    unit_copy("diff", diff_dst(hp), u - 1, qp, 1)
                if qb == 1:
                    if h >= 1:
                        mix_hi(h - 1)
                    else:
                        act.wait_ge(once("swa_out"), 8)
                    mix_square(h)
                if qb == 3:
                    mix_std(h)
            unit_copy("diff", diff_dst(3), 15, 3, 1)
            mix_hi(3)
            mix_square(4)
            mix_std(4)
            mix_hi(4)
            hi_squares("out1", "n2", SQY, Y1)
            std("n2", D, D)
            split("x2_hi", "x2_new", XT, "ffn_pre")
            squares("n3", SQY, XT)
            std("n3", D, D)

            def up(q):
                p0 = FIRST[f"up{q}"][0]

                def conv0(c, k, b, p):
                    act.wait_ge(evac, p + 1)
                    for m in range(2):
                        ins = act.activation(C[:, b, m, :], U[:, b, m, :], ACT.Identity,
                                             bias=col("cb", k + 32 * m), scale=col("cw2", k + 32 * m))
                    ins.then_inc(once("conv0"), 1)

                def a_hi(c, n, b):
                    act.wait_ge(once("a_ready"), n)
                    act.activation(AH[:, q % 2, c, :] if isinstance(c, int) else
                                   AH[:, q % 2, bass.ds(c, 1), :].rearrange("p a n -> p (a n)"),
                                   Z[:, b, :], ACT.Copy).then_inc(once("a_hi"), 1)

                def tanh(n, b):
                    act.wait_ge(once("inner"), n)
                    act.activation(Z[:, b, :], Z[:, b, :], ACT.Tanh, scale=0.7978845608028654).then_inc(once("tanh"), 1)

                def panel(i, b, first):
                    p = i * 2 + (p0 + b)
                    c = i * 2 + b
                    n = c + 8 * q
                    act.wait_ge(panel_done, p + 1)
                    hi(None, (p0 + b) % 2, i + (p0 + b + 2) // 2)
                    conv0(c, n, b, p)
                    if not first:
                        a_hi(c - 1, n, 1 - b)
                    tanh(n + 1, b)

                panel(0, 0, True)
                panel(0, 1, False)
                with act.Fori(1, 4) as i:
                    panel(i, 0, False)
                    panel(i, 1, False)
                a_hi(7, 8 * q + 8, 1)

            up(0)
            up(1)
            hi_stage("dn0")
            up(2)
            hi_stage("dn1")
            up(3)
            hi_stage("dn2")
            hi_squares("dn3", "n4", SQF, FA)
            std("n4", D, D)
            split("x3_hi", "x3_new", XT, "norm2")
            act.dma_start(WIR[:], wi_in).then_inc(loaded_wi, 16)
            act.dma_start(spill, XT[:]).then_inc(spilled, 16)
            squares("n5", SQF, XT)
            std("n5", D, D)
            act.wait_ge(loaded_wi, 16)
            act.activation(WIH[:], WIR[:], ACT.Copy).then_inc(once("wi_hi"), 1)
            hi_stage("in2a")
            act.wait_ge(once("x3_split"), 8)
            act.wait_ge(spilled, 16)
            act.dma_start(RGW[:], rgw_in).then_inc(loaded_b2, 16)
            act.dma_start(UK[:], uk_in).then_inc(loaded_b2, 16)
            act.dma_start(UV[:], uv_in).then_inc(loaded_b2, 16)
            act.wait_ge(evac, FIRST["xr"][0])
            act.activation(CSQ[:, 0, :], CKV[:, 0, :], ACT.Square).then_inc(once("kv_sq"), 1)
            std("kv", 128, 128)
            act.wait_ge(once("ln_x"), 1)
            act.activation(CSQ[:, 1, :], KC[:], ACT.Square).then_inc(once("ln_sq"), 1)
            std("ln", 128, 128)
            act.wait_ge(once("kv_turned"), 1)
            act.activation(CKT[:].rearrange("p a b -> p (a b)"), PX[:, 3, :], ACT.Copy).then_inc(once("kv_copied"), 1)
            for u in range(24):
                n = (u // 8 + 2) * P
                act.wait_ge(once("idx_s"), u + 1)
                if u >= 2:
                    act.wait_ge(once("idx_acc"), u - 1)
                act.activation(RLU[:, u % 2, 0:n], PG[:, u % 4, 0:n], ACT.Relu).then_inc(once("idx_relu"), 1)

            def conv0(t):
                if t >= 2:
                    act.wait_ge(once("rg_ix"), t - 1)
                for m in range(2):
                    act.activation(XC[:, t % 2, m, :], XR[:, 2 * t + m, :], ACT.Identity, bias=col("rb", 2 * t + m),
                                   scale=col("rw", 24 + 2 * t + m)).then_inc(once("rg_conv0"), 1)

            def y_hi(t):
                act.wait_ge(once("rg_y"), t + 1)
                act.activation(RH[:, 2 * t:2 * t + 2, :], RGT[:, 1], ACT.Copy).then_inc(once("rg_hi"), 1)

            p0 = FIRST["xr"][0]
            for t in range(4):
                hi_ahead(p0 + t, p0 + t)
                if t == 3:
                    act.wait_ge(evac, p0 + 3)
                    conv0(0)
            p0 = FIRST["rg"][0]
            for t in range(4):
                r_, i_, a_, m_ = (RGT[:, k] for k in range(4))
                if t >= 1:
                    y_hi(t - 1)
                if t < 3:
                    act.wait_ge(evac, FIRST["xr"][0] + t + 2)
                    conv0(t + 1)
                act.wait_ge(once("rg_proj"), t + 1)
                for m in range(2):
                    step_(act.activation(r_[:, m, :], PX[:, m, :], ACT.Tanh, bias=HALF_B[:, 2 * t + m:2 * t + m + 1], scale=0.5))
                if t >= 1:
                    act.wait_ge(once("rg_lo"), 2 * t)
                for m in range(2):
                    ins = act.activation(i_[:, m, :], PX[:, 2 + m, :], ACT.Tanh,
                                         bias=HALF_B[:, 8 + 2 * t + m:8 + 2 * t + m + 1], scale=0.5)
                ins.then_inc(once("rg_ti"), 1)
                act.wait_ge(act_step, step_.n)
                for m in range(2):
                    c = slice(2 * t + m, 2 * t + m + 1)
                    ins = act.activation(a_[:, m, :], r_[:, m, :], ACT.Exp, bias=NEG_SP4[:, c], scale=NEG_SP4[:, c])
                ins.then_inc(once("rg_a"), 1)
                act.wait_ge(once("rg_a"), t + 1)
                for m in range(2):
                    c = slice(2 * t + m, 2 * t + m + 1)
                    ins = act.activation(r_[:, m, :], r_[:, m, :], ACT.Tanh, bias=POS_SP4[:, c], scale=POS_SP4[:, c])
                ins.then_inc(once("rg_tanh"), 1)
                act.wait_ge(once("rg_m"), t + 1)
                act.activation(m_, m_, ACT.Sqrt).then_inc(once("rg_sqrt"), 1)
                hi_ahead(p0 + 2 * t, p0)
                act.wait_ge(evac, p0 + 2 * t + 1)
                act.activation(r_, GR[:, 2 * t:2 * t + 2, :], ACT.Tanh, scale=0.5).then_inc(once("rg_tg"), 1)
                hi_ahead(p0 + 2 * t + 1, p0 + 1)
            y_hi(3)

            p0 = FIRST["wr"][0]
            act.wait_ge(evac, p0)
            for t in range(4):
                for m in range(2):
                    ins = act.activation(GA[:, 2 * t + m, :], GA[:, 2 * t + m, :], ACT.Sigmoid, bias=col("b_merge", 8 + 2 * t + m))
                ins.then_inc(once("mr_sg"), 1)
                hi_ahead(p0 + t, p0 + t)
            p0 = FIRST["ga"][0]
            for t in range(4):
                hi_ahead(p0 + t, p0 + t)
                act.wait_ge(evac, p0 + t + 1)
                if t >= 1:
                    act.wait_ge(once("silu_ga"), t)
                act.activation(SGA[:], GA[:, 2 * t:2 * t + 2, :], ACT.Sigmoid).then_inc(once("sig_ga"), 1)

            def ql_copy(g):
                act.wait_ge(once("mla_ql"), g + 1)
                for m in range(2):
                    ins = act.activation(QL[:, g % 2, m, :], PX[:, 2 + m, :], ACT.Copy)
                ins.then_inc(once("mla_qlc"), 1)

            ql_copy(0)
            for u in range(32):
                g, qb = divmod(u, NB)
                unit_exp("mla", PM, u, qb)
                if u >= 1:
                    gp, qp = divmod(u - 1, NB)
                    if qp == 0 and gp >= 1:
                        act.wait_ge(once("mla_pv"), gp)
                    unit_copy("mla", lambda m, q: PTM[:, m, 0:q + 1, q * P:(q + 1) * P], u - 1, qp, 2)
                if qb == 1 and g < 7:
                    ql_copy(g + 1)
            unit_copy("mla", lambda m, q: PTM[:, m, 0:q + 1, q * P:(q + 1) * P], 31, 3, 2)
            act.wait_ge(once("mla_y"), 8)
            split("o_hi", None, GA, None, RH)
            p0 = FIRST["mga"][0]
            for t in range(4):
                hi_ahead(p0 + t, p0 + t)
                act.wait_ge(evac, p0 + t + 1)
                for m in range(2):
                    ins = act.activation(MGA[t][:, m, :], MGA[t][:, m, :], ACT.Sigmoid, bias=col("b_merge", 2 * t + m))
                ins.then_inc(once("ma_sg"), 1)
            hi_stage("ap")
            act.wait_ge(evac, FIRST["out2"][0])
            act.dma_start(XT[:], spill).then_inc(reloaded, 16)
            split("m_hi", "m_ready", M2)
            hi_squares("out2", "n6", GA, M2)
            std("n6", D, D)

        @block.vector
        def _(dve):
            step_ = Count(dve_step)

            def link(ins):
                step_(ins)
                dve.wait_ge(dve_step, step_.n)

            def diags(name, dg, k0, n, scale=None):
                for k in range(k0, k0 + n):
                    dve.tensor_scalar(dg[:, k, :], IDN[:], RT[:, k:k + 1], scale, ALU.mult,
                                      *([ALU.mult] if scale is not None else [])).then_inc(once(name + "_diag"), 1)

            def recip_r(name, k=0, n=NB, count=1):
                dve.wait_ge(once(name + "_std"), count)
                link(dve.reciprocal(RT[:, k:k + n], STD[:, k:k + n]))

            def norm(name, dst=R):
                recip_r(name)
                diags(name, DG, 0, NB)
                dve.wait_ge(once(name + "_bc"), 1)
                link(dve.tensor_copy(dst[:], PX[:, 1, :]))

            def split(name, hi_name, src, cname=None, dh=XH, dl=XL):
                for c in range(DC):
                    dve.wait_ge(once(hi_name), c + 1)
                    if cname is None:
                        ins = dve.tensor_tensor(dl[:, c, :], src[:, c, :], dh[:, c, :].bitcast(F32), ALU.subtract)
                    else:
                        ins = dve.scalar_tensor_tensor(out=dl[:, c, :], in0=src[:, c, :], scalar=col(cname, c),
                                                       in1=dh[:, c, :].bitcast(F32), op0=ALU.mult, op1=ALU.subtract)
                    ins.then_inc(once(name), 1)

            def psum_of(p0b):
                s = p0b % 2
                return PG[:, 2 * s:2 * s + 2, :]

            def evac_stage(name, out, p0=None):
                p0, n = FIRST[name]

                def step(p, k, b, i):
                    dve.wait_ge(panel_done, p + 1)
                    out(k, psum_of(p0 + b), b).then_inc(evac, 1)

                pairs(dve, name, step)

            def two(buf, k, off=0):
                if isinstance(k, int):
                    return buf[:, 2 * k + off:2 * k + off + 2, :]
                return buf[:, bass.ds(k * 2 + off, 2), :]

            def rr():
                return R[:].rearrange("p (a n) -> p a n", a=1).broadcast_to([P, 2, S])

            dve.memset(EPST, EPS).then_inc(once("eps_set"), 1)
            dve.wait_ge(loaded_c, 16)
            split("x1_split", "x1_hi", XT, "attn_pre")
            dve.wait_ge(loaded_lam, 16)
            for k in range(2):
                dve.tensor_tensor_reduce(out=R[:, k * HD:(k + 1) * HD], in0=LV[:, 2 * k, :], in1=LV[:, 2 * k + 1, :], scale=1.0,
                                         scalar=0.0, op0=ALU.mult, op1=ALU.add, accum_out=LDOT[:, k:k + 1])\
                    .then_inc(once("lam_dot"), 1)
            lru = col("lru", 0, 8)
            link(dve.tensor_scalar(SP[:, 0:8], lru, -1.0, None, ALU.mult))
            dve.tensor_tensor(SP[:, 0:8], SP[:, 0:8], lru, ALU.max).then_inc(once("lru_abs"), 1)
            dve.tensor_scalar(SINK8, col("sinks", 0, 8), 1.0 / SCALE, None, ALU.mult).then_inc(dve_step, 1)
            step_.n += 1
            dve.wait_ge(once("lam_exp"), 1)
            link(dve.tensor_scalar(LDOT[:, 0:1], LDOT[:, 0:1], LAMBDA_INIT, None, ALU.add))
            link(dve.tensor_tensor(LAM, LDOT[:, 0:1], LDOT[:, 1:2], ALU.subtract))
            dve.wait_ge(once("lru_exp"), 1)
            link(dve.tensor_scalar(SP[:, 0:8], SP[:, 8:16], 2.0, None, ALU.add))
            link(dve.reciprocal(SP[:, 0:8], SP[:, 0:8]))
            link(dve.tensor_tensor(SP[:, 0:8], SP[:, 0:8], SP[:, 8:16], ALU.mult))
            link(dve.tensor_tensor(SP[:, 8:16], SP[:, 0:8], SP[:, 0:8], ALU.mult))
            link(dve.tensor_scalar(SP[:, 16:24], SP[:, 8:16], 1.0 / 17, 1.0 / 15, ALU.mult, ALU.add))
            for d in (13, 11, 9, 7, 5, 3, 1):
                link(dve.tensor_tensor(SP[:, 16:24], SP[:, 16:24], SP[:, 8:16], ALU.mult))
                link(dve.tensor_scalar(SP[:, 16:24], SP[:, 16:24], 1.0 / d, None, ALU.add))
            link(dve.tensor_tensor(SP[:, 16:24], SP[:, 16:24], SP[:, 0:8], ALU.mult))
            link(dve.tensor_scalar(SP[:, 8:16], lru, -1.0, 0.0, ALU.mult, ALU.max))
            link(dve.scalar_tensor_tensor(out=SP[:, 0:8], in0=SP[:, 16:24], scalar=2.0, in1=SP[:, 8:16],
                                          op0=ALU.mult, op1=ALU.add))
            step_(dve.tensor_scalar(NEG_SP4, SP[:, 0:8], -4.0, None, ALU.mult))
            step_(dve.tensor_scalar(HALF_B, COL[:, COLS["b_rg_a"]:COLS["b_rg_a"] + 16], 0.5, None, ALU.mult))
            link(dve.tensor_scalar(POS_SP4, SP[:, 0:8], 4.0, None, ALU.mult))
            dve.wait_ge(consts, 3)
            norm("n1")

            evac_stage("in1", lambda k, ps, b: dve.tensor_tensor(two(PROJ, k), ps, rr(), ALU.mult))

            def swa_logits(h):
                s = h % 2
                dve.wait_ge(once("swa_s"), h + 1)
                if h >= 2:
                    dve.wait_ge(once("swa_turned"), h - 1)
                dve.scalar_tensor_tensor(out=PSW[:, s].rearrange("p a b -> p (a b)"), in0=DS4[:].rearrange("p a b -> p (a b)"),
                                         scalar=-SLOPES_1[h] / SCALE,
                                         in1=PG[:, 2 * s:2 * s + 2, :].rearrange("p a b -> p (a b)"),
                                         op0=ALU.mult, op1=ALU.add).then_inc(once("swa_logits"), 1)
                dve.wait_ge(once("swa_logits"), h + 1)
                link(dve.tensor_reduce(MX, PSW[:, s], AX_X, ALU.max))
                dve.tensor_scalar(NM[:, 4 * s:4 * s + 4], MX, SINK8[:, h:h + 1], -SCALE, ALU.max, ALU.mult)\
                    .then_inc(once("swa_negmax"), 1)

            def swa_probs(h):
                s = h % 2
                den = DEN[:, 4 * s:4 * s + 4]
                dve.wait_ge(once("swa_exp"), h + 1)
                dve.tensor_tensor(den, den, ES, ALU.add).then_inc(once("swa_den"), 1)
                dve.wait_ge(once("swa_den"), h + 1)
                link(dve.reciprocal(den, den))
                for qb in range(NB):
                    ins = dve.tensor_scalar(PSW[:, s, qb, :], PSW[:, s, qb, :], den[:, qb:qb + 1], None, ALU.mult)
                ins.then_inc(once("swa_probs"), 1)

            def swa_out(h):
                g, j = divmod(h, SWA_PAIRS)
                rows = slice(g * HD, (g + 1) * HD)
                dve.wait_ge(once("swa_pv"), h + 1)
                dve.tensor_copy(MIX[rows, j, :], PX[rows, 2 + h % 2, :]).then_inc(once("swa_out"), 1)

            dve.wait_ge(consts, 11)
            swa_logits(0)
            for h in range(8):
                if h + 1 < 8:
                    swa_logits(h + 1)
                swa_probs(h)
                if h >= 1:
                    swa_out(h - 1)
            swa_out(7)

            def unit_logits(pre, buf, u, qb, dist, slopes):
                s, n = u % 3, (qb + 1) * P
                dve.wait_ge(once(pre + "_s"), u + 1)
                if u >= 3:
                    dve.wait_ge(once(pre + "_turned"), u - 2)
                for m in range(2):
                    ins = dve.scalar_tensor_tensor(out=buf[s][:, m, 0:n], in0=dist, scalar=-slopes[m] / SCALE,
                                                   in1=PG[:, 2 * (u % 2) + m, 0:n], op0=ALU.mult, op1=ALU.add)
                ins.then_inc(once(pre + "_logits"), 1)
                dve.wait_ge(once(pre + "_logits"), u + 1)
                link(dve.tensor_reduce(MX[:, 0:2], buf[s][:, :, 0:n], AX_X, ALU.max))
                dve.tensor_scalar(NM3[:, 2 * s:2 * s + 2], MX[:, 0:2], -SCALE, None, ALU.mult).then_inc(once(pre + "_negmax"), 1)

            def diff_probs(u, qb):
                s, n = u % 3, (qb + 1) * P
                den = DEN3[:, 2 * s:2 * s + 2]
                dve.wait_ge(once("diff_exp"), u + 1)
                link(dve.reciprocal(den, den))
                link(dve.tensor_scalar(RTL, den[:, 1:2], LAM, None, ALU.mult))
                link(dve.tensor_scalar(PD[s][:, 1, 0:n], PD[s][:, 1, 0:n], RTL, None, ALU.mult))
                dve.scalar_tensor_tensor(out=PD[s][:, 0, 0:n], in0=PD[s][:, 0, 0:n], scalar=den[:, 0:1],
                                         in1=PD[s][:, 1, 0:n], op0=ALU.mult, op1=ALU.subtract).then_inc(once("diff_probs"), 1)

            def diff_logits(u):
                h, qb = divmod(u, NB)
                sl = SLOPES_1[8 + h]
                unit_logits("diff", PD, u, qb, EC[:, (3 - qb) * P:], [sl, sl])

            def mix_diags(k):
                dve.wait_ge(once("mix_std"), k + 1)
                link(dve.reciprocal(RT[:, 4 * k:4 * k + 4], STD[:, 4 * k:4 * k + 4]))
                if k >= 1:
                    dve.wait_ge(once("mix_bc"), k)
                for b in range(NB):
                    dve.tensor_scalar(DG[:, b, :], IDN[:], RT[:, 4 * k + b:4 * k + b + 1],
                                      1.0 if k == 0 else 1.0 - LAMBDA_INIT, ALU.mult, ALU.mult).then_inc(once("mix_diag"), 1)

            def mix_scale(k):
                dve.wait_ge(once("mix_bc"), k + 1)
                for c in range(4) if k == 0 else [3 + k]:
                    dve.scalar_tensor_tensor(out=MIX[:, c, :], in0=MIX[:, c, :],
                                             scalar=col("swa_out", c) if k == 0 else col("subln", 0),
                                             in1=PX[:, 1, :], op0=ALU.mult, op1=ALU.mult).then_inc(once("mix_y"), 1)

            def mix_lo(k):
                for c in range(4) if k == 0 else [3 + k]:
                    dve.wait_ge(once("mix_hi"), c + 1)
                    dve.tensor_tensor(XL[:, c, :], MIX[:, c, :], XH[:, c, :].bitcast(F32), ALU.subtract)\
                        .then_inc(once("mix_split"), 1)

            def diff_out(h):
                dve.wait_ge(once("diff_pv"), h + 1)
                dve.tensor_copy(MIX[:, 4 + h, :], PX[:, 2, :]).then_inc(once("diff_out"), 1)

            diff_logits(0)
            for u in range(16):
                h, qb = divmod(u, NB)
                if u + 1 < 16:
                    diff_logits(u + 1)
                diff_probs(u, qb)
                if h >= 1 and qb == 0:
                    diff_out(h - 1)
                    mix_scale(h - 1)
                if h >= 1 and qb == 1:
                    mix_lo(h - 1)
                if qb == 3:
                    mix_diags(h)
            diff_out(3)
            mix_scale(3)
            mix_lo(3)
            mix_diags(4)
            mix_scale(4)
            mix_lo(4)
            evac_stage("out1", lambda k, ps, b: dve.tensor_scalar(two(Y1, k), ps, 1.0, None, ALU.mult))

            def post(name, y, cname, new, hi_name, lo_name, gain):
                recip_r(name)
                diags(name, DG, 0, NB)
                dve.wait_ge(once(name + "_bc"), 1)
                base = step_.n
                for c in range(DC + 3):
                    if c < DC:
                        step_(dve.scalar_tensor_tensor(out=y[:, c, :], in0=y[:, c, :], scalar=col(cname, c),
                                                       in1=PX[:, 1, :], op0=ALU.mult, op1=ALU.mult))
                    if 1 <= c <= DC:
                        dve.wait_ge(dve_step, base + c)
                        dve.tensor_tensor(XT[:, c - 1, :], XT[:, c - 1, :], y[:, c - 1, :], ALU.add).then_inc(once(new), 1)
                    if c >= 3:
                        k = c - 3
                        dve.wait_ge(once(hi_name), k + 1)
                        dve.scalar_tensor_tensor(out=XL[:, k, :], in0=XT[:, k, :], scalar=col(gain, k),
                                                 in1=XH[:, k, :].bitcast(F32), op0=ALU.mult, op1=ALU.subtract)\
                            .then_inc(once(lo_name), 1)

            post("n2", Y1, "attn_post", "x2_new", "x2_hi", "x2_split", "ffn_pre")
            norm("n3")

            def up(q):
                p0 = FIRST[f"up{q}"][0]

                def one(buf, c):
                    return buf[:, q % 2, c, :] if isinstance(c, int) else \
                        buf[:, q % 2, bass.ds(c, 1), :].rearrange("p a n -> p (a n)")

                def a_mult(n, b):
                    dve.wait_ge(once("tanh"), n)
                    link(dve.scalar_tensor_tensor(out=Z[:, b, :], in0=Z[:, b, :], scalar=1.0, in1=C[:, b, 0, :],
                                                  op0=ALU.add, op1=ALU.mult))
                    dve.scalar_tensor_tensor(out=Z[:, b, :], in0=Z[:, b, :], scalar=0.5, in1=C[:, b, 1, :],
                                             op0=ALU.mult, op1=ALU.mult).then_inc(once("a_ready"), 1)

                def a_lo(c, n, b):
                    dve.wait_ge(once("a_hi"), n)
                    dve.tensor_tensor(one(AL, c), Z[:, b, :], one(AH, c).bitcast(F32), ALU.subtract)\
                        .then_inc(once("a_lo"), 1)

                def panel(i, b, first):
                    p = i * 2 + (p0 + b)
                    c = i * 2 + b
                    n = c + 8 * q
                    dve.wait_ge(panel_done, p + 1)
                    dve.tensor_tensor(U[:, b], psum_of(p0 + b), rr(), ALU.mult).then_inc(evac, 1)
                    if not first:
                        a_mult(n, 1 - b)
                    dve.wait_ge(evac, p + 1)
                    dve.wait_ge(once("conv0"), n + 1)
                    for m in range(2):
                        step_(dve.scalar_tensor_tensor(out=C[:, b, m, 1:], in0=U[:, b, m, 0:S - 1], scalar=col("cw1", n + 32 * m),
                                                       in1=C[:, b, m, 1:], op0=ALU.mult, op1=ALU.add))
                    dve.wait_ge(dve_step, step_.n)
                    for m in range(2):
                        step_(dve.scalar_tensor_tensor(out=C[:, b, m, 2:], in0=U[:, b, m, 0:S - 2], scalar=col("cw0", n + 32 * m),
                                                       in1=C[:, b, m, 2:], op0=ALU.mult, op1=ALU.add))
                    dve.wait_ge(dve_step, step_.n)
                    link(dve.scalar_tensor_tensor(out=Z[:, b, :], in0=C[:, b, 0, :], scalar=0.044715, in1=C[:, b, 0, :],
                                                  op0=ALU.mult, op1=ALU.mult))
                    dve.scalar_tensor_tensor(out=Z[:, b, :], in0=Z[:, b, :], scalar=1.0, in1=C[:, b, 0, :],
                                             op0=ALU.add, op1=ALU.mult).then_inc(once("inner"), 1)
                    if not first:
                        a_lo(c - 1, n, 1 - b)

                panel(0, 0, True)
                panel(0, 1, False)
                base, per = step_.n, 12
                with dve.Fori(1, 4) as i:
                    step_.n = i * per + (base - per)
                    panel(i, 0, False)
                    panel(i, 1, False)
                step_.n = base + 3 * per
                a_mult(8 * q + 8, 1)
                a_lo(7, 8 * q + 8, 1)

            up(0)
            up(1)
            evac_stage("dn0", lambda k, ps, b: dve.tensor_scalar(two(FA, k), ps, 1.0, None, ALU.mult))
            add_f = lambda k, ps, b: dve.tensor_tensor(two(FA, k), ps, two(FA, k), ALU.add)
            up(2)
            evac_stage("dn1", add_f)
            up(3)
            evac_stage("dn2", add_f)
            evac_stage("dn3", add_f)
            post("n4", FA, "ffn_post", "x3_new", "x3_hi", "x3_split", "norm2")
            norm("n5")

            p0 = FIRST["in2a"][0]
            for t in range(7):
                if t == 2:
                    dve.wait_ge(once("wi_hi"), 1)
                    dve.tensor_tensor(WIL[:], WIR[:], WIH[:].bitcast(F32), ALU.subtract).then_inc(once("wi_split"), 2)
                dve.wait_ge(panel_done, p0 + t + 1)
                dst = CKV[:] if t == 0 else two(QI, t - 1) if t < 3 else two(QT, t - 3)
                dve.tensor_tensor(dst, psum_of(p0 + t), rr(), ALU.mult).then_inc(evac, 1)
                if t == 3:
                    dve.wait_ge(once("wx_ready"), 1)
                    for b in range(NB):
                        step_(dve.tensor_scalar(WX[:, 8 * b:8 * b + 8], PX[:, 2, 8 * b:8 * b + 8], RT[:, b:b + 1],
                                                IDX_HEADS ** -0.5 * HD ** -0.5, ALU.mult, ALU.mult))
            dve.wait_ge(evac, p0 + 7)
            dve.wait_ge(once("ln_mean"), 1)
            dve.scalar_tensor_tensor(out=KC[:], in0=PX[:, 3, :], scalar=-1.0 / P, in1=CKV[:, 1, :],
                                     op0=ALU.mult, op1=ALU.add).then_inc(once("ln_x"), 1)
            recip_r("kv")
            diags("kv", DG, 0, NB)
            dve.wait_ge(once("kv_bc"), 1)
            dve.scalar_tensor_tensor(out=CKV[:, 0, :], in0=CKV[:, 0, :], scalar=col("kv_norm", 0), in1=PX[:, 1, :],
                                     op0=ALU.mult, op1=ALU.mult).then_inc(once("kv_done"), 1)
            recip_r("ln")
            diags("ln", DG, 0, NB)
            dve.wait_ge(once("ln_bc"), 1)
            link(dve.scalar_tensor_tensor(out=KC[:], in0=KC[:], scalar=col("ln_g", 0), in1=PX[:, 2, :],
                                          op0=ALU.mult, op1=ALU.mult))
            dve.tensor_scalar(CKV[:, 1, :], KC[:], col("ln_b", 0), None, ALU.add).then_inc(once("ki_done"), 1)
            OFF = {1: 0, 2: 256, 3: 640}
            for u in range(24):
                qb, j = u // 8 + 1, u % 8
                n = (qb + 1) * P
                acc = MD[:, OFF[qb]:OFF[qb] + n]
                if j == 0:
                    link(dve.tensor_scalar(acc, EC[:, (3 - qb) * P:], 1e29, -3e38, ALU.is_ge, ALU.mult))
                dve.wait_ge(once("idx_relu"), u + 1)
                dve.scalar_tensor_tensor(out=acc, in0=RLU[:, u % 2, 0:n], scalar=WX[:, 8 * qb + j:8 * qb + j + 1],
                                         in1=acc, op0=ALU.mult, op1=ALU.add).then_inc(once("idx_acc"), 1)
                dve.wait_ge(once("idx_acc"), u + 1)

            def settled():
                dve.wait_ge(dve_step, step_.n)
                dve.memset(WORD, 0.0)

            def topk_round():
                blocks = [(M8[:, 8 * qb - 8:8 * qb], MD[:, OFF[qb]:OFF[qb] + (qb + 1) * P]) for qb in (1, 2, 3)]
                for m8, w in blocks:
                    step_(dve.max(m8, w))
                settled()
                for m8, w in blocks:
                    step_(dve.match_replace(out=w, in_to_replace=m8, in_values=w, imm_value=-3.3e38))
                settled()

            def rg_conv(t):
                xc = XC[:, t % 2]
                dve.wait_ge(once("rg_conv0"), 2 * t + 2)
                for d in (1, 2, 3):
                    for m in range(2):
                        ins = dve.scalar_tensor_tensor(out=xc[:, m, d:], in0=XR[:, 2 * t + m, 0:S - d],
                                                       scalar=col("rw", (3 - d) * 8 + 2 * t + m), in1=xc[:, m, d:],
                                                       op0=ALU.mult, op1=ALU.add)
                        step_(ins) if d < 3 else ins.then_inc(once("rg_conv"), 1)
                    if d < 3:
                        dve.wait_ge(dve_step, step_.n)

            p0 = FIRST["xr"][0]
            for t in range(4):
                dve.wait_ge(panel_done, p0 + t + 1)
                dve.tensor_tensor(two(XR, t), psum_of(p0 + t), rr(), ALU.mult).then_inc(evac, 1)
                if t == 3:
                    rg_conv(0)
                for _ in range(3 if t < 3 else 2):
                    topk_round()

            p0 = FIRST["rg"][0]
            r_, i_, a_, m_ = (RGT[:, k] for k in range(4))

            def rg_y(t):
                tt = slice(2 * t, 2 * t + 2)
                dve.scalar_tensor_tensor(out=i_, in0=XR[:, tt, :], scalar=0.5, in1=GR[:, tt, :],
                                         op0=ALU.mult, op1=ALU.mult).then_inc(once("rg_y"), 1)

            def rg_lo(t):
                tt = slice(2 * t, 2 * t + 2)
                dve.wait_ge(once("rg_hi"), t + 1)
                dve.tensor_tensor(RL[:, tt, :], i_, RH[:, tt, :].bitcast(F32), ALU.subtract).then_inc(once("rg_lo"), 2)

            def mr_out(t):
                dve.wait_ge(panel_done, p0 + 2 * t + 2)
                dve.tensor_tensor(two(GA, t), psum_of(p0 + 1), rr(), ALU.mult).then_inc(evac, 1)

            for t in range(4):
                tt = slice(2 * t, 2 * t + 2)
                xc = XC[:, t % 2]
                if t >= 1:
                    rg_y(t - 1)
                if t < 3:
                    rg_conv(t + 1)
                if t >= 1:
                    rg_lo(t - 1)
                    mr_out(t - 1)
                dve.wait_ge(once("rg_conv"), 2 * t + 2)
                dve.wait_ge(once("rg_ti"), t + 1)
                dve.scalar_tensor_tensor(out=i_, in0=i_, scalar=1.0, in1=xc, op0=ALU.add, op1=ALU.mult)\
                    .then_inc(once("rg_ix"), 1)
                dve.wait_ge(once("rg_a"), t + 1)
                link(dve.tensor_tensor(m_, a_, a_, ALU.mult))
                dve.wait_ge(once("rg_tanh"), t + 1)
                dve.scalar_tensor_tensor(out=m_, in0=m_, scalar=1.0, in1=r_, op0=ALU.add, op1=ALU.mult)\
                    .then_inc(once("rg_m"), 1)
                topk_round()
                dve.wait_ge(once("rg_sqrt"), t + 1)
                dve.wait_ge(once("rg_ix"), t + 1)
                link(dve.scalar_tensor_tensor(out=i_, in0=i_, scalar=0.5, in1=m_, op0=ALU.mult, op1=ALU.mult))
                dve.wait_ge(panel_done, p0 + 2 * t + 1)
                dve.tensor_tensor(two(GR, t), psum_of(p0), rr(), ALU.mult).then_inc(evac, 1)
                for m in range(2):
                    step_(dve.tensor_tensor_scan(out=XR[:, 2 * t + m, :], data0=a_[:, m, :], data1=i_[:, m, :],
                                                 initial=0.0, op0=ALU.mult, op1=ALU.add))
                dve.wait_ge(evac, p0 + 2 * t + 1)
                dve.wait_ge(once("rg_tg"), t + 1)
                link(dve.scalar_tensor_tensor(out=GR[:, tt, :], in0=r_, scalar=1.0, in1=GR[:, tt, :],
                                              op0=ALU.add, op1=ALU.mult))
            rg_y(3)
            rg_lo(3)
            mr_out(3)
            topk_round()

            p0 = FIRST["wr"][0]
            for t in range(4):
                dve.wait_ge(panel_done, p0 + t + 1)
                dve.wait_ge(once("mr_sg"), t + 1)
                dve.tensor_tensor(two(M2, t), psum_of(p0 + t), two(GA, t), ALU.mult).then_inc(evac, 1)
            link(dve.tensor_scalar(MD[:], MD[:], -3.2e38, FAR, ALU.is_ge, ALU.mult))
            for qb in (1, 2, 3):
                w = MD[:, OFF[qb]:OFF[qb] + (qb + 1) * P]
                dve.tensor_tensor(w, w, EC[:, (3 - qb) * P:], ALU.add).then_inc(once("md_done"), 1)
            dve.wait_ge(once("md_done"), 3)
            p0 = FIRST["ga"][0]
            for t in range(4):
                dve.wait_ge(panel_done, p0 + t + 1)
                dve.tensor_tensor(two(GA, t), psum_of(p0 + t), rr(), ALU.mult).then_inc(evac, 1)
                dve.wait_ge(once("sig_ga"), t + 1)
                dve.tensor_tensor(two(GA, t), two(GA, t), SGA[:], ALU.mult).then_inc(once("silu_ga"), 1)
            dve.wait_ge(once("silu_ga"), 4)

            def mla_logits(u):
                g, qb = divmod(u, NB)
                dist = EC[:, 3 * P:] if qb == 0 else MD[:, OFF[qb]:OFF[qb] + (qb + 1) * P]
                unit_logits("mla", PM, u, qb, dist, SLOPES_2[2 * g:2 * g + 2])

            def mla_probs(u, qb):
                s, n = u % 3, (qb + 1) * P
                den = DEN3[:, 2 * s:2 * s + 2]
                dve.wait_ge(once("mla_exp"), u + 1)
                link(dve.reciprocal(den, den))
                for m in range(2):
                    ins = dve.tensor_scalar(PM[s][:, m, 0:n], PM[s][:, m, 0:n], den[:, m:m + 1], None, ALU.mult)
                ins.then_inc(once("mla_probs"), 1)

            def mla_gate(g):
                dve.wait_ge(once("mla_yp"), g + 1)
                dve.tensor_tensor(GA[:, g, :], PX[:, 2, :], GA[:, g, :], ALU.mult).then_inc(once("mla_y"), 1)

            mla_logits(0)
            for u in range(32):
                g, qb = divmod(u, NB)
                if u + 1 < 32:
                    mla_logits(u + 1)
                mla_probs(u, qb)
                if qb == 0 and g >= 1:
                    mla_gate(g - 1)
                if qb == NB - 1:
                    dve.wait_ge(once("mla_pv"), g + 1)
                    dve.tensor_copy(OL[:], PX[:, 2:4, :]).then_inc(once("mla_ol"), 1)
            mla_gate(7)
            split("o_split", "o_hi", GA, None, RH, OLO)
            p0 = FIRST["mga"][0]
            for t in range(4):
                dve.wait_ge(panel_done, p0 + t + 1)
                dve.tensor_tensor(MGA[t][:], psum_of(p0 + t), rr(), ALU.mult).then_inc(evac, 1)
            p0 = FIRST["ap"][0]
            for t in range(4):
                dve.wait_ge(panel_done, p0 + t + 1)
                dve.wait_ge(once("ma_sg"), t + 1)
                dve.tensor_tensor(SG[:], psum_of(p0 + t), MGA[t][:], ALU.mult).then_inc(evac, 1)
                dve.wait_ge(evac, p0 + t + 1)
                link(dve.tensor_tensor(two(M2, t), two(M2, t), SG[:], ALU.add))
                dve.tensor_copy(RTL, RTL).then_inc(once("m_ready"), 2)
            split("m_split", "m_hi", M2)
            p0 = FIRST["out2"][0]
            dve.wait_ge(once("m_split"), 8)
            dve.wait_ge(reloaded, 16)
            evac_stage("out2", lambda k, ps, b: dve.tensor_tensor(two(M2, k), ps, two(XT, k), ALU.add))
            norm("n6")
            for c in range(DC):
                dve.scalar_tensor_tensor(out=SQ2[:, c, :], in0=M2[:, c, :], scalar=col("final", c), in1=R[:],
                                         op0=ALU.mult, op1=ALU.mult).then_inc(once("out_ready"), 1)


def kernel(**inputs):
    import numpy as np
    import concourse.bacc as bacc
    from concourse.bass_utils import run_bass_kernel_spmd

    a = {k: np.asarray(v) for k, v in inputs.items()}
    a = {k: (v[0] if v.ndim > 1 and v.shape[0] == 1 and k != "x" else v) for k, v in a.items()}

    def panel(w):
        n = w.shape[1] // 256
        return w.reshape(8, 128, n, 256).transpose(2, 1, 0, 3).reshape(n, 128, 2048)

    perm = np.concatenate([np.arange(64) + 64 * h for j in range(4) for h in (j, 4 + j)])
    w_in = a["w_in"]
    w_in = np.concatenate([w_in[:, :512][:, perm], w_in[:, 512:]], 1)
    w_out = np.concatenate([a["w_out"][:512][perm], a["w_out"][512:]], 0)
    up = a["w_up"].reshape(1024, 2, 32, 128).transpose(0, 2, 1, 3).reshape(1024, 8192)
    w2 = a["w_in_2"]
    off = np.cumsum([0, 1024, 128, 512, 64, 8, 1024, 1024, 1024, 2048])
    q2, ckv, qi, ki, wi, ga, xr, gr, mg = (w2[:, off[i]:off[i + 1]] for i in range(9))

    def inter(x, y):
        x, y = panel(x), panel(y)
        return np.stack([x, y], 1).reshape(2 * x.shape[0], 128, 2048)

    ups, downs = panel(up), [panel(a["w_down"][1024 * q:1024 * (q + 1)]) for q in range(4)]
    panels = np.concatenate([
        panel(w_in), panel(w_out), ups[0:8], ups[8:16], downs[0], ups[16:24], downs[1], ups[24:32],
        downs[2], downs[3],
        panel(np.concatenate([ckv, ki, ki], 1)), panel(qi), panel(q2), panel(xr), inter(gr, mg[:, 1024:]), panel(a["w_rnn_proj_2"]),
        panel(ga), panel(mg[:, :1024]), panel(a["w_attn_proj_2"]), panel(a["w_out_2"]),
    ], 0)

    def cols(v):
        return v.reshape(-1, 128).T

    sink = np.broadcast_to(a["swa_sinks"][None, :], (128, 8))
    twice = lambda v: np.concatenate([v, v])
    col = np.concatenate([
        cols(a["attn_pre_g"]), cols(a["swa_out_g"][perm]), cols(a["diff_subln_g"]), cols(a["attn_post_g"]),
        cols(a["ffn_pre_g"]), cols(a["conv_w"][0]), cols(a["conv_w"][1]), cols(a["conv_w"][2]), cols(a["conv_b"]),
        cols(a["ffn_post_g"]), cols(a["norm_gain_2"]), cols(a["b_merge_2"]), cols(a["kv_norm_gain_2"]),
        cols(twice(a["idx_ln_gain_2"])), cols(twice(a["idx_ln_bias_2"])),
        *[cols(a["conv_w_2"][k]) for k in range(4)], cols(a["conv_b_2"]), cols(a["b_rg_a_2"]), cols(a["b_rg_x_2"]),
        cols(a["lru_lambda_2"]), cols(a["final_norm_gain_2"]), sink], 1)
    lamv = np.stack([a[k] for k in ("diff_lq1", "diff_lk1", "diff_lq2", "diff_lk2")])
    lamv = np.broadcast_to(lamv[None], (128, 4, 64))
    rgw = np.zeros((128, 2, 8, 128), np.float32)
    for k, name in enumerate(("w_rg_a_2", "w_rg_x_2")):
        w = a[name].reshape(8, 2, 64, 64)
        for m in range(2):
            rgw[64 * m:64 * m + 64, k, :, 64 * m:64 * m + 64] = w[:, m].transpose(1, 0, 2)
    uk = a["w_uk_2"].reshape(8, 2, 128, 64).transpose(1, 3, 0, 2).reshape(128, 8, 128)
    uv = a["w_uv_2"].transpose(1, 0, 2)
    wis = wi.reshape(8, 128, 8).transpose(1, 0, 2)
    arrays = {"panels": panels, "xT": a["x"].reshape(512, 1024).T, "cols": col, "lamv": lamv, "wi": wis,
              "rgw": rgw, "uk": uk, "uv": uv}
    arrays = {k: np.ascontiguousarray(v) for k, v in arrays.items()}
    nc = bacc.Bacc("TRN2", target_bir_lowering=False, num_devices=1)
    args = [nc.dram_tensor(k, v.shape, mybir.dt.from_np(v.dtype), kind="ExternalInput").ap() for k, v in arrays.items()]
    args.append(nc.dram_tensor("outT", (1024, 512), F32, kind="ExternalOutput").ap())
    build(nc, *args)
    r = run_bass_kernel_spmd(nc, [arrays], core_ids=[0])
    return np.ascontiguousarray(r.results[0]["outT"].T).reshape(1, 512, 1024)
```

```python
from contextlib import ExitStack

import concourse.bass as bass
from concourse import mybir

F32 = mybir.dt.float32
F32R = mybir.dt.float32r
I32 = mybir.dt.int32
ALU = mybir.AluOpType
ACT = mybir.ActivationFunctionType
AX_X = mybir.AxisListType.X

P = 128
S = 512
D = 1024
DC = D // P
NB = S // P
HD = 64
SWA_PAIRS = 4
DIFF_HEADS = 4
MLA_HEADS = 16
IDX_HEADS = 8
TOPK = 128
EPS = 1e-6
SCALE = HD ** -0.5
FAR = 1e30
LAMBDA_INIT = 0.2
SLOPES_1 = sorted([2.0 ** -(i + 1) for i in range(8)] + [2.0 ** -(0.5 * (2 * i + 1)) for i in range(4)], reverse=True)
SLOPES_2 = [2.0 ** (-8.0 * (i + 1) / MLA_HEADS) for i in range(MLA_HEADS)]

STAGES = [("in1", 8), ("in1v", 1), ("out1", 4), ("up0", 8), ("up1", 8), ("dn0", 4), ("up2", 8), ("dn1", 4),
          ("up3", 8), ("dn2", 4), ("dn3", 4), ("in2a", 7), ("xr", 4), ("rg", 8), ("wr", 4),
          ("ga", 4), ("mga", 4), ("ap", 4), ("out2", 4)]
FIRST, NPANELS = {}, 0
for _name, _n in STAGES:
    FIRST[_name] = (NPANELS, _n)
    NPANELS += _n

COLS, NCOLS = {}, 0
for _name, _n in [("attn_pre", 8), ("swa_out", 4), ("subln", 1), ("attn_post", 8), ("ffn_pre", 8),
                  ("cw0", 64), ("cw1", 64), ("cw2", 64), ("cb", 64), ("ffn_post", 8), ("norm2", 8),
                  ("b_merge", 16), ("kv_norm", 1), ("ln_g", 1), ("ln_b", 1), ("rw", 32), ("rb", 8),
                  ("b_rg_a", 8), ("b_rg_x", 8), ("lru", 8), ("final", 8), ("sinks", 8)]:
    COLS[_name] = NCOLS
    NCOLS += _n


class Count:

    def __init__(self, sem):
        self.sem, self.n = sem, 0

    def __call__(self, ins):
        ins.then_inc(self.sem, 1)
        self.n = self.n + 1


def build(nc, panels, xT, cols_in, lamv_in, wi_in, rgw_in, uk_in, uv_in, outT):
    spill = nc.dram_tensor("x2_spill", (P, DC, S), F32, kind="Internal").ap()
    with ExitStack() as ctx:
        KB = 1024
        ARENA0 = 16512 + 32

        def at(name, shape, kb, dt=F32):
            size = 4
            for n in shape[1:]:
                size *= n
            assert kb * KB + size <= 207.5 * KB, (name, kb, size)
            return nc.alloc_sbuf_tensor_at(name, shape, dt, offset=ARENA0 + int(kb * KB))

        def sem(name):
            return ctx.enter_context(nc.semaphore(name))

        XT = at("XT", [P, DC, S], 0)
        XH = at("XH", [P, DC, S], 16, F32R)
        XL = at("XL", [P, DC, S], 32, F32R)
        WH = at("WH", [P, 2, DC, 256], 48, F32R)
        WL = at("WL", [P, 2, DC, 256], 64, F32R)
        RAW = at("RAW", [P, 2, DC * 256], 80)
        PROJ = at("PROJ", [P, 18, S], 96)
        VA = at("VA", [P, NB, P], 132)
        VB = at("VB", [P, DIFF_HEADS, NB, P], 134)
        MIX = at("MIX", [P, DC, S], 142)
        SQ1 = at("SQ1", [P, DC, S], 142)
        DS4 = at("DS4", [P, NB, 256], 158)
        PSW = at("PSW", [P, 3, NB, 256], 162)
        PD = [at(f"PD{k}", [P, 2, S], 162 + 4 * k) for k in range(3)]
        PTW = [at(f"PTW{k}", [P, NB, 256], kb) for k, kb in enumerate((186, 124))]
        PTD = at("PTD", [P, 2, NB, S], 174)
        MR = at("MR", [P, S], 194)
        DH = at("DH", [P, 2, S], 190)
        MSQ = at("MSQ", [P, DC, S], 96)
        Y1 = at("Y1", [P, DC, S], 142)
        SQY = at("SQY", [P, DC, S], 96)
        AH = at("AH", [P, 2, DC, S], 96, F32R)
        AL = at("AL", [P, 2, DC, S], 128, F32R)
        FA = at("FA", [P, DC, S], 160)
        U = at("U", [P, 2, 2, S], 176)
        C = at("C", [P, 2, 2, S], 184)
        Z = at("Z", [P, 2, S], 192)
        SQF = at("SQF", [P, DC, S], 96)
        QT = at("QT", [P, 8, S], 96)
        CKV = at("CKV", [P, 2, S], 112)
        CKT = at("CKT", [P, NB, P], 116)
        XR = at("XR", [P, 8, S], 118)
        GR = at("GR", [P, 8, S], 134)
        RH = at("RH", [P, 8, S], 118, F32R)
        RL = at("RL", [P, 8, S], 134, F32R)
        GA = at("GA", [P, 8, S], 150)
        MGA = [at(f"MGA{k}", [P, 2, S], kb) for k, kb in enumerate((4, 134, 138, 146))]
        OLO = at("OLO", [P, 8, S], 96, F32R)
        QI = at("QI", [P, 4, S], 150)
        QIH = at("QIH", [P, 4, S], 118, F32R)
        QIL = at("QIL", [P, 4, S], 126, F32R)
        KIH = at("KIH", [P, S], 134, F32R)
        KIL = at("KIL", [P, S], 136, F32R)
        CSQ = at("CSQ", [P, 2, S], 158)
        KC = at("KC", [P, S], 162)
        WIH = at("WIH", [P, DC, 8], 164, F32R)
        WIL = at("WIL", [P, DC, 8], 164.25, F32R)
        WIR = at("WIR", [P, DC, 8], 164.5)
        WXT = at("WXT", [P, S], 187)
        MD = at("MD", [P, 1152], 166)
        RLU = at("RLU", [P, 2, S], 191)
        XC = at("XC", [P, 2, 2, S], 171)
        RGT = at("RGT", [P, 4, 2, S], 179)
        M2 = at("M2", [P, 8, S], 171)
        SG = at("SG", [P, 2, S], 191)
        RGW = at("RGW", [P, 2, 8, P], 0)
        UK = at("UK", [P, 8, P], 8)
        UV = at("UV", [P, MLA_HEADS, HD], 12)
        PM = [at(f"PM{k}", [P, 2, S], kb) for k, kb in enumerate((118, 122, 0))]
        PTM = at("PTM", [P, 2, NB, S], 126)
        OL = at("OL", [P, 2, S], 142)
        SGA = at("SGA", [P, 2, S], 146)
        QLH = at("QLH", [P, 2, S], 187, F32R)
        QLL = at("QLL", [P, 2, S], 191, F32R)
        CKH = at("CKH", [P, S], 114, F32R)
        CKL = at("CKL", [P, S], 204, F32R)
        SQ2 = at("SQ2", [P, DC, S], 118)
        COL = at("COL", [P, NCOLS], 196)
        EC = at("EC", [P, S], 198)
        IDN = at("IDN", [P, P], 200)
        O1024 = at("O1024", [P, P], 200.5)
        O512 = at("O512", [P, P], 203)
        O128 = at("O128", [P, P], 203.5)
        R = at("R", [P, S], 201)
        LV = at("LV", [P, 4, HD], 205)
        SM = at("SM", [P, 224], 206)

        PG = ctx.enter_context(nc.psum_tensor("PG", [P, 4, S], F32))
        PX = ctx.enter_context(nc.psum_tensor("PX", [P, 4, S], F32))

        def col(name, k, n=1):
            return COL[:, COLS[name] + k:COLS[name] + k + n] if isinstance(k, int) else \
                COL[:, bass.ds(k + COLS[name], n)]

        SMN = [0]

        def small(n):
            SMN[0] += n
            assert SMN[0] <= 224
            return SM[:, SMN[0] - n:SMN[0]]

        LAM = small(1)
        LDOT = small(2)
        NEG_SP4 = small(8)
        POS_SP4 = small(8)
        HALF_B = small(16)
        SP = small(24)
        SINK8 = small(8)
        SUBLN = small(1)
        EPST = small(1)
        MX = small(4)
        MX3 = small(6)
        NM = small(12)
        DEN = small(12)
        ES = small(4)
        M8 = small(24)
        WX = small(32)
        NM3 = small(6)
        DEN3 = small(6)
        RTL = small(1)
        WORD = small(1)

        loaded_x = [sem(f"loaded_x{k}") for k in range(4)]
        loaded_lam = sem("loaded_lam")
        loaded_c = sem("loaded_c")
        loaded_b2 = sem("loaded_b2")
        loaded_wi = sem("loaded_wi")
        spilled = sem("spilled")
        reloaded = sem("reloaded")
        stored = sem("stored")
        raw_in = [sem("raw_in0"), sem("raw_in1")]
        w_hi = sem("w_hi")
        w_lo = sem("w_lo")
        panel_done = sem("panel_done")
        evac = sem("evac")
        consts = sem("consts")
        act_step = sem("act_step")
        dve_step = sem("dve_step")
        named = {}

        def once(name):
            if name not in named:
                named[name] = sem(name)
            return named[name]

        block = ctx.enter_context(nc.Block())

        def pairs(eng, name, step, skip=0):
            p0, n = FIRST[name]
            if n - skip >= 4:
                with eng.Fori(0, (n - skip) // 2) as i:
                    for b in range(2):
                        step(i * 2 + (p0 + skip + b), i * 2 + (skip + b), b, i)
            else:
                for k in range(skip, n - (n - skip) % 2):
                    step(p0 + k, k, (k - skip) % 2, None)
            if (n - skip) % 2:
                step(p0 + n - 1, n - 1, 0, None)

        def mla_slot(u):
            return (max(u - 2, 0) // 8 + FIRST["ga"][0]) % 2

        def xT_chunks(k):
            return xT.rearrange("(c p) n -> p c n", p=P)[:, 2 * k:2 * k + 2, :]

        @block.sync
        def _(sp):
            sp.dma_start(COL[:], cols_in).then_inc(loaded_c, 16)
            sp.dma_start(RAW[:, 0, :], panels[0]).then_inc(raw_in[0], 16)
            for k in range(0, 4, 2):
                sp.dma_start(XT[:, 2 * k:2 * k + 2, :], xT_chunks(k)).then_inc(loaded_x[k], 16)
            sp.dma_start(RAW[:, 1, :], panels[1]).then_inc(raw_in[1], 16)
            sp.dma_start(LV[:], lamv_in).then_inc(loaded_lam, 16)
            with sp.Fori(1, NPANELS // 2) as i:
                for s in range(2):
                    sp.wait_ge(w_lo, i * 2 + (s - 1))
                    sp.dma_start(RAW[:, s, :], panels[bass.ds(i * 2 + s, 1), :, :].rearrange("a p n -> p (a n)"))\
                        .then_inc(raw_in[s], 16)
            for k in range(4):
                sp.wait_ge(once("out_ready"), 2 * k + 2)
                sp.dma_start(outT.rearrange("(c p) n -> p c n", p=P)[:, 2 * k:2 * k + 2, :], SQ2[:, 2 * k:2 * k + 2, :])\
                    .then_inc(stored, 16)
            sp.wait_ge(stored, 64)

        @block.gpsimd
        def _(pool):
            pool.memset(O1024[:], 1.0 / 1024).then_inc(consts, 1)
            pool.memset(IDN[:], 0.0).then_inc(consts, 1)
            pool.wait_ge(consts, 2)
            pool.affine_select(out=IDN[:], in_=IDN[:], compare_op=ALU.not_equal, fill=1.0, base=0,
                               pattern=[[-1, P]], channel_multiplier=1).then_inc(consts, 1)

            def lo(s, value):
                pool.wait_ge(w_hi, value)
                pool.tensor_tensor(WL[:, s].rearrange("p a b -> p (a b)"), RAW[:, s, :],
                                   WH[:, s].rearrange("p a b -> p (a b)").bitcast(F32), ALU.subtract)\
                    .then_inc(w_lo, 1)

            lo(0, 1)
            lo(1, 2)
            dist_i = PSW[:, 0, 0:2].rearrange("p a b -> p (a b)")
            pool.iota(EC[:].bitcast(I32), pattern=[[-1, S]], base=(NB - 1) * P, channel_multiplier=1).then_inc(consts, 1)
            pool.wait_ge(consts, 4)
            pool.tensor_copy(dist_i, EC[:].bitcast(I32)).then_inc(consts, 1)
            pool.wait_ge(consts, 5)
            pool.affine_select(out=EC[:], in_=dist_i, compare_op=ALU.is_ge, fill=FAR,
                               base=(NB - 1) * P, pattern=[[-1, S]], channel_multiplier=1).then_inc(consts, 1)
            pool.wait_ge(consts, 6)
            for b in range(NB):
                pool.affine_select(out=DS4[:, b, :], in_=EC[:, 2 * P:], compare_op=ALU.is_ge, fill=FAR,
                                   base=-1, pattern=[[1, 256]], channel_multiplier=-1).then_inc(consts, 1)
            pool.wait_ge(consts, 10)
            pool.memset(DS4[:, 0, 0:P], FAR).then_inc(consts, 1)
            pool.memset(O512[:], 1.0 / 512).then_inc(consts, 1)
            pool.memset(O128[:], 1.0 / 128).then_inc(consts, 1)

            with pool.Fori(1, NPANELS // 2) as i:
                for s in range(2):
                    lo(s, i * 2 + (s + 1))

        @block.tensor
        def _(pe):
            def one_panel(p, s, xh=XH, xl=XL, ready=None):
                pe.wait_ge(w_lo, p + 1)
                if not (isinstance(p, int) and p < 2):
                    pe.wait_ge(evac, p - 1)
                order = [(m, c) for m in range(2) for c in range(DC)]
                if ready is not None:
                    order = [(m, c) for c in range(DC) for m in range(2)]
                for m, c in order:
                    if ready is not None and m == 0:
                        pe.wait_ge(ready[0], ready[1] + c + 1)
                    ms = slice(m * P, (m + 1) * P)
                    o = PG[:, 2 * s + m, :]
                    pe.matmul(o, WH[:, s, c, ms], xh[:, c, :], start=(c == 0), stop=False)
                    pe.matmul(o, WH[:, s, c, ms], xl[:, c, :], start=False, stop=False)
                    mm = pe.matmul(o, WL[:, s, c, ms], xh[:, c, :], start=False, stop=(c == DC - 1))
                mm.then_inc(panel_done, 1)

            def panel_piece(p, piece):
                s = p % 2
                if piece == 0:
                    pe.wait_ge(w_lo, p + 1)
                    pe.wait_ge(evac, p - 1)
                passes = [(m, c, w, x) for m in range(2) for c in range(DC) for w, x in ((WH, XH), (WH, XL), (WL, XH))]
                for n in range(6 * piece, 6 * piece + 6):
                    m, c, w, x = passes[n]
                    mm = pe.matmul(PG[:, 2 * s + m, :], w[:, s, c, m * P:(m + 1) * P], x[:, c, :],
                                   start=(n % 24 == 0), stop=(n % 24 == 23))
                if piece == 7:
                    mm.then_inc(panel_done, 1)

            def gemm(name, xh=XH, xl=XL, ready=None, after={}):
                p0, _ = FIRST[name]
                peeled = 1 + max([-1, *after, 0 if ready else -1, 1 if p0 == 0 else -1])
                for k in range(peeled):
                    one_panel(p0 + k, (p0 + k) % 2, xh, xl, ready if k == 0 else None)
                    if k in after:
                        after[k]()
                pairs(pe, name, lambda p, k, b, i: one_panel(p, (p0 + peeled + b) % 2, xh, xl), peeled)

            def mean_square(name, parts, bank=1):
                for k, (signal, value, tile) in enumerate(parts):
                    pe.wait_ge(signal, value)
                    mm = pe.matmul(PX[:, bank, :], O1024[:], tile, start=(k == 0), stop=(k == len(parts) - 1))
                mm.then_inc(once(name + "_sum"), 1)

            def gemm_sums(name, norm, src, xh=XH, xl=XL, ready=None):
                gemm(name, xh, xl, ready)
                acc, sq = once(norm + "_acc"), once(norm + "_sq")
                mean_square(norm, [(acc, 1, src[:, 0, :]), (acc, 1, src[:, 1, :]), (sq, 4, src[:, 6, :]), (sq, 4, src[:, 7, :])])

            def gemm_norm(name, norm, src, ready, more={}):
                acc = once(norm + "_acc")
                gemm(name, ready=(once(ready), 0),
                     after={0: lambda: mean_square(norm, [(acc, 1, src[:, 0, :]), (acc, 1, src[:, 1, :])]), **more})

            pe.wait_ge(consts, 3)
            gemm_norm("in1", "n1", SQ1, "x1_split")

            def turn_values(t, bank):
                tile = 5 if t == 0 else 13 + t
                for b in range(NB):
                    mm = pe.transpose(PX[:, bank, b * P:(b + 1) * P], PROJ[:, tile, b * P:(b + 1) * P], IDN[:])
                mm.then_inc(once("v_turned"), 1)

            def swa_scores(h):
                g, j = divmod(h, SWA_PAIRS)
                rows = slice(g * HD, (g + 1) * HD)
                if h >= 2:
                    pe.wait_ge(once("swa_logits"), h - 1)
                s = h % 2
                for qb in range(NB):
                    q = PROJ[rows, j, qb * P:(qb + 1) * P]
                    o = PG[:, 2 * s + qb // 2, (qb % 2) * 256:(qb % 2) * 256 + 256]
                    if qb == 0:
                        pe.matmul(o[:, 0:P], q, PROJ[rows, 4, 0:P], start=True, stop=True)
                        mm = pe.matmul(o[:, P:], q, PROJ[rows, 4, 0:P], start=True, stop=True)
                    else:
                        mm = pe.matmul(o, q, PROJ[rows, 4, (qb - 1) * P:(qb + 1) * P], start=True, stop=True)
                mm.then_inc(once("swa_s"), 1)

            def swa_turn(h):
                pe.wait_ge(once("swa_probs"), h + 1)
                if h >= 1:
                    pe.wait_ge(once("swa_copied"), h)
                else:
                    pe.wait_ge(once("v_copied"), 3)
                for kb in range(NB):
                    o = PX[:, kb // 2, (kb % 2) * 256:(kb % 2) * 256 + 256]
                    mm = pe.transpose(o[:, 0:P], PSW[:, h % 3, kb, P:256], IDN[:])
                    if kb < NB - 1:
                        mm = pe.transpose(o[:, P:256], PSW[:, h % 3, kb + 1, 0:P], IDN[:])
                mm.then_inc(once("swa_turned"), 1)

            def swa_pv(h):
                g, j = divmod(h, SWA_PAIRS)
                rows = slice(g * HD, (g + 1) * HD)
                pe.wait_ge(once("swa_copied"), h + 1)
                if h >= 2:
                    pe.wait_ge(once("swa_out"), h - 1)
                for kb in range(NB):
                    n = 256 if kb < NB - 1 else P
                    mm = pe.matmul(PX[rows, 2 + h % 2, kb * P:kb * P + n], VA[:, kb, rows], PTW[h % 2][:, kb, 0:n],
                                   start=(kb == 0), stop=(kb == NB - 1), skip_group_check=True)
                mm.then_inc(once("swa_pv"), 1)

            pe.wait_ge(evac, FIRST["in1v"][0] - 1)
            swa_scores(0)
            pe.wait_ge(evac, FIRST["in1v"][0])
            swa_scores(1)
            for t in range(3):
                if t >= 2:
                    pe.wait_ge(once("v_copied"), t - 1)
                turn_values(t, t % 2)
            for h in range(8):
                if h + 2 < 8:
                    swa_scores(h + 2)
                swa_turn(h)
                if h >= 1:
                    swa_pv(h - 1)
            swa_pv(7)

            def unit_turn(pre, src, u, qb, maps):
                pe.wait_ge(once(pre + "_probs"), u + 1)
                if u >= 1:
                    pe.wait_ge(once(pre + "_copied"), u)
                for m in range(maps):
                    for kb in range(qb + 1):
                        mm = pe.transpose(PX[:, m, kb * P:(kb + 1) * P], src[u % 3][:, m, kb * P:(kb + 1) * P], IDN[:])
                mm.then_inc(once(pre + "_turned"), 1)

            def diff_scores(u):
                h, qb = divmod(u, NB)
                if u >= 1:
                    pe.wait_ge(once("diff_logits"), 2 * u)
                n = (qb + 1) * P
                for m in range(2):
                    rows = slice(m * HD, (m + 1) * HD)
                    mm = pe.matmul(PG[:, 2 + m, 0:n], PROJ[rows, 6 + h, qb * P:(qb + 1) * P],
                                   PROJ[rows, 10 + h, 0:n], start=True, stop=True)
                mm.then_inc(once("diff_s"), 1)

            pe.wait_ge(consts, 13)

            def mix_sums(k):
                tiles = range(4) if k == 0 else [3 + k]
                for c in tiles:
                    pe.wait_ge(once("mix_sq"), c + 1)
                    mm = pe.matmul(PX[:, 1, :], O512[:] if k == 0 else O128[:], MSQ[:, c, :], start=(c == tiles[0]),
                                   stop=(c == tiles[-1]))
                mm.then_inc(once("mix_sum"), 1)

            def diff_pv(h):
                pe.wait_ge(once("diff_copied"), NB * h + NB)
                if h == 2:
                    pe.wait_ge(once("v_copied"), 5)
                if h >= 1:
                    pe.wait_ge(once("diff_out"), h)
                for kb in range(NB):
                    mm = pe.matmul(PX[:, 2, kb * P:], VB[:, h, kb, :], PTD[:, h % 2, kb, kb * P:],
                                   start=(kb == 0), stop=(kb == NB - 1), skip_group_check=True)
                mm.then_inc(once("diff_pv"), 1)

            pe.wait_ge(once("swa_logits"), 8)
            diff_scores(0)
            diff_scores(1)
            for u in range(16):
                h, qb = divmod(u, NB)
                if u == 0:
                    pe.wait_ge(once("swa_out"), 8)
                if u + 2 < 16:
                    diff_scores(u + 2)
                unit_turn("diff", PD, u, qb, 1)
                if u < 8:
                    panel_piece(FIRST["in1v"][0], u)
                if u in (9, 10):
                    pe.wait_ge(evac, FIRST["out1"][0])
                    if u == 10:
                        pe.wait_ge(once("v_copied"), 4)
                    turn_values(u - 6, 3)
                if qb == 2:
                    mix_sums(h)
                if qb == 0 and h >= 1:
                    diff_pv(h - 1)
            diff_pv(3)
            mix_sums(4)
            gemm_sums("out1", "n2", SQY, ready=(once("mix_split"), 0))
            gemm_norm("up0", "n3", SQY, "x2_split")
            gemm("up1")
            for q, nxt in enumerate(["up2", "up3", None, None]):
                pe.wait_ge(once("a_lo"), 8 * (q + 1))
                if q < 3:
                    gemm(f"dn{q}", AH[:, q % 2], AL[:, q % 2])
                if nxt:
                    gemm(nxt)
            gemm_sums("dn3", "n4", SQF, AH[:, 1], AL[:, 1])

            def w_idx():
                pe.wait_ge(once("wi_split"), 2)
                for c in range(DC):
                    o = PX[0:8, 0, :]
                    pe.matmul(o, WIH[:, c, :], XH[:, c, :], start=(c == 0), stop=False)
                    pe.matmul(o, WIL[:, c, :], XH[:, c, :], start=False, stop=False)
                    mm = pe.matmul(o, WIH[:, c, :], XL[:, c, :], start=False, stop=(c == DC - 1))
                mm.then_inc(once("wx_ready"), 1)

            def kv_sums():
                pe.wait_ge(evac, FIRST["in2a"][0] + 1)
                pe.matmul(PX[:, 3, :], O128[:], CKV[:, 1, :], start=True, stop=True).then_inc(once("ln_mean"), 1)
                pe.wait_ge(once("kv_sq"), 1)
                pe.matmul(PX[:, 1, :], O128[:], CSQ[:, 0, :], start=True, stop=True).then_inc(once("kv_sum"), 1)

            def ln_sums():
                pe.wait_ge(once("ln_sq"), 1)
                pe.matmul(PX[:, 2, :], O128[:], CSQ[:, 1, :], start=True, stop=True).then_inc(once("ln_sum"), 1)

            def turns():
                pe.wait_ge(once("wxt"), 1)
                pe.wait_ge(once("ln_x"), 1)
                for b in range(NB):
                    mm = pe.transpose(PX[:, 3, b * 8:(b + 1) * 8], WXT[0:8, b * P:(b + 1) * P], IDN[0:8, 0:8])
                mm.then_inc(once("wx_turned"), 1)
                pe.wait_ge(once("kv_done"), 1)
                for b in range(NB):
                    mm = pe.transpose(PX[:, 0, b * P:(b + 1) * P], CKV[:, 0, b * P:(b + 1) * P], IDN[:])
                mm.then_inc(once("kv_turned"), 1)

            gemm_norm("in2a", "n5", SQF, "x3_split", {1: w_idx, 2: kv_sums, 3: ln_sums, 4: turns})

            pe.wait_ge(once("idx_split"), 2)
            pe.wait_ge(evac, FIRST["xr"][0])

            for u in range(3 * IDX_HEADS):
                qb, j = u // IDX_HEADS + 1, u % IDX_HEADS
                n = (qb + 1) * P
                rows = slice((j % 2) * HD, (j % 2) * HD + HD)
                if u >= 4:
                    pe.wait_ge(once("idx_relu"), u - 3)
                elif u == 3:
                    pe.wait_ge(once("kv_copied"), 1)
                qh, ql = (q[rows, j // 2, qb * P:(qb + 1) * P] for q in (QIH, QIL))
                pe.matmul(PG[:, u % 4, 0:n], qh, KIH[rows, 0:n], start=True, stop=False)
                pe.matmul(PG[:, u % 4, 0:n], qh, KIL[rows, 0:n], start=False, stop=False)
                pe.matmul(PG[:, u % 4, 0:n], ql, KIH[rows, 0:n], start=False, stop=True).then_inc(once("idx_s"), 1)
            pe.wait_ge(once("idx_relu"), 24)
            gemm("xr")

            p0 = FIRST["rg"][0]
            pe.wait_ge(loaded_b2, 48)
            for t in range(4):
                pe.wait_ge(once("rg_conv"), 2 * t + 2)
                if t >= 1:
                    pe.wait_ge(once("rg_ti"), t)
                for m in range(2):
                    pe.matmul(PX[:, m, :], RGW[:, 0, 2 * t + m, :], XC[:, t % 2, m, :], start=True, stop=True)
                    mm = pe.matmul(PX[:, 2 + m, :], RGW[:, 1, 2 * t + m, :], XC[:, t % 2, m, :], start=True, stop=True)
                mm.then_inc(once("rg_proj"), 1)
                one_panel(p0 + 2 * t, p0 % 2)
                one_panel(p0 + 2 * t + 1, (p0 + 1) % 2)
            gemm("wr", RH, RL, ready=(once("rg_lo"), 0))

            def filler(u):
                k, piece = divmod(u, 8)
                if piece == 0 and k >= 1:
                    pe.wait_ge(once("mla_logits"), u + 2)
                panel_piece(FIRST["ga"][0] + 1 + k, piece)

            def qlat(g):
                for m in range(2):
                    rows = slice(m * HD, (m + 1) * HD)
                    mm = pe.matmul(PX[:, 2 + m, :], UK[rows, g, :], QT[rows, g, :], start=True, stop=True)
                mm.then_inc(once("mla_ql"), 1)

            def mla_scores(u):
                g, qb = divmod(u, NB)
                pe.wait_ge(once("mla_qsplit"), g + 1)
                if u >= 1:
                    pe.wait_ge(once("mla_logits"), u)
                if u % 8 == 2 and u > 2:
                    pe.wait_ge(evac, FIRST["ga"][0] + 1 + u // 8)
                n = (qb + 1) * P
                for m in range(2):
                    o = PG[:, 2 * mla_slot(u) + m, 0:n]
                    qh, ql = (q[:, m, qb * P:(qb + 1) * P] for q in (QLH, QLL))
                    pe.matmul(o, qh, CKH[:, 0:n], start=True, stop=False)
                    pe.matmul(o, qh, CKL[:, 0:n], start=False, stop=False)
                    mm = pe.matmul(o, ql, CKH[:, 0:n], start=False, stop=True)
                mm.then_inc(once("mla_s"), 1)

            def mla_y(g):
                pe.wait_ge(once("mla_ol"), g + 1)
                for m in range(2):
                    mm = pe.matmul(PX[m * HD:(m + 1) * HD, 2, :], UV[:, 2 * g + m, :], OL[:, m, :],
                                   start=True, stop=True)
                mm.then_inc(once("mla_yp"), 1)

            pe.wait_ge(once("rg_ti"), 4)
            pe.wait_ge(once("ck_lo"), 1)
            qlat(0)
            one_panel(FIRST["ga"][0], FIRST["ga"][0] % 2)
            pe.wait_ge(evac, FIRST["ga"][0] + 1)
            mla_scores(0)
            mla_scores(1)
            for u in range(32):
                g, qb = divmod(u, NB)
                if u + 2 < 32 and qb != 2:
                    mla_scores(u + 2)
                unit_turn("mla", PM, u, qb, 2)
                if qb == 1 and g < 7:
                    if g >= 1:
                        pe.wait_ge(once("mla_y"), g)
                    qlat(g + 1)
                filler(u)
                if u + 2 < 32 and qb == 2:
                    mla_scores(u + 2)
                if qb == 0 and g >= 1:
                    mla_y(g - 1)
                if qb == NB - 1:
                    pe.wait_ge(once("mla_copied"), u + 1)
                    if g < 7:
                        pe.wait_ge(once("mla_qsplit"), g + 2)
                    else:
                        pe.wait_ge(once("mla_y"), 7)
                    for m in range(2):
                        for kb in range(NB):
                            mm = pe.matmul(PX[:, 2 + m, kb * P:], CKT[:, kb, :], PTM[:, m, kb, kb * P:],
                                           start=(kb == 0), stop=(kb == NB - 1), skip_group_check=True)
                    mm.then_inc(once("mla_pv"), 1)
            mla_y(7)
            for k in range(1, 4):
                one_panel(FIRST["mga"][0] + k, (FIRST["mga"][0] + k) % 2)
            gemm("ap", RH, OLO, ready=(once("o_split"), 0))
            gemm_sums("out2", "n6", GA, ready=(once("m_split"), 0))

        @block.scalar
        def _(act):
            step_ = Count(act_step)

            def hi(p, s, turn):
                act.wait_ge(raw_in[s], turn * 16 + 16)
                act.activation(WH[:, s].rearrange("p a b -> p (a b)"), RAW[:, s, :], ACT.Copy).then_inc(w_hi, 1)

            def hi_ahead(p):
                act.wait_ge(panel_done, p + 1)
                if p + 2 < NPANELS:
                    hi(p + 2, p % 2, (p + 2) // 2)

            def hi_stage(name, skip=0):
                p0, n = FIRST[name]
                q0 = p0 + skip
                with act.Fori(0, (n - skip) // 2) as i:
                    for b in range(2):
                        act.wait_ge(panel_done, i * 2 + (q0 + b + 1))
                        hi(None, (q0 + b) % 2, i + (q0 + b + 2) // 2)
                if (n - skip) % 2:
                    hi_ahead(p0 + n - 1)

            def hi_squares(name, norm, dst, src):
                p0 = FIRST[name][0]
                for k in range(4):
                    hi_ahead(p0 + k)
                    if k == 3:
                        act.activation(ES[:, 0:1], EPST, ACT.Ln)
                    act.wait_ge(evac, p0 + k + 1)
                    act.activation(dst[:, 2 * k:2 * k + 2, :], src[:, 2 * k:2 * k + 2, :], ACT.Square)\
                        .then_inc(once(norm + "_sq"), 1)

            def factor(name, dst, bank=1, count=1):
                act.wait_ge(once(name + "_sum"), count)
                step_(act.activation(dst, PX[:, bank, :], ACT.Ln, bias=EPST))
                act.wait_ge(act_step, step_.n)
                act.activation(dst, dst, ACT.Exp, scale=-0.5).then_inc(once(name + "_r"), 1)

            def squares(name, dst, src):
                for k in range(4):
                    act.activation(dst[:, 2 * k:2 * k + 2, :], src[:, 2 * k:2 * k + 2, :], ACT.Square)\
                        .then_inc(once(name + "_sq"), 1)

            def split(name, ready, src, cname=None, dst=XH, tiles=range(DC)):
                for c in tiles:
                    if ready is not None:
                        act.wait_ge(once(ready), c + 1)
                    if cname is None:
                        act.activation(dst[:, c, :], src[:, c, :], ACT.Copy).then_inc(once(name), 1)
                    else:
                        act.activation(dst[:, c, :], src[:, c, :], ACT.Copy, scale=col(cname, c)).then_inc(once(name), 1)

            for k in (1, 3):
                act.dma_start(XT[:, 2 * k:2 * k + 2, :], xT_chunks(k)).then_inc(loaded_x[k], 16)
            hi(0, 0, 0)
            act.wait_ge(loaded_c, 16)
            for k in range(4):
                act.wait_ge(loaded_x[k], 16)
                for c in (2 * k, 2 * k + 1):
                    act.activation(XH[:, c, :], XT[:, c, :], ACT.Copy, scale=col("attn_pre", c)).then_inc(once("x1_hi"), 1)
            hi(1, 1, 0)
            squares("n1", SQ1, XT)
            act.wait_ge(once("lam_dot"), 2)
            act.activation(LDOT, LDOT, ACT.Exp).then_inc(once("lam_exp"), 1)
            act.wait_ge(once("lru_abs"), 1)
            act.activation(SP[:, 8:16], SP[:, 0:8], ACT.Exp, scale=-1.0).then_inc(once("lru_exp"), 1)
            act.wait_ge(once("eps_set"), 1)
            factor("n1", R[:])
            hi_stage("in1")

            def copy_values(t, bank):
                act.wait_ge(once("v_turned"), t + 1)
                dst = VA[:].rearrange("p a b -> p (a b)") if t == 0 else VB[:, t - 1].rearrange("p a b -> p (a b)")
                act.activation(dst, PX[:, bank, :], ACT.Copy).then_inc(once("v_copied"), 1)

            for t in range(3):
                copy_values(t, t % 2)

            def swa_exp(h):
                act.wait_ge(once("swa_negmax"), h + 1)
                s = h % 3
                for qb in range(NB):
                    act.activation(PSW[:, s, qb, :], PSW[:, s, qb, :], ACT.Exp, bias=NM[:, 4 * s + qb:4 * s + qb + 1],
                                   scale=SCALE, accum_out=DEN[:, 4 * s + qb:4 * s + qb + 1])
                if h >= 1:
                    act.wait_ge(once("swa_den"), h)
                act.activation(ES, NM[:, 4 * s:4 * s + 4], ACT.Exp, bias=col("sinks", h)).then_inc(once("swa_exp"), 1)

            def swa_copy(h):
                act.wait_ge(once("swa_turned"), h + 1)
                if h >= 2:
                    act.wait_ge(once("swa_pv"), h - 1)
                s = h % 2
                act.activation(PTW[s][:, 0:2, :], PX[:, 0, :].rearrange("p (a b) -> p a b", b=256), ACT.Copy)
                act.activation(PTW[s][:, 2:4, :].rearrange("p a b -> p (a b)")[:, 0:384], PX[:, 1, 0:384], ACT.Copy)\
                    .then_inc(once("swa_copied"), 1)

            swa_exp(0)
            for h in range(8):
                if h + 1 < 8:
                    swa_exp(h + 1)
                swa_copy(h)

            def unit_exp(pre, buf, u, qb):
                n = (qb + 1) * P
                act.wait_ge(once(pre + "_negmax"), u + 1)
                s = u % 3
                for m in range(2):
                    ins = act.activation(buf[s][:, m, 0:n], buf[s][:, m, 0:n], ACT.Exp,
                                         bias=NM3[:, 2 * s + m:2 * s + m + 1], scale=SCALE,
                                         accum_out=DEN3[:, 2 * s + m:2 * s + m + 1])
                ins.then_inc(once(pre + "_exp"), 1)

            def unit_copy(pre, dst, u, qb, maps):
                act.wait_ge(once(pre + "_turned"), u + 1)
                for m in range(maps):
                    ins = act.activation(dst(m, qb), PX[:, m, 0:(qb + 1) * P].rearrange("p (a b) -> p a b", b=P), ACT.Copy)
                ins.then_inc(once(pre + "_copied"), 1)

            def diff_dst(h):
                return lambda m, qb: PTD[:, h % 2, 0:qb + 1, qb * P:(qb + 1) * P]

            def mix_square(k):
                if k >= 1:
                    act.wait_ge(once("diff_out"), k)
                for c in range(4) if k == 0 else [3 + k]:
                    act.activation(MSQ[:, c, :], MIX[:, c, :], ACT.Square).then_inc(once("mix_sq"), 1)

            def mix_hi(k):
                for c in range(4) if k == 0 else [3 + k]:
                    act.wait_ge(once("mix_y"), c + 1)
                    act.activation(XH[:, c, :], MIX[:, c, :], ACT.Copy).then_inc(once("mix_hi"), 1)

            unit_exp("diff", PD, 0, 0)
            for u in range(16):
                h, qb = divmod(u, NB)
                if u + 1 < 16:
                    unit_exp("diff", PD, u + 1, (u + 1) % NB)
                if h >= 2 and qb == 0:
                    act.wait_ge(once("diff_pv"), h - 1)
                unit_copy("diff", diff_dst(h), u, qb, 1)
                if u == 8:
                    hi_ahead(FIRST["in1v"][0])
                if u in (9, 10):
                    copy_values(u - 6, 3)
                if u == 9:
                    mix_hi(0)
                if h >= 2 and qb == 1:
                    mix_hi(h - 1)
                if qb == 3:
                    factor("mix", MR[:], 1, h + 1)
                if qb == 1:
                    if h == 0:
                        act.wait_ge(once("swa_out"), 8)
                    mix_square(h)
            mix_hi(3)
            mix_square(4)
            factor("mix", MR[:], 1, 5)
            mix_hi(4)
            hi_squares("out1", "n2", SQY, Y1)
            factor("n2", R[:])
            split("x2_hi", "x2_new", XT, "ffn_pre")
            squares("n3", SQY, XT)
            factor("n3", R[:])

            def up(q):
                p0 = FIRST[f"up{q}"][0]

                def conv0(c, k, b, p):
                    act.wait_ge(evac, p + 1)
                    for m in range(2):
                        ins = act.activation(C[:, b, m, :], U[:, b, m, :], ACT.Identity,
                                             bias=col("cb", k + 32 * m), scale=col("cw2", k + 32 * m))
                    ins.then_inc(once("conv0"), 1)

                def a_hi(c, n, b):
                    act.wait_ge(once("a_ready"), n)
                    act.activation(AH[:, q % 2, c, :] if isinstance(c, int) else
                                   AH[:, q % 2, bass.ds(c, 1), :].rearrange("p a n -> p (a n)"),
                                   Z[:, b, :], ACT.Copy).then_inc(once("a_hi"), 1)

                def tanh(n, b):
                    act.wait_ge(once("inner"), n)
                    act.activation(Z[:, b, :], Z[:, b, :], ACT.Tanh, scale=0.7978845608028654).then_inc(once("tanh"), 1)

                def panel(i, b, first):
                    p = i * 2 + (p0 + b)
                    c = i * 2 + b
                    n = c + 8 * q
                    act.wait_ge(panel_done, p + 1)
                    hi(None, (p0 + b) % 2, i + (p0 + b + 2) // 2)
                    conv0(c, n, b, p)
                    if not first:
                        a_hi(c - 1, n, 1 - b)
                    tanh(n + 1, b)

                panel(0, 0, True)
                panel(0, 1, False)
                with act.Fori(1, 4) as i:
                    panel(i, 0, False)
                    panel(i, 1, False)
                a_hi(7, 8 * q + 8, 1)

            up(0)
            up(1)
            hi_stage("dn0")
            up(2)
            hi_stage("dn1")
            up(3)
            hi_stage("dn2")
            hi_squares("dn3", "n4", SQF, FA)
            factor("n4", R[:])
            split("x3_hi", "x3_new", XT, "norm2")
            act.dma_start(WIR[:], wi_in).then_inc(loaded_wi, 16)
            squares("n5", SQF, XT)
            act.dma_start(spill, XT[:]).then_inc(spilled, 16)
            factor("n5", R[:])
            act.wait_ge(loaded_wi, 16)
            act.activation(WIH[:], WIR[:], ACT.Copy).then_inc(once("wi_hi"), 1)
            p0 = FIRST["in2a"][0]
            for t in range(7):
                hi_ahead(p0 + t)
                if t == 1:
                    act.wait_ge(evac, p0 + 1)
                    act.activation(CSQ[:, 0, :], CKV[:, 0, :], ACT.Square).then_inc(once("kv_sq"), 1)
                if t == 2:
                    factor("kv", CSQ[:, 0, :])
                    act.wait_ge(once("ln_x"), 1)
                    act.activation(CSQ[:, 1, :], KC[:], ACT.Square).then_inc(once("ln_sq"), 1)
                if t == 3:
                    factor("ln", CSQ[:, 1, :], 2)
                    act.wait_ge(evac, p0 + 3)
                    act.activation(QIH[:], QI[:], ACT.Copy).then_inc(once("qi_hi"), 1)
                if t == 5:
                    act.wait_ge(once("ki_done"), 1)
                    act.activation(KIH[:], CKV[:, 1, :], ACT.Copy).then_inc(once("ki_hi"), 1)
                if t == 4:
                    act.wait_ge(once("kv_turned"), 1)
                    act.activation(CKT[:].rearrange("p a b -> p (a b)"), PX[:, 0, :], ACT.Copy).then_inc(once("kv_copied"), 1)
            act.wait_ge(once("x3_split"), 8)
            act.wait_ge(spilled, 16)
            act.dma_start(RGW[:], rgw_in).then_inc(loaded_b2, 16)
            act.dma_start(UK[:], uk_in).then_inc(loaded_b2, 16)
            act.dma_start(UV[:], uv_in).then_inc(loaded_b2, 16)
            act.wait_ge(evac, FIRST["xr"][0])
            act.wait_ge(once("idx_split"), 2)
            act.activation(CKH[:], CKV[:, 0, :], ACT.Copy).then_inc(once("ck_hi"), 1)
            for u in range(24):
                n = (u // 8 + 2) * P
                act.wait_ge(once("idx_s"), u + 1)
                if u >= 2:
                    act.wait_ge(once("idx_acc"), u - 1)
                act.activation(RLU[:, u % 2, 0:n], PG[:, u % 4, 0:n], ACT.Relu).then_inc(once("idx_relu"), 1)

            def conv0(t):
                if t >= 2:
                    act.wait_ge(once("rg_ix"), t - 1)
                for m in range(2):
                    act.activation(XC[:, t % 2, m, :], XR[:, 2 * t + m, :], ACT.Identity, bias=col("rb", 2 * t + m),
                                   scale=col("rw", 24 + 2 * t + m)).then_inc(once("rg_conv0"), 1)

            def y_hi(t):
                act.wait_ge(once("rg_y"), t + 1)
                act.activation(RH[:, 2 * t:2 * t + 2, :], RGT[:, 1], ACT.Copy).then_inc(once("rg_hi"), 1)

            p0 = FIRST["xr"][0]
            for t in range(4):
                hi_ahead(p0 + t)
                if t == 1:
                    act.wait_ge(evac, p0 + 1)
                    conv0(0)
            p0 = FIRST["rg"][0]
            for t in range(4):
                r_, i_, a_, m_ = (RGT[:, k] for k in range(4))
                if t >= 1:
                    y_hi(t - 1)
                if t < 3:
                    act.wait_ge(evac, FIRST["xr"][0] + t + 2)
                    conv0(t + 1)
                act.wait_ge(once("rg_proj"), t + 1)
                for m in range(2):
                    step_(act.activation(r_[:, m, :], PX[:, m, :], ACT.Tanh, bias=HALF_B[:, 2 * t + m:2 * t + m + 1], scale=0.5))
                if t >= 1:
                    act.wait_ge(once("rg_lo"), 2 * t)
                for m in range(2):
                    ins = act.activation(i_[:, m, :], PX[:, 2 + m, :], ACT.Tanh,
                                         bias=HALF_B[:, 8 + 2 * t + m:8 + 2 * t + m + 1], scale=0.5)
                ins.then_inc(once("rg_ti"), 1)
                act.wait_ge(act_step, step_.n)
                for m in range(2):
                    c = slice(2 * t + m, 2 * t + m + 1)
                    ins = act.activation(a_[:, m, :], r_[:, m, :], ACT.Exp, bias=NEG_SP4[:, c], scale=NEG_SP4[:, c])
                ins.then_inc(once("rg_a"), 1)
                act.wait_ge(once("rg_a"), t + 1)
                for m in range(2):
                    c = slice(2 * t + m, 2 * t + m + 1)
                    ins = act.activation(r_[:, m, :], r_[:, m, :], ACT.Tanh, bias=POS_SP4[:, c], scale=POS_SP4[:, c])
                ins.then_inc(once("rg_tanh"), 1)
                act.wait_ge(once("rg_m"), t + 1)
                act.activation(m_, m_, ACT.Sqrt).then_inc(once("rg_sqrt"), 1)
                hi_ahead(p0 + 2 * t)
                act.wait_ge(evac, p0 + 2 * t + 1)
                act.activation(r_, GR[:, 2 * t:2 * t + 2, :], ACT.Tanh, scale=0.5).then_inc(once("rg_tg"), 1)
                hi_ahead(p0 + 2 * t + 1)
            y_hi(3)

            p0 = FIRST["wr"][0]
            act.wait_ge(evac, p0)
            for t in range(4):
                for m in range(2):
                    ins = act.activation(GA[:, 2 * t + m, :], GA[:, 2 * t + m, :], ACT.Sigmoid, bias=col("b_merge", 8 + 2 * t + m))
                ins.then_inc(once("mr_sg"), 1)
                hi_ahead(p0 + t)
            def tanh_ga(k):
                act.wait_ge(evac, FIRST["ga"][0] + k + 1)
                act.activation(SGA[:], GA[:, 2 * k:2 * k + 2, :], ACT.Tanh, scale=0.5).then_inc(once("sig_ga"), 1)

            def ql_hi(g):
                act.wait_ge(once("mla_ql"), g + 1)
                if g >= 1:
                    act.wait_ge(once("mla_s"), 4 * g)
                act.activation(QLH[:], PX[:, 2:4, :], ACT.Copy).then_inc(once("mla_qh"), 1)

            ql_hi(0)
            hi_ahead(FIRST["ga"][0])
            tanh_ga(0)
            unit_exp("mla", PM, 0, 0)
            for u in range(32):
                g, qb = divmod(u, NB)
                if qb == 2 and g < 7:
                    ql_hi(g + 1)
                if u + 1 < 32:
                    unit_exp("mla", PM, u + 1, (u + 1) % NB)
                if qb == 0 and g >= 1:
                    act.wait_ge(once("mla_pv"), g)
                unit_copy("mla", lambda m, q: PTM[:, m, 0:q + 1, q * P:(q + 1) * P], u, qb, 2)
                if u % 8 == 0 and u >= 8:
                    hi_ahead(FIRST["ga"][0] + u // 8)
                if u % 8 == 1 and u >= 8:
                    tanh_ga(u // 8)
            hi_ahead(FIRST["mga"][0])
            act.wait_ge(once("mla_y"), 8)
            split("o_hi", None, GA, None, RH)
            p0 = FIRST["mga"][0]
            for t in range(4):
                if t >= 1:
                    hi_ahead(p0 + t)
                act.wait_ge(evac, p0 + t + 1)
                for m in range(2):
                    ins = act.activation(MGA[t][:, m, :], MGA[t][:, m, :], ACT.Sigmoid, bias=col("b_merge", 2 * t + m))
                ins.then_inc(once("ma_sg"), 1)
            p0 = FIRST["ap"][0]
            for t in range(4):
                hi_ahead(p0 + t)
                split("m_hi", "m_ready", M2, tiles=(2 * t, 2 * t + 1))
                if t == 0:
                    act.dma_start(XT[:], spill).then_inc(reloaded, 16)
            hi_squares("out2", "n6", GA, M2)
            factor("n6", R[:])

        @block.vector
        def _(dve):
            step_ = Count(dve_step)

            def link(ins):
                step_(ins)
                dve.wait_ge(dve_step, step_.n)

            def add_pairs(name, sq, last):
                for k in range(1, last + 1):
                    dve.wait_ge(once(name + "_sq"), k + 1)
                    ins = dve.tensor_tensor(sq[:, 0:2, :], sq[:, 0:2, :], sq[:, 2 * k:2 * k + 2, :], ALU.add)
                    if k < last:
                        link(ins)
                ins.then_inc(once(name + "_acc"), 1)

            def split(name, hi_name, src, cname=None, dh=XH, dl=XL, tiles=range(DC)):
                for c in tiles:
                    dve.wait_ge(once(hi_name), c + 1)
                    if cname is None:
                        ins = dve.tensor_tensor(dl[:, c, :], src[:, c, :], dh[:, c, :].bitcast(F32), ALU.subtract)
                    else:
                        ins = dve.scalar_tensor_tensor(out=dl[:, c, :], in0=src[:, c, :], scalar=col(cname, c),
                                                       in1=dh[:, c, :].bitcast(F32), op0=ALU.mult, op1=ALU.subtract)
                    ins.then_inc(once(name), 1)

            def psum_of(p0b):
                s = p0b % 2
                return PG[:, 2 * s:2 * s + 2, :]

            def evac_sums(name, norm, sq, out):
                p0 = FIRST[name][0]
                for k in range(4):
                    dve.wait_ge(panel_done, p0 + k + 1)
                    out(k, psum_of(p0 + k), k % 2).then_inc(evac, 1)
                    if k == 2:
                        add_pairs(norm, sq, 2)

            def evac_stage(name, out, p0=None):
                p0, n = FIRST[name]

                def step(p, k, b, i):
                    dve.wait_ge(panel_done, p + 1)
                    out(k, psum_of(p0 + b), b).then_inc(evac, 1)

                pairs(dve, name, step)

            def two(buf, k, off=0):
                if isinstance(k, int):
                    return buf[:, 2 * k + off:2 * k + off + 2, :]
                return buf[:, bass.ds(k * 2 + off, 2), :]

            def rr():
                return R[:].rearrange("p (a n) -> p a n", a=1).broadcast_to([P, 2, S])

            dve.memset(EPST, EPS).then_inc(once("eps_set"), 1)
            dve.wait_ge(loaded_c, 16)
            split("x1_split", "x1_hi", XT, "attn_pre")
            add_pairs("n1", SQ1, 3)
            step_(dve.tensor_scalar(SUBLN, col("subln", 0), 1.0 - LAMBDA_INIT, None, ALU.mult))
            dve.wait_ge(loaded_lam, 16)
            for k in range(2):
                dve.tensor_tensor_reduce(out=R[:, k * HD:(k + 1) * HD], in0=LV[:, 2 * k, :], in1=LV[:, 2 * k + 1, :], scale=1.0,
                                         scalar=0.0, op0=ALU.mult, op1=ALU.add, accum_out=LDOT[:, k:k + 1])\
                    .then_inc(once("lam_dot"), 1)
            lru = col("lru", 0, 8)
            link(dve.tensor_scalar(SP[:, 0:8], lru, -1.0, None, ALU.mult))
            dve.tensor_tensor(SP[:, 0:8], SP[:, 0:8], lru, ALU.max).then_inc(once("lru_abs"), 1)
            dve.tensor_scalar(SINK8, col("sinks", 0, 8), 1.0 / SCALE, None, ALU.mult).then_inc(dve_step, 1)
            step_.n += 1
            dve.wait_ge(once("lam_exp"), 1)
            link(dve.tensor_scalar(LDOT[:, 0:1], LDOT[:, 0:1], LAMBDA_INIT, None, ALU.add))
            link(dve.tensor_tensor(LAM, LDOT[:, 0:1], LDOT[:, 1:2], ALU.subtract))
            dve.wait_ge(once("lru_exp"), 1)
            link(dve.tensor_scalar(SP[:, 0:8], SP[:, 8:16], 2.0, None, ALU.add))
            link(dve.reciprocal(SP[:, 0:8], SP[:, 0:8]))
            link(dve.tensor_tensor(SP[:, 0:8], SP[:, 0:8], SP[:, 8:16], ALU.mult))
            link(dve.tensor_tensor(SP[:, 8:16], SP[:, 0:8], SP[:, 0:8], ALU.mult))
            link(dve.tensor_scalar(SP[:, 16:24], SP[:, 8:16], 1.0 / 17, 1.0 / 15, ALU.mult, ALU.add))
            for d in (13, 11, 9, 7, 5, 3, 1):
                link(dve.tensor_tensor(SP[:, 16:24], SP[:, 16:24], SP[:, 8:16], ALU.mult))
                link(dve.tensor_scalar(SP[:, 16:24], SP[:, 16:24], 1.0 / d, None, ALU.add))
            link(dve.tensor_tensor(SP[:, 16:24], SP[:, 16:24], SP[:, 0:8], ALU.mult))
            link(dve.tensor_scalar(SP[:, 8:16], lru, -1.0, 0.0, ALU.mult, ALU.max))
            link(dve.scalar_tensor_tensor(out=SP[:, 0:8], in0=SP[:, 16:24], scalar=2.0, in1=SP[:, 8:16],
                                          op0=ALU.mult, op1=ALU.add))
            step_(dve.tensor_scalar(NEG_SP4, SP[:, 0:8], -4.0, None, ALU.mult))
            step_(dve.tensor_scalar(HALF_B, COL[:, COLS["b_rg_a"]:COLS["b_rg_a"] + 16], 0.5, None, ALU.mult))
            link(dve.tensor_scalar(POS_SP4, SP[:, 0:8], 4.0, None, ALU.mult))
            dve.wait_ge(once("n1_r"), 1)

            evac_stage("in1", lambda k, ps, b: dve.tensor_tensor(two(PROJ, k), ps, rr(), ALU.mult))

            def swa_logits(h):
                s, slot = h % 3, h % 2
                dve.wait_ge(once("swa_s"), h + 1)
                if h >= 3:
                    dve.wait_ge(once("swa_turned"), h - 2)
                dve.scalar_tensor_tensor(out=PSW[:, s].rearrange("p a b -> p (a b)"), in0=DS4[:].rearrange("p a b -> p (a b)"),
                                         scalar=-SLOPES_1[h] / SCALE,
                                         in1=PG[:, 2 * slot:2 * slot + 2, :].rearrange("p a b -> p (a b)"),
                                         op0=ALU.mult, op1=ALU.add).then_inc(once("swa_logits"), 1)
                dve.wait_ge(once("swa_logits"), h + 1)
                link(dve.tensor_reduce(MX, PSW[:, s], AX_X, ALU.max))
                dve.tensor_scalar(NM[:, 4 * s:4 * s + 4], MX, SINK8[:, h:h + 1], -SCALE, ALU.max, ALU.mult)\
                    .then_inc(once("swa_negmax"), 1)

            def swa_probs(h):
                s = h % 3
                den = DEN[:, 4 * s:4 * s + 4]
                dve.wait_ge(once("swa_exp"), h + 1)
                dve.tensor_tensor(den, den, ES, ALU.add).then_inc(once("swa_den"), 1)
                dve.wait_ge(once("swa_den"), h + 1)
                link(dve.reciprocal(den, den))
                for qb in range(NB):
                    ins = dve.tensor_scalar(PSW[:, s, qb, :], PSW[:, s, qb, :], den[:, qb:qb + 1], None, ALU.mult)
                ins.then_inc(once("swa_probs"), 1)

            def swa_out(h):
                g, j = divmod(h, SWA_PAIRS)
                rows = slice(g * HD, (g + 1) * HD)
                dve.wait_ge(once("swa_pv"), h + 1)
                dve.tensor_copy(MIX[rows, j, :], PX[rows, 2 + h % 2, :]).then_inc(once("swa_out"), 1)

            dve.wait_ge(consts, 11)
            swa_logits(0)
            swa_logits(1)
            swa_probs(0)
            for h in range(8):
                if h + 2 < 8:
                    swa_logits(h + 2)
                if h + 1 < 8:
                    swa_probs(h + 1)
                if h >= 1:
                    swa_out(h - 1)
            swa_out(7)

            def unit_logits(pre, buf, u, qb, dist, slopes, slot):
                s, n = u % 3, (qb + 1) * P
                dve.wait_ge(once(pre + "_s"), u + 1)
                if u >= 3:
                    dve.wait_ge(once(pre + "_turned"), u - 2)
                for m in range(2):
                    ins = dve.scalar_tensor_tensor(out=buf[s][:, m, 0:n], in0=dist, scalar=-slopes[m] / SCALE,
                                                   in1=PG[:, 2 * slot + m, 0:n], op0=ALU.mult, op1=ALU.add)
                ins.then_inc(once(pre + "_logits"), 1)
                dve.wait_ge(once(pre + "_logits"), u + 1)
                link(dve.tensor_reduce(MX[:, 0:2], buf[s][:, :, 0:n], AX_X, ALU.max))
                dve.tensor_scalar(NM3[:, 2 * s:2 * s + 2], MX[:, 0:2], -SCALE, None, ALU.mult).then_inc(once(pre + "_negmax"), 1)

            def diff_probs(u, qb):
                s, n = u % 3, (qb + 1) * P
                den = DEN3[:, 2 * s:2 * s + 2]
                dve.wait_ge(once("diff_exp"), u + 1)
                link(dve.reciprocal(den, den))
                link(dve.tensor_scalar(RTL, den[:, 1:2], LAM, None, ALU.mult))
                link(dve.tensor_scalar(PD[s][:, 1, 0:n], PD[s][:, 1, 0:n], RTL, None, ALU.mult))
                dve.scalar_tensor_tensor(out=PD[s][:, 0, 0:n], in0=PD[s][:, 0, 0:n], scalar=den[:, 0:1],
                                         in1=PD[s][:, 1, 0:n], op0=ALU.mult, op1=ALU.subtract).then_inc(once("diff_probs"), 1)

            def diff_logits(u):
                h, qb = divmod(u, NB)
                s, n = u % 3, (qb + 1) * P
                if qb == 0:
                    link(dve.tensor_scalar(DH[:, h % 2, :], EC[:], -SLOPES_1[8 + h] / SCALE, None, ALU.mult))
                dve.wait_ge(once("diff_s"), u + 1)
                if u >= 3:
                    dve.wait_ge(once("diff_turned"), u - 2)
                    dve.wait_ge(once("diff_negmax"), u - 2)
                for m in range(2):
                    dve.tensor_tensor_reduce(out=PD[s][:, m, 0:n], in0=DH[:, h % 2, (3 - qb) * P:], in1=PG[:, 2 + m, 0:n],
                                             scale=1.0, scalar=-3e38, op0=ALU.add, op1=ALU.max,
                                             accum_out=MX3[:, 2 * s + m:2 * s + m + 1]).then_inc(once("diff_logits"), 1)
                dve.wait_ge(once("diff_logits"), 2 * u + 2)
                dve.tensor_scalar(NM3[:, 2 * s:2 * s + 2], MX3[:, 2 * s:2 * s + 2], -SCALE, None, ALU.mult).then_inc(once("diff_negmax"), 1)

            def mix_scale(k):
                dve.wait_ge(once("mix_r"), k + 1)
                for c in range(4) if k == 0 else [3 + k]:
                    dve.scalar_tensor_tensor(out=MIX[:, c, :], in0=MIX[:, c, :],
                                             scalar=col("swa_out", c) if k == 0 else SUBLN,
                                             in1=MR[:], op0=ALU.mult, op1=ALU.mult).then_inc(once("mix_y"), 1)

            def mix_lo(k):
                for c in range(4) if k == 0 else [3 + k]:
                    dve.wait_ge(once("mix_hi"), c + 1)
                    dve.tensor_tensor(XL[:, c, :], MIX[:, c, :], XH[:, c, :].bitcast(F32), ALU.subtract)\
                        .then_inc(once("mix_split"), 1)

            def diff_out(h):
                dve.wait_ge(once("diff_pv"), h + 1)
                dve.tensor_copy(MIX[:, 4 + h, :], PX[:, 2, :]).then_inc(once("diff_out"), 1)

            diff_logits(0)
            diff_logits(1)
            diff_probs(0, 0)
            for u in range(16):
                h, qb = divmod(u, NB)
                if u + 2 < 16:
                    diff_logits(u + 2)
                if u + 1 < 16:
                    diff_probs(u + 1, (u + 1) % NB)
                if h >= 1 and qb == 0:
                    mix_scale(h - 1)
                    diff_out(h - 1)
                if u == 8:
                    dve.wait_ge(panel_done, FIRST["in1v"][0] + 1)
                    dve.tensor_tensor(two(PROJ, 8), psum_of(FIRST["in1v"][0]), rr(), ALU.mult).then_inc(evac, 1)
                if u == 9:
                    mix_lo(0)
                if h >= 2 and qb == 1:
                    mix_lo(h - 1)
            mix_scale(3)
            diff_out(3)
            mix_lo(3)
            mix_scale(4)
            mix_lo(4)
            evac_sums("out1", "n2", SQY, lambda k, ps, b: dve.tensor_scalar(two(Y1, k), ps, 1.0, None, ALU.mult))

            def post(name, y, cname, new, hi_name, lo_name, gain):
                dve.wait_ge(once(name + "_r"), 1)
                base = step_.n
                for c in range(DC + 3):
                    if c < DC:
                        step_(dve.scalar_tensor_tensor(out=y[:, c, :], in0=y[:, c, :], scalar=col(cname, c),
                                                       in1=R[:], op0=ALU.mult, op1=ALU.mult))
                    if 1 <= c <= DC:
                        dve.wait_ge(dve_step, base + c)
                        dve.tensor_tensor(XT[:, c - 1, :], XT[:, c - 1, :], y[:, c - 1, :], ALU.add).then_inc(once(new), 1)
                    if c >= 3:
                        k = c - 3
                        dve.wait_ge(once(hi_name), k + 1)
                        dve.scalar_tensor_tensor(out=XL[:, k, :], in0=XT[:, k, :], scalar=col(gain, k),
                                                 in1=XH[:, k, :].bitcast(F32), op0=ALU.mult, op1=ALU.subtract)\
                            .then_inc(once(lo_name), 1)

            post("n2", Y1, "attn_post", "x2_new", "x2_hi", "x2_split", "ffn_pre")
            add_pairs("n3", SQY, 3)
            dve.wait_ge(once("n3_r"), 1)

            def up(q):
                p0 = FIRST[f"up{q}"][0]

                def one(buf, c):
                    return buf[:, q % 2, c, :] if isinstance(c, int) else \
                        buf[:, q % 2, bass.ds(c, 1), :].rearrange("p a n -> p (a n)")

                def a_mult(n, b):
                    dve.wait_ge(once("tanh"), n)
                    link(dve.scalar_tensor_tensor(out=Z[:, b, :], in0=Z[:, b, :], scalar=1.0, in1=C[:, b, 0, :],
                                                  op0=ALU.add, op1=ALU.mult))
                    dve.scalar_tensor_tensor(out=Z[:, b, :], in0=Z[:, b, :], scalar=0.5, in1=C[:, b, 1, :],
                                             op0=ALU.mult, op1=ALU.mult).then_inc(once("a_ready"), 1)

                def a_lo(c, n, b):
                    dve.wait_ge(once("a_hi"), n)
                    dve.tensor_tensor(one(AL, c), Z[:, b, :], one(AH, c).bitcast(F32), ALU.subtract)\
                        .then_inc(once("a_lo"), 1)

                def panel(i, b, first):
                    p = i * 2 + (p0 + b)
                    c = i * 2 + b
                    n = c + 8 * q
                    dve.wait_ge(panel_done, p + 1)
                    dve.tensor_tensor(U[:, b], psum_of(p0 + b), rr(), ALU.mult).then_inc(evac, 1)
                    if not first:
                        a_mult(n, 1 - b)
                    dve.wait_ge(evac, p + 1)
                    dve.wait_ge(once("conv0"), n + 1)
                    for m in range(2):
                        step_(dve.scalar_tensor_tensor(out=C[:, b, m, 1:], in0=U[:, b, m, 0:S - 1], scalar=col("cw1", n + 32 * m),
                                                       in1=C[:, b, m, 1:], op0=ALU.mult, op1=ALU.add))
                    dve.wait_ge(dve_step, step_.n)
                    for m in range(2):
                        step_(dve.scalar_tensor_tensor(out=C[:, b, m, 2:], in0=U[:, b, m, 0:S - 2], scalar=col("cw0", n + 32 * m),
                                                       in1=C[:, b, m, 2:], op0=ALU.mult, op1=ALU.add))
                    dve.wait_ge(dve_step, step_.n)
                    link(dve.scalar_tensor_tensor(out=Z[:, b, :], in0=C[:, b, 0, :], scalar=0.044715, in1=C[:, b, 0, :],
                                                  op0=ALU.mult, op1=ALU.mult))
                    dve.scalar_tensor_tensor(out=Z[:, b, :], in0=Z[:, b, :], scalar=1.0, in1=C[:, b, 0, :],
                                             op0=ALU.add, op1=ALU.mult).then_inc(once("inner"), 1)
                    if not first:
                        a_lo(c - 1, n, 1 - b)

                panel(0, 0, True)
                panel(0, 1, False)
                base, per = step_.n, 12
                with dve.Fori(1, 4) as i:
                    step_.n = i * per + (base - per)
                    panel(i, 0, False)
                    panel(i, 1, False)
                step_.n = base + 3 * per
                a_mult(8 * q + 8, 1)
                a_lo(7, 8 * q + 8, 1)

            up(0)
            up(1)
            evac_stage("dn0", lambda k, ps, b: dve.tensor_scalar(two(FA, k), ps, 1.0, None, ALU.mult))
            add_f = lambda k, ps, b: dve.tensor_tensor(two(FA, k), ps, two(FA, k), ALU.add)
            up(2)
            evac_stage("dn1", add_f)
            up(3)
            evac_stage("dn2", add_f)
            evac_sums("dn3", "n4", SQF, add_f)
            post("n4", FA, "ffn_post", "x3_new", "x3_hi", "x3_split", "norm2")
            add_pairs("n5", SQF, 3)
            dve.wait_ge(once("n5_r"), 1)

            p0 = FIRST["in2a"][0]
            for t in range(7):
                if t == 1:
                    dve.wait_ge(once("wi_hi"), 1)
                    dve.tensor_tensor(WIL[:], WIR[:], WIH[:].bitcast(F32), ALU.subtract).then_inc(once("wi_split"), 2)
                dve.wait_ge(panel_done, p0 + t + 1)
                dst = CKV[:] if t == 0 else two(QI, t - 1) if t < 3 else two(QT, t - 3)
                dve.tensor_tensor(dst, psum_of(p0 + t), rr(), ALU.mult).then_inc(evac, 1)
                if t == 2:
                    dve.wait_ge(once("wx_ready"), 1)
                    dve.scalar_tensor_tensor(out=WXT[0:8, :], in0=PX[0:8, 0, :], scalar=IDX_HEADS ** -0.5 * HD ** -0.5,
                                             in1=R[0:8, :], op0=ALU.mult, op1=ALU.mult).then_inc(once("wxt"), 1)
                    dve.wait_ge(once("ln_mean"), 1)
                    dve.wait_ge(evac, p0 + 1)
                    dve.scalar_tensor_tensor(out=KC[:], in0=PX[:, 3, :], scalar=-1.0, in1=CKV[:, 1, :],
                                             op0=ALU.mult, op1=ALU.add).then_inc(once("ln_x"), 1)
                    dve.wait_ge(once("kv_r"), 1)
                    dve.scalar_tensor_tensor(out=CKV[:, 0, :], in0=CKV[:, 0, :], scalar=col("kv_norm", 0), in1=CSQ[:, 0, :],
                                             op0=ALU.mult, op1=ALU.mult).then_inc(once("kv_done"), 1)
                if t == 4:
                    dve.wait_ge(once("ln_r"), 1)
                    dve.wait_ge(once("ln_x"), 1)
                    link(dve.scalar_tensor_tensor(out=KC[:], in0=KC[:], scalar=col("ln_g", 0), in1=CSQ[:, 1, :],
                                                  op0=ALU.mult, op1=ALU.mult))
                    dve.tensor_scalar(CKV[:, 1, :], KC[:], col("ln_b", 0), None, ALU.add).then_inc(once("ki_done"), 1)
                    dve.wait_ge(once("qi_hi"), 1)
                    dve.wait_ge(evac, p0 + 3)
                    dve.tensor_tensor(QIL[:], QI[:], QIH[:].bitcast(F32), ALU.subtract).then_inc(once("idx_split"), 1)
                if t == 6:
                    dve.wait_ge(once("ki_hi"), 1)
                    dve.wait_ge(once("ki_done"), 1)
                    dve.tensor_tensor(KIL[:], CKV[:, 1, :], KIH[:].bitcast(F32), ALU.subtract).then_inc(once("idx_split"), 1)
                if t == 5:
                    dve.wait_ge(once("wx_turned"), 1)
                    link(dve.tensor_scalar(WX, PX[:, 3, 0:32], 1.0, None, ALU.mult))
            OFF = {1: 0, 2: 256, 3: 640}
            for u in range(24):
                qb, j = u // 8 + 1, u % 8
                n = (qb + 1) * P
                acc = MD[:, OFF[qb]:OFF[qb] + n]
                if j == 0:
                    link(dve.tensor_scalar(acc, EC[:, (3 - qb) * P:], 1e29, -3e38, ALU.is_ge, ALU.mult))
                dve.wait_ge(once("idx_relu"), u + 1)
                dve.scalar_tensor_tensor(out=acc, in0=RLU[:, u % 2, 0:n], scalar=WX[:, 8 * qb + j:8 * qb + j + 1],
                                         in1=acc, op0=ALU.mult, op1=ALU.add).then_inc(once("idx_acc"), 1)
                dve.wait_ge(once("idx_acc"), u + 1)

            def settled():
                dve.wait_ge(dve_step, step_.n)
                dve.memset(WORD, 0.0)

            def topk_round():
                blocks = [(M8[:, 8 * qb - 8:8 * qb], MD[:, OFF[qb]:OFF[qb] + (qb + 1) * P]) for qb in (1, 2, 3)]
                for m8, w in blocks:
                    step_(dve.max(m8, w))
                settled()
                for m8, w in blocks:
                    step_(dve.match_replace(out=w, in_to_replace=m8, in_values=w, imm_value=-3.3e38))
                settled()

            dve.wait_ge(once("ck_hi"), 1)
            dve.tensor_tensor(CKL[:], CKV[:, 0, :], CKH[:].bitcast(F32), ALU.subtract).then_inc(once("ck_lo"), 1)

            def rg_conv(t):
                xc = XC[:, t % 2]
                dve.wait_ge(once("rg_conv0"), 2 * t + 2)
                for d in (1, 2, 3):
                    for m in range(2):
                        ins = dve.scalar_tensor_tensor(out=xc[:, m, d:], in0=XR[:, 2 * t + m, 0:S - d],
                                                       scalar=col("rw", (3 - d) * 8 + 2 * t + m), in1=xc[:, m, d:],
                                                       op0=ALU.mult, op1=ALU.add)
                        step_(ins) if d < 3 else ins.then_inc(once("rg_conv"), 1)
                    if d < 3:
                        dve.wait_ge(dve_step, step_.n)

            p0 = FIRST["xr"][0]
            for t in range(4):
                dve.wait_ge(panel_done, p0 + t + 1)
                dve.tensor_tensor(two(XR, t), psum_of(p0 + t), rr(), ALU.mult).then_inc(evac, 1)
                if t == 2:
                    rg_conv(0)
                for _ in range(2 if t == 2 else 3):
                    topk_round()

            p0 = FIRST["rg"][0]
            r_, i_, a_, m_ = (RGT[:, k] for k in range(4))

            def rg_y(t):
                tt = slice(2 * t, 2 * t + 2)
                dve.scalar_tensor_tensor(out=i_, in0=XR[:, tt, :], scalar=0.5, in1=GR[:, tt, :],
                                         op0=ALU.mult, op1=ALU.mult).then_inc(once("rg_y"), 1)

            def rg_lo(t):
                tt = slice(2 * t, 2 * t + 2)
                dve.wait_ge(once("rg_hi"), t + 1)
                dve.tensor_tensor(RL[:, tt, :], i_, RH[:, tt, :].bitcast(F32), ALU.subtract).then_inc(once("rg_lo"), 2)

            def mr_out(t):
                dve.wait_ge(panel_done, p0 + 2 * t + 2)
                dve.tensor_tensor(two(GA, t), psum_of(p0 + 1), rr(), ALU.mult).then_inc(evac, 1)

            for t in range(4):
                tt = slice(2 * t, 2 * t + 2)
                xc = XC[:, t % 2]
                if t >= 1:
                    rg_y(t - 1)
                if t < 3:
                    rg_conv(t + 1)
                if t >= 1:
                    rg_lo(t - 1)
                    mr_out(t - 1)
                dve.wait_ge(once("rg_conv"), 2 * t + 2)
                dve.wait_ge(once("rg_ti"), t + 1)
                dve.scalar_tensor_tensor(out=i_, in0=i_, scalar=1.0, in1=xc, op0=ALU.add, op1=ALU.mult)\
                    .then_inc(once("rg_ix"), 1)
                dve.wait_ge(once("rg_a"), t + 1)
                link(dve.tensor_tensor(m_, a_, a_, ALU.mult))
                dve.wait_ge(once("rg_tanh"), t + 1)
                dve.scalar_tensor_tensor(out=m_, in0=m_, scalar=1.0, in1=r_, op0=ALU.add, op1=ALU.mult)\
                    .then_inc(once("rg_m"), 1)
                topk_round()
                dve.wait_ge(once("rg_sqrt"), t + 1)
                dve.wait_ge(once("rg_ix"), t + 1)
                link(dve.scalar_tensor_tensor(out=i_, in0=i_, scalar=0.5, in1=m_, op0=ALU.mult, op1=ALU.mult))
                dve.wait_ge(panel_done, p0 + 2 * t + 1)
                dve.tensor_tensor(two(GR, t), psum_of(p0), rr(), ALU.mult).then_inc(evac, 1)
                for m in range(2):
                    step_(dve.tensor_tensor_scan(out=XR[:, 2 * t + m, :], data0=a_[:, m, :], data1=i_[:, m, :],
                                                 initial=0.0, op0=ALU.mult, op1=ALU.add))
                dve.wait_ge(evac, p0 + 2 * t + 1)
                dve.wait_ge(once("rg_tg"), t + 1)
                link(dve.scalar_tensor_tensor(out=GR[:, tt, :], in0=r_, scalar=1.0, in1=GR[:, tt, :],
                                              op0=ALU.add, op1=ALU.mult))
            rg_y(3)
            rg_lo(3)
            mr_out(3)
            topk_round()

            p0 = FIRST["wr"][0]
            for t in range(4):
                dve.wait_ge(panel_done, p0 + t + 1)
                dve.wait_ge(once("mr_sg"), t + 1)
                dve.tensor_tensor(two(M2, t), psum_of(p0 + t), two(GA, t), ALU.mult).then_inc(evac, 1)
            link(dve.tensor_scalar(MD[:], MD[:], -3.2e38, FAR, ALU.is_ge, ALU.mult))
            for qb in (1, 2, 3):
                w = MD[:, OFF[qb]:OFF[qb] + (qb + 1) * P]
                dve.tensor_tensor(w, w, EC[:, (3 - qb) * P:], ALU.add).then_inc(once("md_done"), 1)
            dve.wait_ge(once("md_done"), 3)
            def ga_out(k):
                p = FIRST["ga"][0] + k
                dve.wait_ge(panel_done, p + 1)
                dve.tensor_tensor(two(GA, k), psum_of(p), rr(), ALU.mult).then_inc(evac, 1)

            def silu_ga(k):
                dve.wait_ge(once("sig_ga"), k + 1)
                dve.wait_ge(evac, FIRST["ga"][0] + k + 1)
                dve.scalar_tensor_tensor(out=two(GA, k), in0=SGA[:], scalar=1.0, in1=two(GA, k),
                                         op0=ALU.add, op1=ALU.mult).then_inc(once("silu_ga"), 1)

            def mla_logits(u):
                g, qb = divmod(u, NB)
                dist = EC[:, 3 * P:] if qb == 0 else MD[:, OFF[qb]:OFF[qb] + (qb + 1) * P]
                unit_logits("mla", PM, u, qb, dist, SLOPES_2[2 * g:2 * g + 2], mla_slot(u))

            def mla_probs(u, qb):
                s, n = u % 3, (qb + 1) * P
                den = DEN3[:, 2 * s:2 * s + 2]
                dve.wait_ge(once("mla_exp"), u + 1)
                link(dve.reciprocal(den, den))
                for m in range(2):
                    ins = dve.tensor_scalar(PM[s][:, m, 0:n], PM[s][:, m, 0:n], den[:, m:m + 1], None, ALU.mult)
                ins.then_inc(once("mla_probs"), 1)

            def mla_gate(g):
                dve.wait_ge(once("mla_yp"), g + 1)
                dve.wait_ge(once("silu_ga"), g // 2 + 1)
                dve.scalar_tensor_tensor(out=GA[:, g, :], in0=PX[:, 2, :], scalar=0.5, in1=GA[:, g, :],
                                         op0=ALU.mult, op1=ALU.mult).then_inc(once("mla_y"), 1)

            def ql_lo(g):
                dve.wait_ge(once("mla_qh"), g + 1)
                dve.tensor_tensor(QLL[:], PX[:, 2:4, :], QLH[:].bitcast(F32), ALU.subtract).then_inc(once("mla_qsplit"), 1)

            def mla_ol(g):
                dve.wait_ge(once("mla_pv"), g + 1)
                dve.tensor_copy(OL[:], PX[:, 2:4, :]).then_inc(once("mla_ol"), 1)

            ql_lo(0)
            ga_out(0)
            mla_logits(0)
            silu_ga(0)
            mla_logits(1)
            mla_probs(0, 0)
            for u in range(32):
                g, qb = divmod(u, NB)
                if u % 8 == 0 and u >= 8:
                    ga_out(u // 8)
                if g >= 1 and qb == 0:
                    mla_ol(g - 1)
                if g >= 1 and qb == 1:
                    mla_gate(g - 1)
                if u + 2 < 32 and qb != 2:
                    mla_logits(u + 2)
                if qb == 2 and g < 7:
                    ql_lo(g + 1)
                if u + 1 < 32:
                    mla_probs(u + 1, (u + 1) % NB)
                if qb == 2 and g < 7:
                    mla_logits(u + 2)
                if u % 8 == 2 and u >= 8:
                    silu_ga(u // 8)
            mla_ol(7)
            mla_gate(7)
            split("o_split", "o_hi", GA, None, RH, OLO)
            p0 = FIRST["mga"][0]
            for t in range(4):
                dve.wait_ge(panel_done, p0 + t + 1)
                dve.tensor_tensor(MGA[t][:], psum_of(p0 + t), rr(), ALU.mult).then_inc(evac, 1)
            p0 = FIRST["ap"][0]
            for t in range(4):
                dve.wait_ge(panel_done, p0 + t + 1)
                dve.wait_ge(once("ma_sg"), t + 1)
                if t >= 1:
                    dve.wait_ge(once("m_ready"), 2 * t)
                dve.tensor_tensor(SG[:], psum_of(p0 + t), MGA[t][:], ALU.mult).then_inc(evac, 1)
                dve.wait_ge(evac, p0 + t + 1)
                dve.tensor_tensor(two(M2, t), two(M2, t), SG[:], ALU.add).then_inc(once("m_ready"), 2)
                if t >= 1:
                    split("m_split", "m_hi", M2, tiles=(2 * t - 2, 2 * t - 1))
            split("m_split", "m_hi", M2, tiles=(6, 7))
            p0 = FIRST["out2"][0]
            dve.wait_ge(once("m_split"), 8)
            dve.wait_ge(reloaded, 16)
            evac_sums("out2", "n6", GA, lambda k, ps, b: dve.tensor_tensor(two(M2, k), ps, two(XT, k), ALU.add))
            dve.wait_ge(once("n6_r"), 1)
            for c in range(DC):
                dve.scalar_tensor_tensor(out=SQ2[:, c, :], in0=M2[:, c, :], scalar=col("final", c), in1=R[:],
                                         op0=ALU.mult, op1=ALU.mult).then_inc(once("out_ready"), 1)


def kernel(**inputs):
    import numpy as np
    import concourse.bacc as bacc
    from concourse.bass_utils import run_bass_kernel_spmd

    a = {k: np.asarray(v) for k, v in inputs.items()}
    a = {k: (v[0] if v.ndim > 1 and v.shape[0] == 1 and k != "x" else v) for k, v in a.items()}

    def panel(w):
        n = w.shape[1] // 256
        return w.reshape(8, 128, n, 256).transpose(2, 1, 0, 3).reshape(n, 128, 2048)

    perm = np.concatenate([np.arange(64) + 64 * h for j in range(4) for h in (j, 4 + j)])
    w_in = a["w_in"]
    w_in = np.concatenate([w_in[:, :512][:, perm], w_in[:, 512:]], 1)
    w_out = np.concatenate([a["w_out"][:512][perm], a["w_out"][512:]], 0)
    up = a["w_up"].reshape(1024, 2, 32, 128).transpose(0, 2, 1, 3).reshape(1024, 8192)
    w2 = a["w_in_2"]
    off = np.cumsum([0, 1024, 128, 512, 64, 8, 1024, 1024, 1024, 2048])
    q2, ckv, qi, ki, wi, ga, xr, gr, mg = (w2[:, off[i]:off[i + 1]] for i in range(9))

    def inter(x, y):
        x, y = panel(x), panel(y)
        return np.stack([x, y], 1).reshape(2 * x.shape[0], 128, 2048)

    ups, downs = panel(up), [panel(a["w_down"][1024 * q:1024 * (q + 1)]) for q in range(4)]
    panels = np.concatenate([
        panel(w_in), panel(w_out), ups[0:8], ups[8:16], downs[0], ups[16:24], downs[1], ups[24:32],
        downs[2], downs[3],
        panel(np.concatenate([ckv, ki, ki], 1)), panel(qi), panel(q2), panel(xr), inter(gr, mg[:, 1024:]), panel(a["w_rnn_proj_2"]),
        panel(ga), panel(mg[:, :1024]), panel(a["w_attn_proj_2"]), panel(a["w_out_2"]),
    ], 0)

    def cols(v):
        return v.reshape(-1, 128).T

    sink = np.broadcast_to(a["swa_sinks"][None, :], (128, 8))
    twice = lambda v: np.concatenate([v, v])
    col = np.concatenate([
        cols(a["attn_pre_g"]), cols(a["swa_out_g"][perm]), cols(a["diff_subln_g"]), cols(a["attn_post_g"]),
        cols(a["ffn_pre_g"]), cols(a["conv_w"][0]), cols(a["conv_w"][1]), cols(a["conv_w"][2]), cols(a["conv_b"]),
        cols(a["ffn_post_g"]), cols(a["norm_gain_2"]), cols(a["b_merge_2"]), cols(a["kv_norm_gain_2"]),
        cols(twice(a["idx_ln_gain_2"])), cols(twice(a["idx_ln_bias_2"])),
        *[cols(a["conv_w_2"][k]) for k in range(4)], cols(a["conv_b_2"]), cols(a["b_rg_a_2"]), cols(a["b_rg_x_2"]),
        cols(a["lru_lambda_2"]), cols(a["final_norm_gain_2"]), sink], 1)
    lamv = np.stack([a[k] for k in ("diff_lq1", "diff_lk1", "diff_lq2", "diff_lk2")])
    lamv = np.broadcast_to(lamv[None], (128, 4, 64))
    rgw = np.zeros((128, 2, 8, 128), np.float32)
    for k, name in enumerate(("w_rg_a_2", "w_rg_x_2")):
        w = a[name].reshape(8, 2, 64, 64)
        for m in range(2):
            rgw[64 * m:64 * m + 64, k, :, 64 * m:64 * m + 64] = w[:, m].transpose(1, 0, 2)
    uk = a["w_uk_2"].reshape(8, 2, 128, 64).transpose(1, 3, 0, 2).reshape(128, 8, 128)
    uv = a["w_uv_2"].transpose(1, 0, 2)
    wis = wi.reshape(8, 128, 8).transpose(1, 0, 2)
    arrays = {"panels": panels, "xT": a["x"].reshape(512, 1024).T, "cols": col, "lamv": lamv, "wi": wis,
              "rgw": rgw, "uk": uk, "uv": uv}
    arrays = {k: np.ascontiguousarray(v) for k, v in arrays.items()}
    nc = bacc.Bacc("TRN2", target_bir_lowering=False, num_devices=1)
    args = [nc.dram_tensor(k, v.shape, mybir.dt.from_np(v.dtype), kind="ExternalInput").ap() for k, v in arrays.items()]
    args.append(nc.dram_tensor("outT", (1024, 512), F32, kind="ExternalOutput").ap())
    build(nc, *args)
    r = run_bass_kernel_spmd(nc, [arrays], core_ids=[0])
    return np.ascontiguousarray(r.results[0]["outT"].T).reshape(1, 512, 1024)
```
